# Optimizing a Trainium2 kernel written in Bass

```python
import functools
import jax, jax.numpy as jnp
from jax import lax
import numpy as np

D_MODEL = 2048
BATCH = 1
SEQ = 256
DEPTH = 1
DEC_BATCH = 8
DEC_SEQ = 4
PAST_LEN = 1024
PAGE_SIZE = 128

HEAD_DIM = 64
D_MIX = D_MODEL
D_ATT = D_MIX // 4
D_SSD = D_MIX // 2
D_LRU = D_MIX - D_ATT - D_SSD
H_ATT = D_ATT // HEAD_DIM
H_SSD = D_SSD // HEAD_DIM
SSD_GROUPS = 2
SSD_STATE = 128
SSD_CHUNK = 128
CONV_W = 4
SSD_CONV_DIM = D_SSD + 2 * SSD_GROUPS * SSD_STATE
LRU_BLOCKS = D_LRU // HEAD_DIM
LRU_BW = D_LRU // LRU_BLOCKS
LRU_C = 8.0
D_FF = ((8 * D_MODEL // 3 + 127) // 128) * 128
Q_BLOCK = 128
RMS_EPS = 1e-6
IN_SIZES = (D_ATT, D_ATT, D_ATT, H_ATT, D_SSD, SSD_CONV_DIM, H_SSD, D_LRU, D_LRU)
N_IN = sum(IN_SIZES)

kernel_name = "hymba_fox_ssd_rglru_macaron_step"

F32 = jnp.float32

def rmsnorm(x, g):
    xf = x.astype(F32)
    xf = xf * lax.rsqrt(jnp.mean(xf * xf, axis=-1, keepdims=True) + RMS_EPS)
    return (xf * g.astype(F32)).astype(x.dtype)

def swiglu(x, wg, wu, wd):
    return (jax.nn.silu(x @ wg) * (x @ wu)) @ wd

def causal_conv(u, hist, w, b):
    l = u.shape[1]
    full = jnp.concatenate([hist.astype(u.dtype), u], axis=1)
    out = b + full[:, 0:l] * w[0]
    for j in range(1, CONV_W):
        out = out + full[:, j:j + l] * w[j]
    return out, full[:, l:]

def fox_prompt(q, k, v, logf):
    b, s, h, d = q.shape
    nb = s // Q_BLOCK
    scale = 1.0 / np.sqrt(d)
    c_k = jnp.cumsum(logf, axis=1).transpose(0, 2, 1)
    q_blocks = q.reshape(b, nb, Q_BLOCK, h, d).swapaxes(0, 1)
    c_blocks = c_k.reshape(b, h, nb, Q_BLOCK).transpose(2, 0, 1, 3)
    k_pos = jnp.arange(s)

    def block(args):
        qi, ci, i = args
        sc = jnp.einsum('bqhd,bkhd->bhqk', qi, k, preferred_element_type=F32) * scale
        sc = sc + ci[..., :, None] - c_k[..., None, :]
        q_pos = i * Q_BLOCK + jnp.arange(Q_BLOCK)
        sc = jnp.where(k_pos[None, :] <= q_pos[:, None], sc, -jnp.inf)
        pr = jax.nn.softmax(sc, axis=-1)
        return jnp.einsum('bhqk,bkhd->bqhd', pr.astype(v.dtype), v)

    out = lax.map(block, (q_blocks, c_blocks, jnp.arange(nb)))
    return out.swapaxes(0, 1).reshape(b, s, h * d)

def fox_sample(q, k, v, logf, pk, pv, plf):
    b, t, h, d = q.shape
    n_past = pk.shape[1]
    scale = 1.0 / np.sqrt(d)
    plf = plf.astype(F32)
    suffix = lax.cumsum(plf, axis=1, reverse=True) - plf
    cn = jnp.cumsum(logf, axis=1).transpose(0, 2, 1)
    s_past = jnp.einsum('bthd,bshd->bhts', q, pk, preferred_element_type=F32) * scale
    s_past = s_past + cn[..., None] + suffix.transpose(0, 2, 1)[:, :, None, :]
    s_new = jnp.einsum('bthd,bkhd->bhtk', q, k, preferred_element_type=F32) * scale
    s_new = s_new + cn[..., :, None] - cn[..., None, :]
    s_new = jnp.where(jnp.tril(jnp.ones((t, t), bool)), s_new, -jnp.inf)
    pr = jax.nn.softmax(jnp.concatenate([s_past, s_new], axis=-1), axis=-1)
    out = (jnp.einsum('bhts,bshd->bthd', pr[..., :n_past].astype(pv.dtype), pv)
           + jnp.einsum('bhtk,bkhd->bthd', pr[..., n_past:].astype(v.dtype), v))
    return out.reshape(b, t, h * d)

def ssd_scan(x, dt, a, bm, cm, d_skip, h0, chunk):
    b, l, h, p = x.shape
    g, n = bm.shape[2], bm.shape[3]
    nc = l // chunk
    xf = x.astype(F32)
    bh = jnp.repeat(bm.astype(F32), h // g, axis=2).reshape(b, nc, chunk, h, n)
    ch = jnp.repeat(cm.astype(F32), h // g, axis=2).reshape(b, nc, chunk, h, n)
    xdt = (xf * dt[..., None]).reshape(b, nc, chunk, h, p)
    acs = jnp.cumsum((dt * a).reshape(b, nc, chunk, h).transpose(0, 3, 1, 2), axis=-1)
    tri = jnp.tril(jnp.ones((chunk, chunk), bool))
    seg = acs[..., :, None] - acs[..., None, :]
    lmat = jnp.where(tri, jnp.exp(jnp.where(tri, seg, 0.0)), 0.0)
    scores = jnp.einsum('bclhn,bcshn->bhcls', ch, bh) * lmat
    y_diag = jnp.einsum('bhcls,bcshp->bclhp', scores, xdt)
    decay_states = jnp.exp(acs[..., -1:] - acs)
    states = jnp.einsum('bclhn,bhcl,bclhp->bchpn', bh, decay_states, xdt)
    cs = jnp.cumsum(jnp.concatenate([jnp.zeros((b, h, 1), F32), acs[..., -1]], axis=-1), axis=-1)
    tri2 = jnp.tril(jnp.ones((nc + 1, nc + 1), bool))
    seg2 = cs[..., :, None] - cs[..., None, :]
    dchunk = jnp.where(tri2, jnp.exp(jnp.where(tri2, seg2, 0.0)), 0.0)
    all_states = jnp.concatenate([h0.astype(F32)[:, None], states], axis=1)
    new_states = jnp.einsum('bhzc,bchpn->bzhpn', dchunk, all_states)
    y_off = jnp.einsum('bclhn,bchpn,bhcl->bclhp', ch, new_states[:, :-1], jnp.exp(acs))
    y = (y_diag + y_off).reshape(b, l, h, p) + xf * d_skip.astype(F32)[:, None]
    return y, new_states[:, -1]

def rglru(u, w_a, b_a, w_x, b_x, lam, h0):
    b, l, dl = u.shape
    uf = u.astype(F32)
    ub = uf.reshape(b, l, LRU_BLOCKS, LRU_BW)
    r = jax.nn.sigmoid(jnp.einsum('blhi,hij->blhj', ub, w_a.astype(F32)).reshape(b, l, dl) + b_a)
    i = jax.nn.sigmoid(jnp.einsum('blhi,hij->blhj', ub, w_x.astype(F32)).reshape(b, l, dl) + b_x)
    log_a = -LRU_C * r * jax.nn.softplus(-lam.astype(F32))
    a = jnp.exp(log_a)
    inp = jnp.sqrt(-jnp.expm1(2.0 * log_a)) * (i * uf)
    inp = inp.at[:, 0].add(a[:, 0] * h0.astype(F32))

    def combine(e1, e2):
        return e1[0] * e2[0], e2[0] * e1[1] + e2[1]

    _, hs = lax.associative_scan(combine, (a, inp), axis=1)
    return hs, hs[:, -1]

def token_mix(xn, lp, attend, ssd_hist, ssd_h0, lru_hist, lru_h0, chunk):
    b, l, _ = xn.shape
    splits = np.cumsum(IN_SIZES)[:-1].tolist()
    q, k, v, f_raw, z, xbc, dt_raw, g_raw, u_raw = jnp.split(xn @ lp['w_in'], splits, axis=-1)
    q = q.reshape(b, l, H_ATT, HEAD_DIM)
    k = k.reshape(b, l, H_ATT, HEAD_DIM)
    v = v.reshape(b, l, H_ATT, HEAD_DIM)
    logf = jax.nn.log_sigmoid(f_raw.astype(F32) + lp['fox_b_f'].astype(F32))
    att = attend(q, k, v, logf)
    xbc, ssd_hist_new = causal_conv(xbc, ssd_hist, lp['ssd_conv_w'], lp['ssd_conv_b'])
    xbc = jax.nn.silu(xbc)
    xs, bm, cm = jnp.split(xbc, [D_SSD, D_SSD + SSD_GROUPS * SSD_STATE], axis=-1)
    dt = jax.nn.softplus(dt_raw.astype(F32) + lp['ssd_dt_bias'].astype(F32))
    a = -jnp.exp(lp['ssd_a_log'].astype(F32))
    y, ssd_state = ssd_scan(xs.reshape(b, l, H_SSD, HEAD_DIM), dt, a,
                            bm.reshape(b, l, SSD_GROUPS, SSD_STATE), cm.reshape(b, l, SSD_GROUPS, SSD_STATE),
                            lp['ssd_d'], ssd_h0, chunk)
    yg = (y.reshape(b, l, D_SSD) * jax.nn.silu(z.astype(F32))).reshape(b, l, SSD_GROUPS, D_SSD // SSD_GROUPS)
    yg = yg * lax.rsqrt(jnp.mean(yg * yg, axis=-1, keepdims=True) + RMS_EPS)
    ssd_out = yg.reshape(b, l, D_SSD) * lp['ssd_norm'].astype(F32)
    u, lru_hist_new = causal_conv(u_raw, lru_hist, lp['lru_conv_w'], lp['lru_conv_b'])
    hs, lru_state = rglru(u, lp['lru_w_a'], lp['lru_b_a'], lp['lru_w_x'], lp['lru_b_x'], lp['lru_lambda'], lru_h0)
    lru_out = hs * jax.nn.gelu(g_raw.astype(F32))
    merged = jnp.concatenate([att.astype(xn.dtype), ssd_out.astype(xn.dtype), lru_out.astype(xn.dtype)], axis=-1)
    return merged @ lp['w_out'], (k, v, logf, ssd_state, ssd_hist_new, lru_state, lru_hist_new)

def decoder_layer(x, lp, attend, ssd_hist, ssd_h0, lru_hist, lru_h0, chunk):
    x = x + 0.5 * swiglu(rmsnorm(x, lp['ffn1_norm']), lp['ffn1_w_gate'], lp['ffn1_w_up'], lp['ffn1_w_down'])
    m, st = token_mix(rmsnorm(x, lp['mix_norm']), lp, attend, ssd_hist, ssd_h0, lru_hist, lru_h0, chunk)
    x = x + m
    x = x + 0.5 * swiglu(rmsnorm(x, lp['ffn2_norm']), lp['ffn2_w_gate'], lp['ffn2_w_up'], lp['ffn2_w_down'])
    return x, st

def setup_inputs(seed: int = 0) -> dict:
    key = jax.random.key(seed)
    ks = iter(jax.random.split(key, 48))
    nrm = lambda shape, s=1.0: jax.random.normal(next(ks), shape, F32) * s
    n_pages = PAST_LEN // PAGE_SIZE
    n_used = DEC_BATCH * n_pages
    n_pool = n_used + n_used // 4
    page_table = jax.random.permutation(next(ks), n_pool)[:n_used].reshape(DEC_BATCH, n_pages).astype(jnp.int32)
    dt0 = jnp.exp(jax.random.uniform(next(ks), (DEPTH, H_SSD), F32, np.log(1e-3), np.log(1e-1)))
    lam_s = jax.random.uniform(next(ks), (DEPTH, D_LRU), F32, 0.9, 0.999) ** (1.0 / LRU_C)
    inp = {
        'x_prompt': nrm((BATCH, SEQ, D_MODEL)),
        'x_sample': nrm((DEC_BATCH, DEC_SEQ, D_MODEL)),
        'cache_k': nrm((DEPTH, n_pool, PAGE_SIZE, H_ATT, HEAD_DIM)),
        'cache_v': nrm((DEPTH, n_pool, PAGE_SIZE, H_ATT, HEAD_DIM)),
        'cache_logf': jax.nn.log_sigmoid(3.0 + nrm((DEPTH, n_pool, PAGE_SIZE, H_ATT))),
        'page_table': page_table,
        'state_ssd': nrm((DEPTH, DEC_BATCH, H_SSD, HEAD_DIM, SSD_STATE), 0.1),
        'state_ssd_conv': nrm((DEPTH, DEC_BATCH, CONV_W - 1, SSD_CONV_DIM)),
        'state_lru': nrm((DEPTH, DEC_BATCH, D_LRU), 0.5),
        'state_lru_conv': nrm((DEPTH, DEC_BATCH, CONV_W - 1, D_LRU)),
        'ffn1_norm': 1.0 + nrm((DEPTH, D_MODEL), 0.02),
        'ffn1_w_gate': nrm((DEPTH, D_MODEL, D_FF), D_MODEL ** -0.5),
        'ffn1_w_up': nrm((DEPTH, D_MODEL, D_FF), D_MODEL ** -0.5),
        'ffn1_w_down': nrm((DEPTH, D_FF, D_MODEL), D_FF ** -0.5),
        'mix_norm': 1.0 + nrm((DEPTH, D_MODEL), 0.02),
        'w_in': nrm((DEPTH, D_MODEL, N_IN), D_MODEL ** -0.5),
        'fox_b_f': jax.random.uniform(next(ks), (DEPTH, H_ATT), F32, 1.0, 5.0),
        'ssd_conv_w': nrm((DEPTH, CONV_W, SSD_CONV_DIM), CONV_W ** -0.5),
        'ssd_conv_b': nrm((DEPTH, SSD_CONV_DIM), 0.02),
        'ssd_dt_bias': dt0 + jnp.log(-jnp.expm1(-dt0)),
        'ssd_a_log': jnp.log(jax.random.uniform(next(ks), (DEPTH, H_SSD), F32, 1.0, 16.0)),
        'ssd_d': 1.0 + nrm((DEPTH, H_SSD), 0.1),
        'ssd_norm': 1.0 + nrm((DEPTH, D_SSD), 0.02),
        'lru_conv_w': nrm((DEPTH, CONV_W, D_LRU), CONV_W ** -0.5),
        'lru_conv_b': nrm((DEPTH, D_LRU), 0.02),
        'lru_w_a': nrm((DEPTH, LRU_BLOCKS, LRU_BW, LRU_BW), LRU_BW ** -0.5),
        'lru_b_a': nrm((DEPTH, D_LRU), 0.02),
        'lru_w_x': nrm((DEPTH, LRU_BLOCKS, LRU_BW, LRU_BW), LRU_BW ** -0.5),
        'lru_b_x': nrm((DEPTH, D_LRU), 0.02),
        'lru_lambda': jnp.log(lam_s) - jnp.log1p(-lam_s),
        'w_out': nrm((DEPTH, D_MIX, D_MODEL), D_MIX ** -0.5),
        'ffn2_norm': 1.0 + nrm((DEPTH, D_MODEL), 0.02),
        'ffn2_w_gate': nrm((DEPTH, D_MODEL, D_FF), D_MODEL ** -0.5),
        'ffn2_w_up': nrm((DEPTH, D_MODEL, D_FF), D_MODEL ** -0.5),
        'ffn2_w_down': nrm((DEPTH, D_FF, D_MODEL), D_FF ** -0.5),
        'final_norm': 1.0 + nrm((D_MODEL,), 0.02),
    }
    return inp

def reference(x_prompt, x_sample, cache_k, cache_v, cache_logf, page_table, state_ssd, state_ssd_conv,
              state_lru, state_lru_conv, ffn1_norm, ffn1_w_gate, ffn1_w_up, ffn1_w_down, mix_norm, w_in,
              fox_b_f, ssd_conv_w, ssd_conv_b, ssd_dt_bias, ssd_a_log, ssd_d, ssd_norm, lru_conv_w,
              lru_conv_b, lru_w_a, lru_b_a, lru_w_x, lru_b_x, lru_lambda, w_out, ffn2_norm, ffn2_w_gate,
              ffn2_w_up, ffn2_w_down, final_norm):
    bp, s_len, _ = x_prompt.shape
    bd, t_len, _ = x_sample.shape
    past = page_table.shape[1] * PAGE_SIZE
    yp, ys = x_prompt, x_sample
    st_p, st_s = [], []
    for l in range(DEPTH):
        lp = dict(ffn1_norm=ffn1_norm[l], ffn1_w_gate=ffn1_w_gate[l], ffn1_w_up=ffn1_w_up[l],
                  ffn1_w_down=ffn1_w_down[l], mix_norm=mix_norm[l], w_in=w_in[l], fox_b_f=fox_b_f[l],
                  ssd_conv_w=ssd_conv_w[l], ssd_conv_b=ssd_conv_b[l], ssd_dt_bias=ssd_dt_bias[l],
                  ssd_a_log=ssd_a_log[l], ssd_d=ssd_d[l], ssd_norm=ssd_norm[l], lru_conv_w=lru_conv_w[l],
                  lru_conv_b=lru_conv_b[l], lru_w_a=lru_w_a[l], lru_b_a=lru_b_a[l], lru_w_x=lru_w_x[l],
                  lru_b_x=lru_b_x[l], lru_lambda=lru_lambda[l], w_out=w_out[l], ffn2_norm=ffn2_norm[l],
                  ffn2_w_gate=ffn2_w_gate[l], ffn2_w_up=ffn2_w_up[l], ffn2_w_down=ffn2_w_down[l])
        yp, sp = decoder_layer(
            yp, lp, fox_prompt,
            jnp.zeros((bp, CONV_W - 1, SSD_CONV_DIM), yp.dtype), jnp.zeros((bp, H_SSD, HEAD_DIM, SSD_STATE), F32),
            jnp.zeros((bp, CONV_W - 1, D_LRU), yp.dtype), jnp.zeros((bp, D_LRU), F32),
            min(SSD_CHUNK, s_len))
        st_p.append(sp)
        pk = cache_k[l][page_table].reshape(bd, past, H_ATT, HEAD_DIM)
        pv = cache_v[l][page_table].reshape(bd, past, H_ATT, HEAD_DIM)
        plf = cache_logf[l][page_table].reshape(bd, past, H_ATT)
        attend_s = functools.partial(fox_sample, pk=pk, pv=pv, plf=plf)
        ys, ss = decoder_layer(ys, lp, attend_s, state_ssd_conv[l], state_ssd[l], state_lru_conv[l],
                               state_lru[l], t_len)
        st_s.append(ss)
    y_prompt = rmsnorm(yp, final_norm)
    y_sample = rmsnorm(ys, final_norm)
    k_p = jnp.stack([s[0] for s in st_p]); v_p = jnp.stack([s[1] for s in st_p]); lf_p = jnp.stack([s[2] for s in st_p])
    ssd_p = jnp.stack([s[3] for s in st_p]); ssdc_p = jnp.stack([s[4] for s in st_p])
    lru_p = jnp.stack([s[5] for s in st_p]); lruc_p = jnp.stack([s[6] for s in st_p])
    k_s = jnp.stack([s[0] for s in st_s]); v_s = jnp.stack([s[1] for s in st_s]); lf_s = jnp.stack([s[2] for s in st_s])
    ssd_s = jnp.stack([s[3] for s in st_s]); ssdc_s = jnp.stack([s[4] for s in st_s])
    lru_s = jnp.stack([s[5] for s in st_s]); lruc_s = jnp.stack([s[6] for s in st_s])
    return (y_prompt, y_sample, k_p, v_p, lf_p, k_s, v_s, lf_s, ssd_p, ssdc_p, ssd_s, ssdc_s,
            lru_p, lruc_p, lru_s, lruc_s)


_drawn_inputs = setup_inputs


def setup_inputs(seed=0):
    import zlib

    import numpy as np

    out = dict(_drawn_inputs(seed))
    spreads = {}
    factors = {'cache_logf': 198.79,
     'ffn1_norm': 4.503,
     'ssd_norm': 24.042,
     'lru_b_a': 8.0,
     'lru_b_x': 7.977,
     'ffn2_norm': 8.0,
     'final_norm': 24.392,
     'cache_k': 9.663,
     'cache_v': 2.684}
    for name, (base, spread) in spreads.items():
        noise = np.random.default_rng([zlib.crc32(name.encode()), seed]).standard_normal(out[name].shape)
        drawn = base * np.exp(spread * noise) if base else spread * noise
        out[name] = __import__('jax').numpy.asarray(drawn.astype(out[name].dtype))
    for name, factor in factors.items():
        out[name] = (out[name] * factor).astype(out[name].dtype)
    return out
```

```python
from contextlib import ExitStack

import numpy as np

import concourse.bass as bass
from concourse import mybir

F32 = mybir.dt.float32
F32R = mybir.dt.float32r
I32 = mybir.dt.int32
ACT = mybir.ActivationFunctionType
ALU = mybir.AluOpType
AX = mybir.AxisListType

P = 128
D = 2048
KT = D // P
NP_, ND, NT = 256, 8, 4
NS = ND * NT
N = NP_ + NS
DFF = 5504
FT = DFF // P
GROUPS = (15, 15, 13)
HG = max(GROUPS)
EPS = 1e-6
H_ATT, H_SSD, HD, ST = 8, 16, 64, 128
PAGE, PAGES = 128, 8
PAST = PAGE * PAGES
POOLP = 80
VRING = 4
SEGW = 3 * P + NS
CW = 4
HC = CW - 1
XBC, DSSD, DLRU = 1536, 1024, 512
XT_, LT_ = XBC // P, DLRU // P
LRU_C = 8.0
O_Q, O_K, O_V, O_F, O_Z = 0, 512, 1024, 1536, 1544
O_XBC, O_DT, O_G, O_U = 2568, 4104, 4120, 4632
BIG = 1.0e30
MIX = 1
IN_TILES, OUT_TILES = 41, 32
LOADS = 4
R_CW, R_CB, R_LW, R_LB, R_BA, R_BX, R_LAM, R_NRM = 0, 48, 60, 76, 80, 84, 88, 92
NPAR = 100


AT = {}


class Plan:

    def __init__(self, nc, at, end):
        self.nc, self.at, self.end = nc, at, end

    def __call__(self, name, shape, dtype=F32):
        size = 4 * int(np.prod(shape[1:]))
        t = self.nc.alloc_sbuf_tensor_at(name, list(shape), dtype, offset=self.at)
        AT[name] = self.at
        self.at += -(-size // 32) * 32
        assert self.at <= self.end, (name, self.at, self.end)
        return t


def build(nc, I, O):
    ctx = ExitStack()
    sems = {}

    def sem(name):
        if name not in sems:
            sems[name] = ctx.enter_context(nc.semaphore(name))
        return sems[name]

    SB0, SB1 = 4224, 229344
    fixed = Plan(nc, SB0, SB1)
    wraw = fixed("wraw", [P, LOADS, KT * P])
    whi = fixed("whi", [P, 2, KT * P], F32R)
    wlo = fixed("wlo", [P, 2, KT * P], F32R)
    xn_hi = fixed("xn_hi", [P, KT, N], F32R)
    xn_lo = fixed("xn_lo", [P, KT, N], F32R)
    ident = fixed("ident", [P, P])
    ones = fixed("ones", [P, P])
    gains = fixed("gains", [P, 4, KT])
    params = fixed("params", [P, NPAR])
    xf = fixed("xf", [P, 3, N])
    sq = fixed("sq", [P, 2, N])
    ssum = fixed("ssum", [P, N])
    rs = fixed("rs", [P, 3, N])
    XAT = fixed.at
    xT = fixed("xT", [P, KT, N])
    ARENA = fixed.at

    ffn = Plan(nc, ARENA, SB1)
    h_hi = ffn("h_hi", [P, HG, N], F32R)
    h_lo = ffn("h_lo", [P, HG, N], F32R)
    sg = ffn("sg", [P, 2, N])
    hm = ffn("hm", [P, 2, N])
    hin = Plan(nc, ARENA, SB1)
    histn = hin("histn", [HC * ND, 16 * P])
    h0n = hin("h0n", [ND, DLRU])
    fin = Plan(nc, ARENA, SB1)

    mix = Plan(nc, XAT, SB1)
    kpage = mix("kpage", [P, 4, 512])
    vpage = mix("vpage", [P, VRING, 512])
    qblk = mix("qblk", [P, 4, 4, 32])
    kts = mix("kts", [P, 2, 512])
    bias = mix("bias", [P, PAST])
    ps = mix("ps", [P, PAST + NS])
    att_o = ps[:, 0:512]
    pts = mix("pts", [P, PAST + P])
    qT = mix("qT", [P, 4, N])
    kT = mix("kT", [P, 4, N])
    kvn = mix("kvn", [P, 3, 1024])
    maskp = mix("maskp", [P, 384])
    masks = mix("masks", [P, 2, NS])
    A1 = mix.at
    pid = mix("pid", [1, ND * PAGES], I32)
    bmask = mix("bmask", [NS, ND])
    lfo = mix("lfo", [P, 3, H_ATT])
    head_rows = mix("head_rows", [H_ATT, NS])
    fold = mix("fold", [NS, NT])
    total = mix("total", [64, H_ATT])
    lafter = mix("lafter", [64, H_ATT])
    sc48 = mix("sc48", [P, 3, N])
    nat = mix("nat", [P, 3, 144])
    nat_e = mix("nat_e", [P, 48])
    negc = mix("negc", [P, N])
    seqmask = mix("seqmask", [P, N])
    col = mix("col", [P, 8])
    eend = mix("eend", [P, ND])
    e48 = mix("e48", [P, NS])
    dec = mix("dec", [P, 8, ND])
    histT = mix("histT", [P, 16, HC * ND])
    histO = mix("histO", [P, 16, HC + HC * ND])
    h0T = mix("h0T", [P, 4, ND])
    lam = mix("lam", [P, 8, 4])
    dcol = mix("dcol", [P, 8])
    raw = mix("raw", [P, 2, 315])
    ctmp = mix("ctmp", [P, 312])
    nm = mix("nm", [P, 4])
    rsum = mix("rsum", [P, 4])
    rr = mix("rr", [P, 4])
    lwa = mix("lwa", [P, 4, P])
    lwx = mix("lwx", [P, 4, P])
    cpad = mix("cpad", [P, 2, ND, NS])
    tri = mix("tri", [P, 384])
    tris = mix("tris", [P, NS])
    LATE = mix.at
    xsT = mix("xsT", [P, 12, N])
    attT = mix("attT", [P, 4, N])
    uT = mix("uT", [P, 4, N])
    gT = mix("gT", [P, 4, N])
    pro = Plan(nc, LATE, SB1)
    xnat = pro("xnat", [P, 3, D])
    gnat = pro("gnat", [64, P])
    pnat = pro("pnat", [NPAR, P])
    early = Plan(nc, LATE, SB1)
    lfp = early("lfp", [64, PAGE, H_ATT])
    sfx = early("sfx", [64, H_ATT, PAGE + 1])
    later = early("later", [64, 64])
    zero = early("zero", [64, PAGE])
    ep = Plan(nc, XAT, A1)
    lru_r = ep("lru_r", [P, 4, N])
    lru_i = ep("lru_i", [P, 4, N])
    lru_a = ep("lru_a", [P, 4, N])
    ep = Plan(nc, ARENA, A1)
    xsn = ep("xsn", [P, 3, DSSD])
    bnat = ep("bnat", [P, 3, 256])
    cbm = ep("cbm", [P, 2, SEGW])
    zT = ep("zT", [P, 8, N])
    lst = ep("lst", [P, 4, 9])
    lseg = ep("lseg", [P, 2, SEGW])
    mseg = ep("mseg", [P, 2, SEGW])
    sst = ep("sst", [P, 2, 512])
    hout = Plan(nc, AT["lru_a"] + 4 * 4 * N, ARENA)("hout", [P, 2, 512])
    bexp = Plan(nc, AT["lseg"], A1)("bexp", [P, 4, 256])
    snew = Plan(nc, AT["sst"], A1)("snew", [P, 2, 512])
    def over(other, name, shape):
        return Plan(nc, AT[other], SB1)(name, shape)

    h0 = Plan(nc, AT["xn_lo"] + 4 * 4 * N, AT["ident"])("h0", [P, 4, 512])
    m_hi = Plan(nc, AT["lseg"], A1)("m_hi", [P, 8, N], F32R)
    m_lo = Plan(nc, AT["attT"], AT["gT"])("m_lo", [P, 8, N], F32R)
    h0t = over("gT", "h0t", [P, 2, 512])
    ys = over("uT", "ys", [P, 1024])
    lrs = over("lwa", "lrs", [P, 512])
    ysq = over("xsn", "ysq", [P, 8, N])
    fin.at += 4 * KT * N
    yT = Plan(nc, AT["xn_hi"], AT["xn_lo"])("yT", [P, KT, N])
    ynat = fin("ynat", [P, 3, D])

    bank = [ctx.enter_context(nc.psum_tensor(f"bank{i}", [P, 512], F32)) for i in range(8)]
    STAT = 7

    seg, at = {}, 0
    for f in range(2):
        for g, n in enumerate(GROUPS):
            for what, m in (("up", 2 * n), ("down", KT)):
                seg[what, f, g] = at
                at += m
        if f == 0 and MIX:
            seg["in"], seg["out"] = at, at + IN_TILES
            at += IN_TILES + OUT_TILES
    FF0 = {(f, g): f * FT + sum(GROUPS[:g]) for f in range(2) for g in range(3)}
    XA0 = {(f, g): (f * 3 + g) * KT + f * MIX * OUT_TILES for f in range(2) for g in range(3)}
    XO0 = 3 * KT
    NORM = {"ffn1": (0, 0, 0), "mix": (1, XO0, 1), "ffn2": (1 + MIX, XA0[1, 0], 2), "final": (2 + MIX, XA0[1, 2] + KT, 3)}
    FN = [NORM["ffn1"][0], NORM["ffn2"][0]]

    def cols(w, k0, nk, c0, width=P):
        rows = w.rearrange("(k p) c -> p k c", p=P)
        return rows[:, k0:k0 + nk, bass.ds(c0, width)]

    def tile_ap(buf, slot, nk):
        return buf[:, slot, 0:nk * P]

    WG = [I["ffn1_w_gate"][0], I["ffn2_w_gate"][0]]
    WU = [I["ffn1_w_up"][0], I["ffn2_w_up"][0]]
    WD = [I["ffn1_w_down"][0], I["ffn2_w_down"][0]]

    IN0, OUT0 = seg["in"], seg["out"]
    T_Q, T_K, T_V, T_X, T_U, T_G, T_Z = 1, 5, 9, 13, 25, 29, 33
    IN_COL = [O_F] + [o + P * j for o, c in ((O_Q, 4), (O_K, 4), (O_V, 4), (O_XBC, 12), (O_U, 4), (O_G, 4), (O_Z, 8))
                      for j in range(c)]
    x_save = nc.dram_tensor("x_save", [P, KT, N], F32, kind="Internal").ap()
    suf_d = nc.dram_tensor("suf_d", [ND, H_ATT, PAST], F32, kind="Internal").ap()
    SC, CS, WDC = 0, 1, 2
    SR = slice(32, 48)

    def sampled(ap):
        return ap.rearrange("p (b t) -> p b t", t=NT)

    def strided(ap, at, *dims):
        return bass.AP(ap.tensor, ap.offset + at, [list(ap.ap[0])] + [list(d) for d in dims])

    def windows(ap, at):
        return strided(ap, at, (HC + NT, ND), (1, NT))

    STEPS = [("in", 0), ("suffix",), ("in", 1), ("gates",), ("in", 2), ("turn_gates",)]
    STEPS += [("in", t) for t in range(3, T_X + 1)] + [("turn_kv",)]
    tiles = iter(range(T_X + 1, IN_TILES))

    def tile():
        return [("in", next(tiles))]

    for n in range(H_ATT + 2):
        STEPS += [("prompt", n)] + [("keys", n)] * (n < 8) + tile()
    STEPS += [("max", 0)] + tile() + [("probs", 0), ("keys", 8)] + tile()
    for r in range(4):
        STEPS += [("values", r), ("keys", 9 + r)] + tile()
    STEPS += [("scale", 0), ("keys", 13)] + tile() + [("merge_heads", 0), ("keys", 14)] + tile() + [("keys", 15)] + tile()
    STEPS += [("max", 1)] + tile() + [("probs", 1), ("values", 4), ("values", 5)] + tile()
    STEPS += [("values", 6), ("values", 7), ("scale", 1), ("merge_heads", 1)] + tile()
    STEPS += [("lru_gates",), ("hist", 0), ("hist", 1)] + tile() + [("lru_decay",), ("hist", 2), ("hist", 3), ("lru_scan",)]
    STEPS += [("turn_x", b) for b in range(3)] + [("scores",)] + tile() + [("lru_out",)]
    heads = iter(range(H_SSD + 2))
    for t in tiles:
        STEPS += [("ssd", next(heads)) for _ in range(3)] + [("in", t)]
    STEPS += [("ssd", next(heads)) for _ in range(2)] + [("in", IN_TILES), ("merge", 0)]
    outs = iter(range(KT))
    for n, h in enumerate(heads):
        STEPS += [("ssd", h)] + ([("out", next(outs))] if n % 2 == 0 else [])
    STEPS += [("decay_x",), ("state", 0), ("state", 1), ("out", next(outs))]
    for u in range(2 * ND + 1):
        STEPS += [("unit", u)] + ([("out", next(outs))] if u % 3 == 2 and u < 15 else [])
    rest = [("out", n) for n in outs]
    last_steps = [("carry",), ("gate",), ("group", 0), ("group", 1)]
    for n, what in enumerate(last_steps):
        STEPS += [what] + rest[n * len(rest) // 4:(n + 1) * len(rest) // 4]

    JOB = {}
    for step in STEPS:
        what, i = step[0], step[-1]
        names = {"suffix": [("later",)], "turn_gates": [("nat",), ("dec",)],
                 "turn_kv": [(x, b) for b in range(3) for x in "kv"],
                 "keys": [("kt", u) for u in range(4 * i, 4 * i + 4)] if what == "keys" else [],
                 "probs": [("pt", i, q) for q in range(3)], "merge_heads": [("heads", i)],
                 "lru_gates": [(x, c) for c in range(4) for x in ("r", "i")],
                 "hist": [("hist", i)], "lru_out": [("lru_state",)],
                 "turn_x": [("x", i, 0), ("x", i, 1), ("b", i)], "scores": [("cb", 0), ("cb", 1)],
                 "state": [("state", i)], "carry": [("ys",)], "group": [("mean", i)]}.get(what, [])
        if what == "prompt":
            names = [("sc", i)] * (i < H_ATT) + [("p", i - 1)] * (1 <= i <= H_ATT) \
                + [("pv", i - 2)] * (i >= 2)
        if what == "ssd":
            names = [("acs", i)] * (i < H_SSD) + [("y", (i - 2) // 2)] * (i >= 2 and i % 2 == 0)
        if what == "unit":
            names = ([("ht", i)] if i < 2 * ND else []) + ([("up", i - 1)] if i else [])
        for name in names:
            JOB[name] = len(JOB)

    def side(*name):
        return bank[5 + JOB[name] % 3]

    def claim(pe, *name):
        j = JOB[name]
        if j >= 3:
            pe.wait_ge(sem(f"side_read{j % 3}"), j // 3)
        return side(*name)

    def side_done(*name):
        return sem(f"side_done{JOB[name] % 3}")

    def side_read(*name):
        return sem(f"side_read{JOB[name] % 3}")

    def take(eng, *name):
        eng.wait_ge(side_done(*name), JOB[name] // 3 + 1)
        return side(*name)

    def copied(eng, *name):
        eng.wait_ge(side_read(*name), JOB[name] // 3 + 1)

    def h0_of(name, u):
        t = I[name] if name in I else O[name]
        return t[0, u // 2, 8 * (u % 2):8 * (u % 2) + 8].rearrange("(j e) p n -> (e p) j n", e=2)

    def spread(ap, n):
        return ap.unsqueeze(2).to_broadcast([ap.shape[0], ap.shape[1], n])

    def back(ap):
        step, n = ap.ap[-1]
        return bass.AP(ap.tensor, ap.offset + step * (n - 1), [list(d) for d in ap.ap[:-1]] + [[-step, n]])

    def rows_of(blk):
        return P if blk < 2 else NS

    def toks(blk):
        return slice(blk * P, blk * P + rows_of(blk))

    PAIRS = ((slice(0, NP_), 0, slice(0, NP_)), (slice(NP_, 3 * P), 1, slice(P, NP_)),
             (slice(3 * P, SEGW), 2, slice(NP_, N)))

    block = ctx.enter_context(nc.Block())

    @block.sync
    def _(sp):
        for r in range(2):
            sp.dma_start(xnat[:, r, :], I["x_prompt"][0, r * P:(r + 1) * P, :]).then_inc(sem("x_loaded"), 16)
        sp.dma_start(xnat[0:NS, 2, :], I["x_sample"].rearrange("b t d -> (b t) d")).then_inc(sem("x_loaded"), 16)
        for n, name in enumerate(("ffn1_norm", "mix_norm", "ffn2_norm")):
            sp.dma_start(gnat[n * KT:(n + 1) * KT, :], I[name][0].rearrange("(k p) -> k p", p=P))\
                .then_inc(sem("gains_loaded"), 16)
        sp.dma_start(gnat[3 * KT:, :], I["final_norm"].rearrange("(k p) -> k p", p=P))\
            .then_inc(sem("gains_loaded"), 16)
        rows = ((R_CW, I["ssd_conv_w"][0].rearrange("w (c p) -> (w c) p", p=P)),
                (R_CB, I["ssd_conv_b"][0].rearrange("(c p) -> c p", p=P)),
                (R_LW, I["lru_conv_w"][0].rearrange("w (c p) -> (w c) p", p=P)),
                (R_LB, I["lru_conv_b"][0].rearrange("(c p) -> c p", p=P)),
                (R_BA, I["lru_b_a"][0].rearrange("(c p) -> c p", p=P)),
                (R_BX, I["lru_b_x"][0].rearrange("(c p) -> c p", p=P)),
                (R_LAM, I["lru_lambda"][0].rearrange("(c p) -> c p", p=P)),
                (R_NRM, I["ssd_norm"][0].rearrange("(c p) -> c p", p=P)))
        for r, src in rows:
            sp.dma_start(pnat[r:r + src.shape[0], :], src).then_inc(sem("params_loaded"), 16)

        sp.dma_start(histn[:, 0:XBC], I["state_ssd_conv"][0].rearrange("b w c -> (b w) c")).then_inc(sem("hist_loaded"), 16)
        sp.dma_start(histn[:, XBC:], I["state_lru_conv"][0].rearrange("b w c -> (b w) c")).then_inc(sem("hist_loaded"), 16)
        sp.dma_start(h0n[:], I["state_lru"][0]).then_inc(sem("hist_loaded"), 16)

        def load(base, it4, j, src, nk):
            i = base + j + it4
            if not isinstance(i, int) or i >= LOADS:
                sp.wait_ge(sem("lo_done"), i - LOADS + 1)
            slot = (base + j) % LOADS
            sp.dma_start(tile_ap(wraw, slot, nk).rearrange("p (k c) -> p k c", k=nk), src)\
                .then_inc(sem(f"raw_ready{slot}"), 16)

        for f in range(2):
            for g, n in enumerate(GROUPS):
                f0 = sum(GROUPS[:g])
                base = seg["up", f, g]
                for m in range(3):
                    for j, w in enumerate((WG, WU)):
                        load(base + 2 * m, 0, j, cols(w[f], 0, KT, (f0 + m) * P), KT)
                with sp.Fori(0, (n - 3) // 2) as it:
                    for m in range(2):
                        for j, w in enumerate((WG, WU)):
                            load(base + 6, it * 4, 2 * m + j, cols(w[f], 0, KT, it * (2 * P) + (f0 + 3 + m) * P), KT)
                base = seg["down", f, g]
                for j in range(4):
                    load(base, 0, j, cols(WD[f], f0, n, j * P), n)
                with sp.Fori(1, KT // 4) as it:
                    for j in range(4):
                        load(base, it * 4, j, cols(WD[f], f0, n, it * (4 * P) + j * P), n)

            if f == 0 and MIX:
                sp.wait_ge(sem("lo_done"), IN0 - LOADS + 1)
                win = I["w_in"][0]
                slot = IN0 % LOADS
                to = tile_ap(wraw, slot, KT).rearrange("p (k c) -> p k c", k=KT)
                sp.dma_start(to[:, :, 0:H_ATT], cols(win, 0, KT, O_F, H_ATT)).then_inc(sem("w_small"), 16)
                sp.dma_start(to[:, :, 64:72], cols(win, 0, KT, O_F, H_ATT)).then_inc(sem("w_small"), 16)
                sp.dma_start(to[:, :, 32:48], cols(win, 0, KT, O_DT, H_SSD)).then_inc(sem(f"raw_ready{slot}"), 16)
                wo = I["w_out"][0].rearrange("(a k p) c -> p a k c", a=4, p=P)

                def load_out(part, it4, j):
                    slot = (OUT0 + j) % LOADS
                    sp.wait_ge(sem("lo_done"), it4 + (OUT0 + part * KT + j - LOADS + 1))
                    for a, q in enumerate(((0, 3), (1, 2))[part]):
                        sp.dma_start(wraw[:, slot, a * 512:(a + 1) * 512].rearrange("p (k c) -> p k c", k=4),
                                     wo[:, q, :, bass.ds(it4 * P + j * P, P)])\
                            .then_inc(sem(f"wo_half{slot}" if a else f"raw_ready{slot}"), 16)

                def load_mix(n):
                    if n < IN_TILES:
                        load(IN0, 0, n, cols(win, 0, KT, IN_COL[n], P), KT)
                    else:
                        n -= IN_TILES
                        load_out(n // KT, 0, n % KT)

                def load_page(buf, slot, name, u):
                    page = sp.value_load(pid[0:1, u:u + 1], min_val=0, max_val=POOLP - 1)
                    sp.dma_start(buf[:, slot, :],
                                 I[name][0].rearrange("n s h d -> (n s) (h d)")[bass.ds(page * PAGE, PAGE), :])\
                        .then_inc(sem(f"{name}_loaded{slot}"), 16)

                def load_h0(u):
                    sp.dma_start(h0[:, u % 4, :].rearrange("q (j n) -> q j n", j=4), h0_of("state_ssd", u))\
                        .then_inc(sem(f"h0_loaded{u % 4}"), 16)

                AHEAD = LOADS - 1
                for n in range(1, AHEAD):
                    load_mix(n)
                sp.wait_ge(sem("pid_loaded"), 16)
                for step in STEPS:
                    what, i = step[0], step[-1]
                    if what == "in" and i < IN_TILES:
                        load_mix(i + AHEAD)
                    elif what == "out":
                        load_mix(IN_TILES + i + AHEAD)
                    elif what == "keys":
                        if i == 0:
                            sp.wait_ge(sem("x_saved"), 16)
                            sp.wait_ge(sem("xf_ready"), 2 * KT)
                        for u in range(4 * i, 4 * i + 4):
                            if u >= 4:
                                take(sp, "kt", u - 4)
                            load_page(kpage, u % 4, "cache_k", u)
                    elif what == "values":
                        for u in range(PAGES * i, PAGES * (i + 1)):
                            if u >= VRING:
                                sp.wait_ge(sem("vpage_used"), u - VRING + 1)
                            load_page(vpage, u % VRING, "cache_v", u)
                    elif what == "merge":
                        sp.wait_ge(sem("merged"), 8)
                        for u in range(4):
                            load_h0(u)
                    elif what == "unit" and i:
                        u = i - 1
                        copied(sp, "up", u)
                        sp.dma_start(h0_of("ssd_state_sample", u), snew[:, u % 2, :].rearrange("q (j n) -> q j n", j=4))\
                            .then_inc(sem(f"snew_stored{u % 2}"), 16)
                        if u + 4 < 2 * ND:
                            load_h0(u + 4)
                load_mix(IN_TILES + KT + AHEAD)
                with sp.Fori(1, KT // 4) as it:
                    for j in range(4):
                        load_out(1, it * 4, j)

        sp.wait_ge(sem("y_ready"), 6)
        sp.wait_ge(sem("y_ready2"), 6)
        for r in range(2):
            sp.dma_start(O["y_prompt"][0, r * P:(r + 1) * P, :], ynat[:, r, :]).then_inc(sem("stored"), 16)
        sp.dma_start(O["y_sample"].rearrange("b t d -> (b t) d"), ynat[0:NS, 2, :]).then_inc(sem("stored"), 16)
        sp.wait_ge(sem("stored"), 48)
        sp.wait_ge(sem("kv_stored"), 16 * 7)
        for q in range(2):
            sp.wait_ge(sem(f"hist_stored{q}"), 64)
            sp.wait_ge(sem(f"snew_stored{q}"), 16 * ND)
        sp.wait_ge(sem("lru_stored"), 16 * 2)
        sp.wait_ge(sem("state_stored"), 16 * 2)

    @block.gpsimd
    def _(pool):
        pool.memset(tri[:], 1.0).then_inc(sem("pool_fill"), 1)
        pool.memset(tris[0:NS, :], 1.0).then_inc(sem("pool_fill"), 1)
        pool.memset(bmask[:], 1.0).then_inc(sem("pool_fill"), 1)
        pool.memset(seqmask[:], 1.0).then_inc(sem("pool_fill"), 1)
        pool.memset(head_rows[:], 1.0).then_inc(sem("pool_fill"), 1)
        pool.memset(cpad[:], 0.0)
        pool.memset(raw[:], 0.0)
        pool.memset(lwa[:], 0.0)
        pool.memset(lwx[:], 0.0)
        pool.memset(col[:], 0.0).then_inc(sem("pool_fill"), 1)
        pool.wait_ge(sem("pool_fill"), 6)
        for c in (0, 2):
            pool.affine_select(out=tri[:, c * P:(c + 1) * P], in_=tri[:, c * P:(c + 1) * P], compare_op=ALU.is_ge, fill=0.0,
                               base=0, pattern=[[1, P]], channel_multiplier=-1)
        bt = sampled(tris[0:NS, :])
        pool.affine_select(out=bt, in_=bt, compare_op=ALU.is_ge, fill=0.0, base=0, pattern=[[-NT, ND], [0, NT]],
                           channel_multiplier=1).then_inc(sem("pool_fill"), 1)
        pool.affine_select(out=bmask[:], in_=bmask[:], compare_op=ALU.is_ge, fill=0.0, base=0, pattern=[[-NT, ND]],
                           channel_multiplier=1).then_inc(sem("pool_fill"), 1)
        pool.affine_select(out=head_rows[:], in_=head_rows[:], compare_op=ALU.is_ge, fill=0.0, base=0, pattern=[[1, NS]],
                           channel_multiplier=-NT).then_inc(sem("pool_fill"), 1)
        pool.wait_ge(sem("pool_fill"), 9)
        pool.affine_select(out=head_rows[:], in_=head_rows[:], compare_op=ALU.is_ge, fill=0.0, base=NT - 1,
                           pattern=[[-1, NS]], channel_multiplier=NT)
        pool.affine_select(out=bt, in_=bt, compare_op=ALU.is_ge, fill=0.0, base=0, pattern=[[NT, ND], [1, NT]],
                           channel_multiplier=-1)
        pool.affine_select(out=bmask[:], in_=bmask[:], compare_op=ALU.is_ge, fill=0.0, base=NT - 1,
                           pattern=[[NT, ND]], channel_multiplier=-1)
        pool.memset(seqmask[:, 0:1], 0.0)
        pool.memset(strided(seqmask[:], NP_, (NT, ND)), 0.0)
        pool.memset(col[0:72, 0:1], -1.0).then_inc(sem("pool_fill"), 1)
        pool.wait_ge(sem("pool_fill"), 10)
        pool.memset(col[SR, 0:1], 1.0).then_inc(sem("tables_ready"), 1)
        pool.wait_ge(sem("tables_ready"), 1)
        pool.dma_start(pid[:], I["page_table"].rearrange("b g -> (b g)").unsqueeze(0)).then_inc(sem("pid_loaded"), 16)
        for r0 in (0, 64):
            pool.dma_start(col[r0:r0 + H_ATT, 1:2], I["fox_b_f"][0].unsqueeze(1)).then_inc(sem("small_loaded"), 16)
        pool.dma_start(col[SR, 1:2], I["ssd_dt_bias"][0].unsqueeze(1)).then_inc(sem("small_loaded"), 16)
        pool.dma_start(col[SR, 2:3], I["ssd_a_log"][0].unsqueeze(1)).then_inc(sem("small_loaded"), 16)
        d = I["ssd_d"]
        for e in range(2):
            half = slice(e * HD, (e + 1) * HD)
            pool.dma_start(dcol[half, :].unsqueeze(2), bass.AP(d.tensor, d.offset + e, [[0, HD], [2, H_SSD // 2], [1, 1]]),
                           allow_slow_non_contiguous=True)\
                .then_inc(sem("small_loaded"), 16)
            for w, name in ((lwa, "lru_w_a"), (lwx, "lru_w_x")):
                pool.dma_start(w[half, :, half], I[name][0].rearrange("(c e) i j -> e i c j", e=2)[e])\
                    .then_inc(sem("small_loaded"), 16)
        pool.memset(ident[:], 0.0).then_inc(sem("ident_zero"), 1)
        pool.memset(ones[:], 1.0).then_inc(sem("const_ready"), 1)
        pool.wait_ge(sem("ident_zero"), 1)
        pool.affine_select(out=ident[:], in_=ident[:], compare_op=ALU.not_equal, fill=1.0, base=0,
                           pattern=[[-1, P]], channel_multiplier=1).then_inc(sem("const_ready"), 1)

        def sum_square(n, k):
            pool.wait_ge(sem("squared"), n * KT + k + 1)
            if isinstance(k, int) and k == 0:
                if n:
                    pool.wait_ge(sem("stat_ready"), n)
                pool.tensor_copy(ssum[:], sq[:, 0, :]).then_inc(sem("summed"), 1)
            else:
                raise AssertionError

        def sum_rest(n, k, odd):
            pool.wait_ge(sem("squared"), n * KT + k + 1)
            pool.wait_ge(sem("summed"), n * KT + k)
            pool.tensor_tensor(ssum[:], ssum[:], sq[:, odd, :], ALU.add).then_inc(sem("summed"), 1)

        def sums(n):
            sum_square(n, 0)
            sum_rest(n, 1, 1)
            with pool.Fori(1, KT // 2) as it:
                sum_rest(n, it * 2, 0)
                sum_rest(n, it * 2 + 1, 1)

        sums(0)
        pool.wait_ge(sem("x_turned"), 9)
        pool.memset(later[:], 1.0).then_inc(sem("later_step"), 1)
        pool.wait_ge(sem("later_step"), 1)
        lv = later[:].rearrange("p (b g) -> p b g", g=PAGES)
        pool.affine_select(out=lv, in_=lv, compare_op=ALU.is_gt, fill=0.0, base=PAGES,
                           pattern=[[PAGES, ND], [0, PAGES]], channel_multiplier=-1).then_inc(sem("later_step"), 1)
        pool.wait_ge(sem("later_step"), 2)
        pool.affine_select(out=lv, in_=lv, compare_op=ALU.is_gt, fill=0.0, base=0,
                           pattern=[[-PAGES, ND], [-1, PAGES]], channel_multiplier=1).then_inc(sem("later_step"), 1)
        pool.wait_ge(sem("masks_step"), 1)
        for g in range(2):
            mv = sampled(masks[:, g, :])
            pool.affine_select(out=mv, in_=mv, compare_op=ALU.is_ge, fill=0.0, base=P * g, pattern=[[-32, ND], [0, NT]],
                               channel_multiplier=1).then_inc(sem("masks_step"), 1)
        pool.wait_ge(sem("masks_step"), 3)
        for g in range(2):
            mv = sampled(masks[:, g, :])
            pool.affine_select(out=mv, in_=mv, compare_op=ALU.is_ge, fill=0.0, base=31 - P * g,
                               pattern=[[32, ND], [0, NT]], channel_multiplier=-1).then_inc(sem("masks_step"), 1)
        pool.wait_ge(sem("pid_loaded"), 16)
        lf_pages = I["cache_logf"][0].rearrange("n s h -> n (s h)")
        for i in range(ND * PAGES):
            page = pool.value_load(pid[0:1, i:i + 1], min_val=0, max_val=POOLP - 1)
            pool.dma_start(lfp[i:i + 1].rearrange("p s h -> p (s h)"), lf_pages[bass.ds(page, 1), :])\
                .then_inc(sem("lf_loaded"), 16)
        sums(1)
        pool.dma_start(x_save, xT[:]).then_inc(sem("x_saved"), 16)
        pool.wait_ge(sem("x_saved"), 16)
        pool.wait_ge(sem("xf_ready"), 2 * KT)
        pool.memset(qblk[:], 0.0)
        pool.memset(maskp[:], 0.0).then_inc(sem("maskp_step"), 1)
        pool.wait_ge(sem("maskp_step"), 1)
        for c in (0, 2):
            pool.affine_select(out=maskp[:, c * P:(c + 1) * P], in_=maskp[:, c * P:(c + 1) * P], compare_op=ALU.is_ge,
                               fill=-BIG, base=0, pattern=[[-1, P]], channel_multiplier=1).then_inc(sem("maskp_step"), 1)

        KO, VO = [O["k_prompt"][0, 0], O["k_sample"][0]], [O["v_prompt"][0, 0], O["v_sample"][0]]
        for step in STEPS:
            what, i = step[0], step[-1]
            if what == "suffix":
                pool.wait_ge(sem("sfx_ready"), 1)
                for b in range(ND):
                    pool.dma_start(suf_d[b].rearrange("h (g s) -> g h s", g=PAGES), sfx[b * PAGES:(b + 1) * PAGES, :, 1:])\
                        .then_inc(sem("suf_stored"), 16)
            elif what == "turn_gates":
                pool.wait_ge(sem("nat_ready"), 1)
                for b in range(2):
                    pool.dma_start(O["logf_prompt"][0, 0, toks(b), :], lfo[:, b, :]).then_inc(sem("kv_stored"), 16)
                pool.dma_start(O["logf_sample"][0].rearrange("b t h -> (b t) h"), lfo[0:NS, 2, :]).then_inc(sem("kv_stored"), 16)
            elif what == "turn_kv":
                for x in "kv":
                    for b in range(3):
                        copied(pool, x, b)
                for o, (po, so) in enumerate((KO, VO)):
                    pool.dma_start(po.rearrange("(b s) h d -> s b (h d)", s=P), kvn[:, 0:2, o * 512:(o + 1) * 512])\
                        .then_inc(sem("kv_stored"), 16)
                    pool.dma_start(so.rearrange("b t h d -> (b t) (h d)"), kvn[0:NS, 2, o * 512:(o + 1) * 512])\
                        .then_inc(sem("kv_stored"), 16)
            elif what == "keys":
                g = i // 8
                if i % 8 == 0:
                    pool.wait_ge(sem("suf_stored"), 16 * ND)
                    if g:
                        pool.wait_ge(sem("scores_read"), g)
                    for q in range(4):
                        src = suf_d[4 * g + q]
                        pool.dma_start(bias[32 * q:32 * (q + 1), :],
                                       bass.AP(src.tensor, src.offset, [[PAST, H_ATT], [0, NT], [1, PAST]]))\
                            .then_inc(sem("bias_loaded"), 16)
            elif what == "hist":
                copied(pool, "hist", i)
                so, po = ("ssd_conv_sample", "ssd_conv_prompt") if i < 3 else ("lru_conv_sample", "lru_conv_prompt")
                c = slice(i * 512, (i + 1) * 512) if i < 3 else slice(0, 512)
                pool.dma_start(O[po][0, 0, :, c], hout[0:HC, i % 2, :])\
                    .then_inc(sem(f"hist_stored{i % 2}"), 16)
                pool.dma_start(O[so][0].rearrange("b w c -> (b w) c")[:, c], hout[HC:HC + HC * ND, i % 2, :])\
                    .then_inc(sem(f"hist_stored{i % 2}"), 16)
            elif what == "lru_out":
                copied(pool, "lru_state")
                pool.dma_start(O["lru_state_prompt"][0], lrs[0:1, :]).then_inc(sem("lru_stored"), 16)
                pool.dma_start(O["lru_state_sample"][0], lrs[1:1 + ND, :]).then_inc(sem("lru_stored"), 16)
                for q in range(2):
                    pool.wait_ge(sem(f"hist_stored{q}"), 64)
                pool.wait_ge(sem("lru_done"), 1)
                pool.dma_start(xT[:], x_save).then_inc(sem("x_back"), 16)
            elif what == "state":
                copied(pool, "state", i)
                pool.dma_start(O["ssd_state_prompt"][0, 0, 8 * i:8 * i + 8].rearrange("(j e) p n -> (e p) j n", e=2),
                               sst[:, i, :].rearrange("q (j n) -> q j n", j=4)).then_inc(sem("state_stored"), 16)
            elif what == "ssd" and 1 <= i <= H_SSD:
                h = i - 1
                pool.wait_ge(sem("lseg_exp"), h + 1)
                if h == 0:
                    copied(pool, "cb", 1)
                if h >= 2:
                    if h % 2:
                        take(pool, "y", (h - 2) // 2)
                    else:
                        pool.wait_ge(sem("y_even"), h // 2)
                for n, cs in ((P, slice(0, 3 * P)), (NS, slice(3 * P, SEGW))):
                    m = pool.tensor_tensor(mseg[0:n, h % 2, cs], lseg[0:n, h % 2, cs], cbm[0:n, h // 8, cs], ALU.mult)
                m.then_inc(sem("mseg_ready"), 1)
        sums(2)
        sums(3)

    @block.tensor
    def _(pe):
        pe.wait_ge(sem("const_ready"), 2)
        pe.wait_ge(sem("gains_loaded"), 4 * 16)
        pe.transpose(bank[0][0:P, 0:64], gnat[:], ident[0:64, 0:64])
        pe.wait_ge(sem("params_loaded"), 8 * 16)
        pe.transpose(bank[0][0:P, 64:64 + NPAR], pnat[:], ident[0:NPAR, 0:NPAR]).then_inc(sem("params_turned"), 1)
        pe.wait_ge(sem("x_loaded"), 48)
        for b in range(2):
            for kg in range(4):
                to = bank[(1 + 4 * b + kg) % 8]
                if b == 1 and kg == 3:
                    pe.wait_ge(sem("params_kept"), 1)
                for k in range(4):
                    m = pe.transpose(to[:, k * P:(k + 1) * P], xnat[:, b, (4 * kg + k) * P:(4 * kg + k + 1) * P],
                                     ident[:])
                m.then_inc(sem("x_turned"), 1)
        pe.wait_ge(sem("x_kept"), 1)
        for k in range(KT):
            m = pe.transpose(bank[1][:, k * NS:(k + 1) * NS], xnat[0:NS, 2, k * P:(k + 1) * P], ident[0:NS, 0:NS])
        m.then_inc(sem("x_turned"), 1)
        pe.wait_ge(sem("hist_loaded"), 48)
        pe.wait_ge(sem("x_kept2"), 1)
        for c in range(16):
            pe.transpose(bank[2][:, c * 24:(c + 1) * 24], histn[:, c * P:(c + 1) * P], ident[0:24, 0:24])
        for c in range(4):
            pe.transpose(bank[2][:, 384 + c * ND:384 + (c + 1) * ND], h0n[:, c * P:(c + 1) * P], ident[0:ND, 0:ND])
        pe.wait_ge(sem("tables_ready"), 1)
        pe.wait_ge(sem("fold_ready"), 1)
        for r in range(4):
            m = pe.matmul(bank[2][32 * r:32 * r + 32, 416:420], tris[0:NS, :], fold[:], start=True, stop=True)
        m.then_inc(sem("hist_turned"), 1)

        def stat(n):
            pe.wait_ge(sem("summed"), (n + 1) * KT)
            pe.matmul(bank[STAT][:, 0:N], ones[:], ssum[:], start=True, stop=True).then_inc(sem("stat_ready"), 1)

        def products(out, slot, k, nk, rhs_hi, rhs_lo):
            hi = whi[:, slot, k * P:(k + 1) * P]
            lo = wlo[:, slot, k * P:(k + 1) * P]
            pe.matmul(out, hi, rhs_hi, start=k == 0, stop=False)
            pe.matmul(out, lo, rhs_hi, start=False, stop=False)
            return pe.matmul(out, hi, rhs_lo, start=False, stop=k == nk - 1)

        def up_pair(f, base, it4, m, first_norm):
            for j in range(2):
                i = base + it4 + 2 * m + j
                pe.wait_ge(sem("lo_done"), i + 1)
                for k in range(KT):
                    if first_norm and j == 0:
                        pe.wait_ge(sem("xn_ready"), FN[f] * KT + k + 1)
                    last = products(bank[(base + 2 * m + j) % 4][:, 0:N], (base + j) % 2, k, KT,
                                    xn_hi[:, k, :], xn_lo[:, k, :])
                last.then_inc(sem("w_used"), 1)
                if first_norm and j == 0:
                    stat(FN[f])

        def mix_tensor():
            def one_row(rows, r, n=P):
                return ident[rows, r:r + 1].to_broadcast([rows.stop - rows.start, n])

            def turn(out, src, n=P):
                return pe.transpose(out, src, ident[0:n, 0:n])

            def in_tile(t):
                i = IN0 + t
                pe.wait_ge(sem("lo_done"), i + 1)
                if t >= 2:
                    pe.wait_ge(sem("in_taken"), t - 1)
                elif t == 0:
                    pe.wait_ge(sem("x_added"), XO0 - 1)
                for k in range(KT):
                    if t == 0:
                        pe.wait_ge(sem("xn_ready"), KT + k + 1)
                    last = products(bank[t % 2][:, 0:N], i % 2, k, KT, xn_hi[:, k, :], xn_lo[:, k, :])
                last.then_inc(sem("w_used"), 1)
                if t == 0:
                    stat(1)

            def prompt_pv(h):
                to = claim(pe, "pv", h)[(h % 2) * HD:(h % 2 + 1) * HD, :]
                at = (h % 2) * 384
                v = slice(512 + h * HD, 512 + (h + 1) * HD)
                copied(pe, "p", h)
                pe.matmul(to[:, 0:P], kvn[:, 0, v], pts[:, at:at + P], start=True, stop=True)
                pe.matmul(to[:, P:NP_], kvn[:, 0, v], pts[:, at + P:at + NP_], start=True, stop=False)
                m = pe.matmul(to[:, P:NP_], kvn[:, 1, v], pts[:, at + NP_:at + 384], start=False, stop=True)
                m.then_inc(side_done("pv", h), 1)

            def key_scores(u):
                g, r, pg = u // 32, u // PAGES % 4, u % PAGES
                rows = slice(32 * r, 32 * r + 32)
                copied(pe, "kt", u)
                if u % 32 == 0:
                    pe.wait_ge(sem("qblk_ready"), g + 1)
                    if g:
                        pe.wait_ge(sem("scores_read"), g)
                    else:
                        pe.wait_ge(sem("x_added"), XO0)
                for p in range(4):
                    m = pe.matmul(bank[2 + pg // 4][rows, pg % 4 * P:(pg % 4 + 1) * P], qblk[:, r, p, :],
                                  kts[:, u % 2, p * P:(p + 1) * P], start=p == 0, stop=p == 3)
                m.then_inc(sem("kts_used"), 1)

            def ssd_y(h):
                if h % 2 == 0:
                    claim(pe, "y", h // 2)
                to = side("y", h // 2)[(h % 2) * HD:(h % 2 + 1) * HD, :]
                c = slice(h * HD, (h + 1) * HD)
                m = mseg[:, h % 2, :]
                pe.wait_ge(sem("mseg_ready"), h + 1)
                pe.matmul(to[:, 0:P], xsn[:, 0, c], m[:, 0:P], start=True, stop=True)
                pe.matmul(to[:, P:NP_], xsn[:, 0, c], m[:, P:NP_], start=True, stop=False)
                pe.matmul(to[:, P:NP_], xsn[:, 1, c], m[:, NP_:3 * P], start=False, stop=True)
                last = pe.matmul(to[:, NP_:N], xsn[0:NS, 2, c], m[0:NS, 3 * P:SEGW], start=True, stop=True)
                last.then_inc(side_done("y", h // 2) if h % 2 else sem("y_even"), 1)

            def out_tile(part, n, it4, first):
                i = OUT0 + part * KT + n + it4
                pe.wait_ge(sem("lo_done"), i + 1)
                if not (first and part == 0 and n < 2):
                    pe.wait_ge(sem("x_added"), XO0 + part * KT + n + it4 - 1)
                for k in range(8):
                    if part == 0:
                        rhs = [x[:, k + 8 * (k >= 4), :] for x in (xn_hi, xn_lo)]
                    else:
                        rhs = [x[:, k, :] for x in (m_hi, m_lo)]
                    last = products(bank[n % 2][:, 0:N], (OUT0 + n) % 2, k, 8, *rhs)
                last.then_inc(sem("w_used"), 1)

            for step in STEPS:
                what, i = step[0], step[-1]
                if what == "in" and i < IN_TILES:
                    in_tile(i)
                elif what == "suffix":
                    to = claim(pe, "later")
                    pe.wait_ge(sem("total_ready"), 1)
                    pe.wait_ge(sem("later_step"), 3)
                    pe.matmul(to[0:64, 0:H_ATT], later[:], total[:], start=True, stop=True)\
                        .then_inc(side_done("later"), 1)
                elif what == "turn_gates":
                    to = claim(pe, "nat")
                    pe.wait_ge(sem("decay_ready"), 1)
                    for b in range(3):
                        for pl in range(3):
                            turn(to[0:rows_of(b), b * 144 + pl * 48:b * 144 + pl * 48 + 48], sc48[0:48, pl, toks(b)], 48)
                    turn(to[0:NS, 432:480], e48[0:48, :], 48).then_inc(side_done("nat"), 1)
                    to = claim(pe, "dec")
                    for j in range(8):
                        for e in range(2):
                            m = pe.matmul(to[e * HD:(e + 1) * HD, j * ND:(j + 1) * ND], one_row(SR, 32 + 2 * j + e, HD),
                                          strided(e48[SR, :], NT - 1, (NT, ND)), start=True, stop=True)
                    m.then_inc(side_done("dec"), 1)
                elif what == "turn_kv":
                    for b in range(3):
                        for x, src in (("k", kT), ("v", attT)):
                            to = claim(pe, x, b)
                            pe.wait_ge(sem("in_taken"), T_V if x == "k" else T_X)
                            for j in range(4):
                                m = turn(to[0:rows_of(b), j * P:(j + 1) * P], src[:, j, toks(b)])
                            m.then_inc(side_done(x, b), 1)
                elif what == "prompt":
                    if i < H_ATT:
                        to = claim(pe, "sc", i)
                        f = slice((i % 2) * HD, (i % 2 + 1) * HD)
                        c = slice((i % 2) * HD, (i % 2) * HD + H_ATT)
                        if i == 0:
                            pe.wait_ge(sem("negc_ready"), 1)
                        for out, q, k in ((to[:, 0:P], slice(0, P), slice(0, P)),
                                          (to[:, P:384], slice(P, NP_), slice(0, NP_))):
                            pe.matmul(out, qT[f, i // 2, q], kT[f, i // 2, k], start=True, stop=False)
                            m = pe.matmul(out, one_row(c, c.start + i), negc[c, k], start=False, stop=True)
                        m.then_inc(side_done("sc", i), 1)
                    if 1 <= i <= H_ATT:
                        to = claim(pe, "p", i - 1)
                        pe.wait_ge(sem("probs_ready"), i)
                        for q in range(3):
                            at = (i - 1) % 2 * 384 + q * P
                            m = turn(to[:, q * P:(q + 1) * P], ps[:, at:at + P])
                        m.then_inc(side_done("p", i - 1), 1)
                    if i >= 2:
                        prompt_pv(i - 2)
                elif what == "keys":
                    g = i // 8
                    for u in range(4 * i, 4 * i + 4):
                        to = claim(pe, "kt", u)
                        pe.wait_ge(sem(f"cache_k_loaded{u % 4}"), 16 * (u // 4 + 1))
                        for p in range(4):
                            m = turn(to[:, p * P:(p + 1) * P], kpage[:, u % 4, p * P:(p + 1) * P])
                        m.then_inc(side_done("kt", u), 1)
                        if u % 32:
                            key_scores(u - 1)
                    if i % 8 == 7:
                        key_scores(u)
                        if g:
                            pe.wait_ge(sem("att_o_ready"), g)
                        else:
                            pe.wait_ge(sem("x_added"), XO0)
                        for q in range(4):
                            rows = slice(32 * q, 32 * q + 32)
                            for p in range(4):
                                pe.matmul(bank[4][rows, 0:NS], qblk[:, q, p, :], kT[:, p, NP_:N], start=p == 0, stop=False)
                            m = pe.matmul(bank[4][rows, 0:NS], head_rows[:], negc[0:H_ATT, NP_:N],
                                          start=False, stop=True)
                        m.then_inc(sem("scores_ready"), 1)
                elif what == "probs":
                    pe.wait_ge(sem("sexp_ready"), i + 1)
                    for q in range(3):
                        to = claim(pe, "pt", i, q)
                        for c in range(4 if q < 2 else 1):
                            at = q * 512 + c * P
                            if q < 2:
                                m = turn(to[:, c * P:(c + 1) * P], ps[:, at:at + P])
                            else:
                                m = turn(to[0:NS, 0:P], ps[:, at:at + NS])
                        m.then_inc(side_done("pt", i, q), 1)
                elif what == "values":
                    r = i % 4
                    if r == 0:
                        copied(pe, "pt", i // 4, 2)
                    rows = slice(32 * r, 32 * r + 32)
                    for pg in range(PAGES):
                        u = PAGES * i + pg
                        pe.wait_ge(sem(f"cache_v_loaded{u % VRING}"), 16 * (u // VRING + 1))
                        pe.matmul(bank[4][rows, :], pts[:, pg * P + 32 * r:pg * P + 32 * r + 32],
                                  vpage[:, u % VRING, :], start=pg == 0, stop=False).then_inc(sem("vpage_used"), 1)
                    m = pe.matmul(bank[4][rows, :], pts[0:NS, PAST + 32 * r:PAST + 32 * r + 32], kvn[0:NS, 2, 512:],
                                  start=False, stop=True)
                    if r == 3:
                        m.then_inc(sem("sample_pv"), 1)
                elif what == "merge_heads":
                    to = claim(pe, "heads", i)
                    pe.wait_ge(sem("att_o_ready"), i + 1)
                    for p in range(4):
                        m = turn(to[:, p * P:(p + 1) * P], att_o[:, p * P:(p + 1) * P])
                    m.then_inc(side_done("heads", i), 1)
                elif what == "lru_gates":
                    pe.wait_ge(sem("conv_done"), XT_ + LT_)
                    pe.wait_ge(sem("small_loaded"), 16 * 10)
                    for c in range(4):
                        for x, w in (("r", lwa), ("i", lwx)):
                            to = claim(pe, x, c)
                            pe.matmul(to[:, 0:N], w[:, c, :], uT[:, c, :], start=True, stop=True)\
                                .then_inc(side_done(x, c), 1)
                elif what == "hist":
                    to = claim(pe, "hist", i)
                    pe.wait_ge(sem("conv_done"), XT_ + LT_)
                    for c in range(4):
                        m = turn(to[0:HC + HC * ND, c * P:(c + 1) * P], histO[:, 4 * i + c, :])
                    m.then_inc(side_done("hist", i), 1)
                elif what == "lru_out":
                    to = claim(pe, "lru_state")
                    pe.wait_ge(sem("lst_ready"), 1)
                    for c in range(4):
                        m = turn(to[0:1 + ND, c * P:(c + 1) * P], lst[:, c, :])
                    m.then_inc(side_done("lru_state"), 1)
                elif what == "turn_x":
                    pe.wait_ge(sem("conv_silu"), 3)
                    for half in range(2):
                        to = claim(pe, "x", i, half)
                        for c in range(4):
                            m = turn(to[0:rows_of(i), c * P:(c + 1) * P], xsT[:, 4 * half + c, toks(i)])
                        m.then_inc(side_done("x", i, half), 1)
                    to = claim(pe, "b", i)
                    for c in range(2):
                        m = turn(to[0:rows_of(i), c * P:(c + 1) * P], xsT[:, 8 + c, toks(i)])
                    m.then_inc(side_done("b", i), 1)
                elif what == "scores":
                    for g in range(2):
                        to = claim(pe, "cb", g)
                        for cs, kb, q in PAIRS:
                            m = pe.matmul(to[0:rows_of(kb), cs], xsT[:, 8 + g, toks(kb)], xsT[:, 10 + g, q],
                                          start=True, stop=True)
                        m.then_inc(side_done("cb", g), 1)
                elif what == "ssd":
                    if i < H_SSD:
                        to = claim(pe, "acs", i)
                        pe.matmul(to[:, 0:N], one_row(SR, 32 + i), sc48[SR, CS, :], start=True, stop=True)\
                            .then_inc(side_done("acs", i), 1)
                    if i >= 2:
                        ssd_y(i - 2)
                elif what == "merge":
                    pe.wait_ge(sem("merged"), 8)
                elif what == "out":
                    out_tile(0, i, 0, True)
                elif what == "state":
                    to = claim(pe, "state", i)
                    pe.wait_ge(sem("xw_ready"), 1)
                    for j in range(4):
                        c = 4 * i + j
                        for b in range(2):
                            m = pe.matmul(to[:, j * P:(j + 1) * P], xsn[:, b, c * P:(c + 1) * P], bnat[:, b, i * ST:(i + 1) * ST],
                                          start=b == 0, stop=b == 1)
                    m.then_inc(side_done("state", i), 1)
                elif what == "unit":
                    if i < 2 * ND:
                        to = claim(pe, "ht", i)
                        pe.wait_ge(sem(f"h0_loaded{i % 4}"), 16 * (i // 4 + 1))
                        for j in range(4):
                            m = turn(to[:, j * P:(j + 1) * P], h0[:, i % 4, j * P:(j + 1) * P])
                        m.then_inc(side_done("ht", i), 1)
                    if i:
                        b, g = (i - 1) // 2, (i - 1) % 2
                        to = claim(pe, "up", i - 1)
                        pe.wait_ge(sem("bexp_ready"), b + 1)
                        for j in range(4):
                            c = 4 * g + j
                            m = pe.matmul(to[:, j * P:(j + 1) * P], xsn[0:NS, 2, c * P:(c + 1) * P],
                                          bexp[0:NS, b % 4, g * ST:(g + 1) * ST], start=True, stop=True)
                        m.then_inc(side_done("up", i - 1), 1)
                        copied(pe, "ht", i - 1)
                        pe.matmul(bank[2 + g][0:NS, :], cpad[:, g, b, :], h0t[:, (i - 1) % 2, :], start=b == 0, stop=b == ND - 1)\
                            .then_inc(sem("h0t_used"), 1)
                elif what == "carry":
                    to = claim(pe, "ys")
                    pe.wait_ge(sem("ys_ready"), 2)
                    for j in range(8):
                        m = turn(to[:, j * NS:(j + 1) * NS], ys[0:NS, j * P:(j + 1) * P], NS)
                    m.then_inc(side_done("ys"), 1)
                elif what == "group":
                    to = claim(pe, "mean", i)
                    for j in range(4):
                        pe.wait_ge(sem("y_squared"), 4 * i + j + 1)
                        m = pe.matmul(to[:, 0:N], ones[:], ysq[:, 4 * i + j, :], start=j == 0, stop=j == 3)
                    m.then_inc(side_done("mean", i), 1)
            pe.wait_ge(sem("merged"), 16)
            for j in range(4):
                out_tile(1, j, 0, True)
            with pe.Fori(1, KT // 4) as it:
                for j in range(4):
                    out_tile(1, j, it * 4, False)

        for f in range(2):
            if f:
                mix_tensor()
            for g, n in enumerate(GROUPS):
                base, ff0, xa0 = seg["up", f, g], FF0[f, g], XA0[f, g]
                for m in range(3):
                    if m == 0 and xa0:
                        pe.wait_ge(sem("x_added"), xa0 - 2)
                    if m == 1 and xa0:
                        pe.wait_ge(sem("x_added"), xa0)
                    if m == 2:
                        pe.wait_ge(sem("gated"), ff0 + 1)
                    up_pair(f, base, 0, m, g == 0 and m == 0)
                with pe.Fori(0, (n - 3) // 2) as it:
                    for m in range(2):
                        pe.wait_ge(sem("gated"), it * 2 + (ff0 + m + 2))
                        up_pair(f, base + 6, it * 4, m, False)
                base = seg["down", f, g]

                def down(it4, j, first):
                    i = base + it4 + j
                    pe.wait_ge(sem("lo_done"), i + 1)
                    if first:
                        pe.wait_ge(sem("gated"), ff0 + n - 1 + (j >= 2))
                    else:
                        pe.wait_ge(sem("x_added"), xa0 + it4 + j - 3)
                    for k in range(n):
                        if first and j == 0 and k in (0, n - 1):
                            pe.wait_ge(sem("h_ready"), ff0 + (n - 1 if k == 0 else n))
                        last = products(bank[(base + j) % 4][:, 0:N], (base + j) % 2, k, n,
                                        h_hi[:, k, :], h_lo[:, k, :])
                    last.then_inc(sem("w_used"), 1)

                for j in range(4):
                    down(0, j, True)
                with pe.Fori(1, KT // 4) as it:
                    for j in range(4):
                        down(it * 4, j, False)
        pe.wait_ge(sem("summed"), 4 * KT)
        pe.matmul(bank[STAT][:, 0:3], ones[:], ones[:, 0:3], start=True, stop=True)
        for b in range(3):
            m = pe.matmul(bank[STAT][0:rows_of(b), b:b + 1], ssum[:, toks(b)], ones[:, 0:1], start=True, stop=True)
        m.then_inc(sem("stat_ready"), 1)
        for kg in range(4):
            for b in range(3):
                rows = P if b < 2 else NS
                t = 3 * kg + b
                if t >= 7:
                    pe.wait_ge(sem("y_ready2" if (t - 7) % 2 else "y_ready"), (t - 7) // 2 + 1)
                for k in range(4):
                    pe.wait_ge(sem("xf_ready"), 3 * KT + 4 * kg + k + 1)
                    m = pe.transpose(bank[t % 7][0:rows, k * P:(k + 1) * P], yT[:, 4 * kg + k, b * P:b * P + rows],
                                     ident[:])
                m.then_inc(sem("y_turned"), 1)

    @block.scalar
    def _(act):
        for b in range(2):
            for kg in (1, 3):
                act.wait_ge(sem("x_turned"), 4 * b + kg + 1)
                act.copy(xT[:, 4 * kg:4 * kg + 4, b * P:(b + 1) * P],
                         bank[(1 + 4 * b + kg) % 8][:, :].rearrange("p (k t) -> p k t", k=4)).then_inc(sem("x_kept2"), 1)

        def square(n, k, odd, wait_pool):
            if wait_pool:
                act.wait_ge(sem("summed"), n * KT + k - 1)
            act.activation(sq[:, odd, :], xT[:, bass.ds(k, 1), :].rearrange("p o t -> p (o t)"), ACT.Square)\
                .then_inc(sem("squared"), 1)

        def hi(base, it4, j, nk):
            i = base + it4 + j
            slot = (base + j) % LOADS
            act.wait_ge(sem(f"raw_ready{slot}"), 16 * ((base + j) // LOADS + 1) + it4 * 4)
            if not isinstance(i, int) or i >= 2:
                act.wait_ge(sem("w_used"), i - 1)
            act.copy(tile_ap(whi, (base + j) % 2, nk), tile_ap(wraw, slot, nk)).then_inc(sem("hi_done"), 1)

        def silu(ff, par):
            act.wait_ge(sem("scaled"), ff + 1)
            act.activation(sg[:, par, :], sg[:, par, :], ACT.Silu).then_inc(sem("silu_done"), 1)

        def root(n):
            act.wait_ge(sem("mean_ready"), n + 1)
            act.activation(rs[:, 1, :], rs[:, 0, :], ACT.Ln).then_inc(sem("root_step"), 1)
            act.wait_ge(sem("root_step"), 2 * n + 1)
            act.activation(rs[:, 1, :], rs[:, 1, :], ACT.Exp, scale=-0.5).then_inc(sem("root_step"), 1)

        def finish_x(n, k, odd, wait_pool):
            act.wait_ge(sem("xf_ready"), n * KT + k + 1)
            if n < 3:
                act.copy(xn_hi[:, bass.ds(k, 1), :].rearrange("p o t -> p (o t)"), xf[:, odd, :])\
                    .then_inc(sem("xhi_ready"), 1)
            square(n, k, odd, wait_pool)

        def mix_scalar():
            def hi_mix(n):
                if n < IN_TILES:
                    hi(IN0, 0, n, KT)
                else:
                    n -= IN_TILES
                    act.wait_ge(sem(f"wo_half{(OUT0 + n) % LOADS}"), 16 * (n // 4 + 1))
                    hi(OUT0, 0, n, 8)

            act.wait_ge(sem("w_small"), 32)
            hi_mix(0)
            finish_x(1, KT - 1, 1, True)
            for step in STEPS:
                what, i = step[0], step[-1]
                if what == "in":
                    if i == 1:
                        root(1)
                    if i < IN_TILES:
                        hi_mix(i + 1)
                    if i in (T_Z + 5, T_Z + 8):
                        q = (i - T_Z) // 8
                        act.wait_ge(sem("in_taken"), T_Z + 4 * q + 4)
                        act.activation(zT[:, 4 * q:4 * q + 4, :], zT[:, 4 * q:4 * q + 4, :], ACT.Silu)\
                            .then_inc(sem("z_silu"), 1)
                    if i in (T_X + 5, T_X + 9, T_X + 13):
                        q = (i - T_X - 5) // 4
                        act.wait_ge(sem("conv_done"), 4 * q + 4)
                        act.activation(xsT[:, 4 * q:4 * q + 4, :], xsT[:, 4 * q:4 * q + 4, :], ACT.Silu)\
                            .then_inc(sem("conv_silu"), 1)
                elif what == "gates":
                    act.wait_ge(sem("abs_ready"), 1)
                    act.activation(ps[0:72, 0:N], ps[0:72, 0:N], ACT.Exp, scale=-1.0).then_inc(sem("exp_ready"), 1)
                    act.wait_ge(sem("abs_ready"), 2)
                    act.activation(lam[:, 1, :], lam[:, 1, :], ACT.Exp, scale=-1.0).then_inc(sem("exp_ready"), 1)
                    act.wait_ge(sem("tables_ready"), 1)
                    act.wait_ge(sem("small_loaded"), 16 * 10)
                    act.activation(col[0:72, 3:4], col[0:72, 2:3], ACT.Exp).then_inc(sem("coef_ready"), 1)
                    act.wait_ge(sem("sums_ready"), 1)
                    act.activation(e48[0:72, :], sc48[0:72, CS, NP_:N], ACT.Exp)
                    act.activation(sc48[0:72, WDC, :], sc48[0:72, WDC, :], ACT.Exp).then_inc(sem("decay_ready"), 1)
                elif what == "turn_kv":
                    for b in range(3):
                        src = take(act, "v", b)
                        act.copy(kvn[0:rows_of(b), b, 512:], src[0:rows_of(b), :]).then_inc(side_read("v", b), 1)
                elif what == "prompt":
                    if i < H_ATT:
                        act.wait_ge(sem("fox_max"), i + 1)
                        for b, c in enumerate((slice(0, P), slice(P, 384))):
                            w = ps[:, (i % 2) * 384 + c.start:(i % 2) * 384 + c.stop]
                            n = 2 * (i % 2) + b
                            m = act.activation(w, w, ACT.Exp, bias=nm[:, n:n + 1], accum_out=rsum[:, n:n + 1])
                        m.then_inc(sem("fox_exp"), 1)
                    if 1 <= i <= H_ATT:
                        h = i - 1
                        src = take(act, "p", h)
                        if h >= 2:
                            take(act, "pv", h - 2)
                        act.copy(pts[:, h % 2 * 384:(h % 2 + 1) * 384], src[:, 0:384]).then_inc(side_read("p", h), 1)
                elif what == "keys":
                    for u in range(4 * i, 4 * i + 4):
                        src = take(act, "kt", u)
                        if u >= 2:
                            act.wait_ge(sem("kts_used"), u - 1)
                        act.copy(kts[:, u % 2, :], src[:, :]).then_inc(side_read("kt", u), 1)
                elif what == "max":
                    act.wait_ge(sem("sample_max"), i + 1)
                    act.activation(ps[:, 0:PAST + NS], ps[:, 0:PAST + NS], ACT.Exp, bias=nm[:, 0:1],
                                   accum_out=rsum[:, 0:1]).then_inc(sem("sexp_ready"), 1)
                elif what == "probs":
                    for q in range(3):
                        src = take(act, "pt", i, q)
                        if q == 0:
                            if i:
                                act.wait_ge(sem("sample_pv"), i)
                            else:
                                take(act, "pv", H_ATT - 1)
                        if q < 2:
                            m = act.copy(pts[:, q * 512:(q + 1) * 512], src[:, :])
                        else:
                            m = act.copy(pts[0:NS, PAST:PAST + P], src[0:NS, 0:P])
                        m.then_inc(side_read("pt", i, q), 1)
                elif what == "lru_gates":
                    for c in range(4):
                        for x, to, r0 in (("r", lru_r, R_BA), ("i", lru_i, R_BX)):
                            src = take(act, x, c)
                            act.activation(to[:, c, :], src[:, 0:N], ACT.Sigmoid, bias=params[:, r0 + c:r0 + c + 1])\
                                .then_inc(side_read(x, c), 1)
                elif what == "lru_decay":
                    for x, c in (("r", 3), ("i", 3), ("i", 2)):
                        copied(act, x, c)
                    for c in range(4):
                        act.activation(lru_a[:, c, :], lru_r[:, c, :], ACT.Exp, scale=lam[:, 2, c:c + 1])
                    for c in range(4):
                        m = act.activation(lru_r[:, c, :], lru_r[:, c, :], ACT.Tanh, scale=lam[:, 0, c:c + 1])
                    m.then_inc(sem("lru_decayed"), 1)
                elif what == "hist":
                    src = take(act, "hist", i)
                    if i >= 2:
                        act.wait_ge(sem(f"hist_stored{i % 2}"), 32)
                    act.copy(hout[0:HC + HC * ND, i % 2, :], src[0:HC + HC * ND, :]).then_inc(side_read("hist", i), 1)
                elif what == "lru_scan":
                    act.wait_ge(sem("lru_square"), 1)
                    act.activation(uT[:], uT[:], ACT.Sqrt).then_inc(sem("lru_root"), 1)
                elif what == "lru_out":
                    act.wait_ge(sem("in_taken"), T_Z)
                    act.activation(gT[:], gT[:], ACT.Gelu_apprx_tanh).then_inc(sem("g_ready"), 1)
                elif what == "merge":
                    act.wait_ge(sem("w_used"), IN0 + IN_TILES)
                    copied(act, "heads", 1)
                    act.copy(xn_hi[:, 0:4, :], attT[:])
                    act.wait_ge(sem("lru_done"), 1)
                    act.copy(xn_hi[:, 12:16, :], gT[:]).then_inc(sem("m_rounded"), 1)
                elif what == "ssd":
                    if i < H_SSD:
                        copied(act, "acs", i)
                        w, s = lseg[:, i % 2, 0:3 * P], lseg[0:NS, i % 2, 3 * P:]
                        act.activation(w, w, ACT.Exp)
                        act.activation(s, s, ACT.Exp).then_inc(sem("lseg_exp"), 1)
                elif what == "out":
                    hi_mix(IN_TILES + i + 1)
                elif what == "state":
                    src = take(act, "state", i)
                    act.copy(sst[:, i, :], src[:, :]).then_inc(side_read("state", i), 1)
                elif what == "unit" and i < 2 * ND:
                    src = take(act, "ht", i)
                    if i >= 2:
                        act.wait_ge(sem("h0t_used"), i - 1)
                    act.copy(h0t[:, i % 2, :], src[:, :]).then_inc(side_read("ht", i), 1)
                elif what == "gate":
                    act.wait_ge(sem("gated_y"), 1)
                    for j in range(8):
                        act.activation(ysq[:, j, :], xsT[:, j, :], ACT.Square).then_inc(sem("y_squared"), 1)
                elif what == "group":
                    copied(act, "mean", i)
                    act.activation(rs[:, 1, :], rs[:, 0, :], ACT.Ln).then_inc(sem("groot_step"), 1)
                    act.wait_ge(sem("groot_step"), 2 * i + 1)
                    act.activation(rs[:, 1, :], rs[:, 1, :], ACT.Exp, scale=-0.5).then_inc(sem("groot_step"), 1)
                    act.wait_ge(sem("yn_done"), i + 1)
                    if i == 0:
                        for q in range(2):
                            act.wait_ge(sem(f"snew_stored{q}"), 16 * ND)
                    act.copy(m_hi[:, 4 * i:4 * i + 4, :], zT[:, 4 * i:4 * i + 4, :]).then_inc(sem("m_rounded"), 1)
            for j in range(1, 4):
                hi_mix(IN_TILES + KT + j)
                if j >= 2:
                    finish_x(2, j - 2, j % 2, False)
            with act.Fori(1, KT // 4) as it:
                for j in range(4):
                    act.wait_ge(sem(f"wo_half{(OUT0 + j) % LOADS}"), it * 16 + 16 * 5)
                    hi(OUT0 + KT, it * 4, j, 8)
                    finish_x(2, it * 4 + (j - 2), j % 2, True)
            finish_x(2, KT - 2, 0, True)
            for q in range(2):
                act.wait_ge(sem(f"snew_stored{q}"), 16 * ND)

        for f in range(2):
            if f:
                mix_scalar()
            hi(seg["up", f, 0], 0, 0, KT)
            if f == 0:
                hi(0, 0, 1, KT)
                act.wait_ge(sem("x_kept2"), 4)
                act.wait_ge(sem("x_kept"), 5)
                for k in range(KT):
                    finish_x(0, k, k % 2, k >= 2)
            else:
                finish_x(2, KT - 1, 1, True)
                hi(seg["up", f, 0], 0, 1, KT)
            root(FN[f])
            for g, n in enumerate(GROUPS):
                base, ff0 = seg["up", f, g], FF0[f, g]
                for m in range(3):
                    for j in range(2):
                        if g or m:
                            hi(base + 2 * m, 0, j, KT)
                    silu(ff0 + m, (ff0 + m) % 2)
                with act.Fori(0, (n - 3) // 2) as it:
                    for m in range(2):
                        for j in range(2):
                            hi(base + 6, it * 4, 2 * m + j, KT)
                        silu(it * 2 + (ff0 + 3 + m), (ff0 + 3 + m) % 2)
                base = seg["down", f, g]
                for j in range(4):
                    hi(base, 0, j, n)
                    if g == 2 and j >= 2:
                        finish_x(FN[f] + 1, j - 2, j % 2, False)
                with act.Fori(1, KT // 4) as it:
                    for j in range(4):
                        hi(base, it * 4, j, n)
                        if g == 2:
                            finish_x(FN[f] + 1, it * 4 + (j - 2), j % 2, True)
                if g == 2:
                    finish_x(FN[f] + 1, KT - 2, 0, True)
        finish_x(3, KT - 1, 1, True)
        act.wait_ge(sem("mean_ready"), 4)
        act.activation(rs[:, 1, 0:3], rs[:, 0, 0:3], ACT.Ln).then_inc(sem("root_step"), 1)
        act.wait_ge(sem("root_step"), 7)
        act.activation(rs[:, 1, 0:3], rs[:, 1, 0:3], ACT.Exp, scale=-0.5).then_inc(sem("root_step"), 1)
        for kg in range(4):
            for b in range(3):
                t = 3 * kg + b
                if t % 2:
                    rows = P if b < 2 else NS
                    act.wait_ge(sem("y_turned"), t + 1)
                    act.wait_ge(sem("newton"), 16)
                    act.activation(ynat[0:rows, b, kg * 512:(kg + 1) * 512], bank[t % 7][0:rows, :], ACT.Copy,
                                   scale=rs[0:rows, 2, b:b + 1]).then_inc(sem("y_ready2"), 1)

    @block.vector
    def _(dve):
        dve.wait_ge(sem("params_turned"), 1)
        dve.tensor_copy(gains[:].rearrange("p n k -> p (n k)"), bank[0][:, 0:64])
        dve.tensor_copy(params[:], bank[0][:, 64:64 + NPAR]).then_inc(sem("params_kept"), 1)
        for b in range(2):
            for kg in (0, 2):
                dve.wait_ge(sem("x_turned"), 4 * b + kg + 1)
                dve.tensor_copy(xT[:, 4 * kg:4 * kg + 4, b * P:(b + 1) * P],
                                bank[(1 + 4 * b + kg) % 8][:, :].rearrange("p (k t) -> p k t", k=4))\
                    .then_inc(sem("x_kept"), 1)
        dve.wait_ge(sem("x_turned"), 9)
        dve.tensor_copy(xT[:, :, NP_:], bank[1][:, :].rearrange("p (k t) -> p k t", k=KT)).then_inc(sem("x_kept"), 1)

        def root(n, w=N):
            y, z, v = rs[:, 1, 0:w], rs[:, 2, 0:w], rs[:, 0, 0:w]
            dve.wait_ge(sem("stat_ready"), n + 1)
            dve.tensor_scalar(v, bank[STAT][:, 0:w], 1.0 / D, EPS, ALU.mult, ALU.add).then_inc(sem("mean_ready"), 1)
            dve.wait_ge(sem("root_step"), 2 * n + 2)
            dve.tensor_tensor(z, y, y, ALU.mult).then_inc(sem("newton"), 1)
            dve.wait_ge(sem("newton"), 4 * n + 1)
            dve.tensor_tensor(z, z, v, ALU.mult).then_inc(sem("newton"), 1)
            dve.wait_ge(sem("newton"), 4 * n + 2)
            dve.tensor_scalar(z, z, -0.5, 1.5, ALU.mult, ALU.add).then_inc(sem("newton"), 1)
            dve.wait_ge(sem("newton"), 4 * n + 3)
            dve.tensor_tensor(z, z, y, ALU.mult).then_inc(sem("newton"), 1)
            dve.wait_ge(sem("newton"), 4 * n + 4)

        def scale_x(n, k, odd, added=None):
            if added is not None:
                dve.wait_ge(sem("x_added"), added)
            gain = gains[:, n, bass.ds(k, 1)]
            xk = xT[:, bass.ds(k, 1), :].rearrange("p o t -> p (o t)")
            if n == 3:
                to = yT[:, bass.ds(k, 1), :].rearrange("p o t -> p (o t)")
            else:
                to = xf[:, odd, :]
                if n or k >= 2:
                    dve.wait_ge(sem("xn_ready"), n * KT + k - 1)
            dve.tensor_scalar(to, xk, gain, None, ALU.mult).then_inc(sem("xf_ready"), 1)

        def split_x(n, k, odd):
            if n < 3:
                dve.wait_ge(sem("xhi_ready"), n * KT + k + 1)
                dve.tensor_tensor(xn_lo[:, bass.ds(k, 1), :].rearrange("p o t -> p (o t)"), xf[:, odd, :],
                                  xn_hi[:, bass.ds(k, 1), :].rearrange("p o t -> p (o t)").bitcast(F32), ALU.subtract)\
                    .then_inc(sem("xn_ready"), 1)

        def lo(base, it4, j, nk):
            i = base + it4 + j
            dve.wait_ge(sem("hi_done"), i + 1)
            s = (base + j) % 2
            dve.tensor_tensor(tile_ap(wlo, s, nk), tile_ap(wraw, (base + j) % LOADS, nk),
                              tile_ap(whi, s, nk).bitcast(F32), ALU.subtract).then_inc(sem("lo_done"), 1)

        def pre(i, bk, ff, par):
            dve.wait_ge(sem("w_used"), i + 1)
            if not isinstance(ff, int) or ff >= 2:
                dve.wait_ge(sem("gated"), ff - 1)
            dve.tensor_tensor(sg[:, par, :], bank[bk][:, 0:N], rs[:, 2, :], ALU.mult).then_inc(sem("scaled"), 1)

        def gate(i, bk, ff, par, slot):
            dve.wait_ge(sem("w_used"), i + 1)
            if not isinstance(ff, int) or ff >= 2:
                dve.wait_ge(sem("h_ready"), ff - 1)
            dve.tensor_tensor(hm[:, par, :], bank[bk][:, 0:N], rs[:, 2, :], ALU.mult).then_inc(sem("up_scaled"), 1)
            dve.wait_ge(sem("up_scaled"), ff + 1)
            dve.wait_ge(sem("silu_done"), ff + 1)
            dve.tensor_tensor(hm[:, par, :], hm[:, par, :], sg[:, par, :], ALU.mult).then_inc(sem("gated"), 1)
            dve.wait_ge(sem("gated"), ff + 1)
            dve.tensor_copy(h_hi[:, bass.ds(slot, 1), :].rearrange("p o t -> p (o t)"), hm[:, par, :])\
                .then_inc(sem("h_rounded"), 1)
            dve.wait_ge(sem("h_rounded"), ff + 1)
            dve.tensor_tensor(h_lo[:, bass.ds(slot, 1), :].rearrange("p o t -> p (o t)"), hm[:, par, :],
                              h_hi[:, bass.ds(slot, 1), :].rearrange("p o t -> p (o t)").bitcast(F32),
                              ALU.subtract).then_inc(sem("h_ready"), 1)

        def add_x(i, bk, n_add, before, k, scale):
            dve.wait_ge(sem("w_used"), i + 1)
            if before is not None:
                dve.wait_ge(sem("x_added"), before)
            xk = xT[:, bass.ds(k, 1), :].rearrange("p o t -> p (o t)")
            dve.scalar_tensor_tensor(out=xk, in0=bank[bk][:, 0:N], scalar=scale, in1=xk, op0=ALU.mult,
                                     op1=ALU.add).then_inc(sem("x_added"), 1)

        class Chain:
            n = 0

            def __call__(self, instruction):
                instruction.then_inc(sem("chain"), 1)
                self.n += 1
                dve.wait_ge(sem("chain"), self.n)

        chain = Chain()

        def absolute(e, v):
            dve.scalar_tensor_tensor(out=e, in0=v, scalar=-1.0, in1=v, op0=ALU.mult, op1=ALU.max)\
                .then_inc(sem("abs_ready"), 1)

        def softplus(v, e, s, p, q, nth):
            dve.wait_ge(sem("exp_ready"), nth)
            chain(dve.tensor_scalar(s, e, 2.0, None, ALU.add))
            chain(dve.reciprocal(s, s))
            chain(dve.tensor_tensor(s, s, e, ALU.mult))
            chain(dve.tensor_tensor(p, s, s, ALU.mult))
            chain(dve.tensor_scalar(q, p, 1.0 / 17, None, ALU.mult))
            for c in range(15, 1, -2):
                chain(dve.scalar_tensor_tensor(out=q, in0=q, scalar=1.0 / c, in1=p, op0=ALU.add, op1=ALU.mult))
            chain(dve.scalar_tensor_tensor(out=q, in0=q, scalar=1.0, in1=s, op0=ALU.add, op1=ALU.mult))
            chain(dve.tensor_scalar(v, v, 0.0, None, ALU.max))
            chain(dve.scalar_tensor_tensor(out=v, in0=q, scalar=2.0, in1=v, op0=ALU.mult, op1=ALU.add))

        dve.wait_ge(sem("const_ready"), 2)
        dve.tensor_reduce(fold[:], ident[0:NS, 0:NS].rearrange("p (b t) -> p t b", t=NT), AX.X, ALU.add)\
            .then_inc(sem("fold_ready"), 1)
        dve.wait_ge(sem("hist_turned"), 1)
        dve.tensor_copy(histT[:].rearrange("p c h -> p (c h)"), bank[2][:, 0:384])
        dve.tensor_copy(h0T[:].rearrange("p c b -> p (c b)"), bank[2][:, 384:416])
        dve.tensor_copy(masks[:].rearrange("p g (b t) -> p (g b) t", t=NT),
                        bank[2][:, 416:420].unsqueeze(1).to_broadcast([P, 2 * ND, NT])).then_inc(sem("masks_step"), 1)

        def out_add(n, part):
            dve.wait_ge(sem("w_used"), OUT0 + part * KT + n + 1)
            if part:
                dve.wait_ge(sem("x_added"), XO0 + n + 1)
            elif n == 0:
                dve.wait_ge(sem("x_back"), 16)
            dve.tensor_tensor(xT[:, n, :], xT[:, n, :], bank[n % 2][:, 0:N], ALU.add).then_inc(sem("x_added"), 1)

        def mix_vector():
            rms = rs[:, 2, :]

            def take_in(t):
                dve.wait_ge(sem("w_used"), IN0 + t + 1)
                acc = bank[t % 2][:, 0:N]
                if t == 0:
                    dve.wait_ge(sem("tables_ready"), 1)
                    dve.wait_ge(sem("small_loaded"), 16 * 10)
                    dve.tensor_tensor(col[0:72, 1:2], col[0:72, 1:2], col[0:72, 0:1], ALU.mult)
                    chain(dve.tensor_tensor(sc48[0:72, SC, :], acc[0:72, :], rms[0:72, :], ALU.mult))
                    dve.tensor_scalar(sc48[0:72, SC, :], sc48[0:72, SC, :], col[0:72, 0:1], col[0:72, 1:2], ALU.mult, ALU.add)\
                        .then_inc(sem("in_taken"), 1)
                elif t < T_K:
                    dve.scalar_tensor_tensor(out=qT[:, t - T_Q, :], in0=acc, scalar=HD ** -0.5, in1=rms, op0=ALU.mult,
                                             op1=ALU.mult).then_inc(sem("in_taken"), 1)
                elif t < T_X:
                    to = kT[:, t - T_K, :] if t < T_V else attT[:, t - T_V, :]
                    dve.tensor_tensor(to, acc, rms, ALU.mult).then_inc(sem("in_taken"), 1)
                elif t < T_G:
                    c = t - T_X
                    conv(c, t, acc)
                else:
                    to = gT[:, t - T_G, :] if t < T_Z else zT[:, t - T_Z, :]
                    dve.tensor_tensor(to, acc, rms, ALU.mult).then_inc(sem("in_taken"), 1)

            def conv(c, t, acc):
                r = raw[:, c % 2, :]
                if c == 0:
                    dve.wait_ge(sem("suf_stored"), 16 * ND)
                if c >= 2:
                    dve.wait_ge(sem("conv_done"), c - 1)
                dve.tensor_tensor(r[:, HC:HC + NP_], acc[:, 0:NP_], rms[:, 0:NP_], ALU.mult)
                dve.tensor_copy(strided(r, HC + NP_, (HC + NT, ND), (1, HC)), strided(histT[:, c, :], 0, (HC, ND), (1, HC)))
                dve.tensor_tensor(windows(r, 2 * HC + NP_), sampled(acc[:, NP_:N]), sampled(rms[:, NP_:N]), ALU.mult).then_inc(sem("in_taken"), 1)
                dve.wait_ge(sem("in_taken"), t + 1)
                n, r0, rb, to = (XT_, R_CW, R_CB, xsT) if c < XT_ else (LT_, R_LW, R_LB, uT)
                k = c if c < XT_ else c - XT_
                w = [params[:, r0 + j * n + k:r0 + j * n + k + 1] for j in range(CW)]
                if c:
                    dve.wait_ge(sem("conv_done"), c)
                chain(dve.tensor_scalar(ctmp[:], r[:, 0:312], w[0], params[:, rb + k:rb + k + 1], ALU.mult, ALU.add))
                for j in (1, 2):
                    chain(dve.scalar_tensor_tensor(out=ctmp[:], in0=r[:, j:j + 312], scalar=w[j], in1=ctmp[:],
                                                   op0=ALU.mult, op1=ALU.add))
                dve.scalar_tensor_tensor(out=to[:, k, 0:NP_], in0=r[:, HC:HC + NP_], scalar=w[3], in1=ctmp[:, 0:NP_],
                                         op0=ALU.mult, op1=ALU.add)
                dve.scalar_tensor_tensor(out=sampled(to[:, k, NP_:N]), in0=windows(r, 2 * HC + NP_), scalar=w[3],
                                         in1=windows(ctmp[:], HC + NP_), op0=ALU.mult, op1=ALU.add)
                dve.tensor_copy(histO[:, c, 0:HC], r[:, NP_:NP_ + HC])
                dve.tensor_copy(strided(histO[:, c, :], HC, (HC, ND), (1, HC)),
                                strided(r, HC + NP_ + NT, (HC + NT, ND), (1, HC))).then_inc(sem("conv_done"), 1)

            scratch = [ps[0:72, c * N:(c + 1) * N] for c in range(3)] + [bias[0:72, 0:N]]
            def lo_mix(n):
                if n < IN_TILES:
                    lo(IN0, 0, n, KT)
                else:
                    lo(OUT0, 0, n - IN_TILES, 8)

            lo_mix(0)
            add_x(IN0 - 1, (IN0 - 1) % 4, 0, XO0 - KT, KT - 1, 0.5)
            scale_x(1, KT - 1, 1, XO0)
            split_x(1, KT - 2, 0)
            split_x(1, KT - 1, 1)
            for step in STEPS:
                what, i = step[0], step[-1]
                if what == "in":
                    if i == 1:
                        root(1)
                    if i:
                        take_in(i - 1)
                    if i < IN_TILES:
                        lo_mix(i + 1)
                elif what == "suffix":
                    dve.wait_ge(sem("lf_loaded"), 16 * ND * PAGES)
                    by_head = lfp[:].rearrange("p s h -> p h s")
                    dve.tensor_reduce(total[:], by_head, AX.X, ALU.add).then_inc(sem("total_ready"), 1)
                    src = take(dve, "later")
                    dve.tensor_copy(lafter[:], src[0:64, 0:H_ATT]).then_inc(side_read("later"), 1)
                    copied(dve, "later")
                    dve.tensor_copy(sfx[:, :, PAGE:].rearrange("p h o -> p (h o)"), lafter[:])
                    for h in range(H_ATT):
                        m = dve.tensor_tensor_scan(back(sfx[:, h, 0:PAGE]), ones[0:64, :],
                                                   back(lfp[:, :, h]), lafter[:, h:h + 1], ALU.mult, ALU.add)
                    m.then_inc(sem("sfx_ready"), 1)
                elif what == "gates":
                    dve.wait_ge(sem("in_taken"), 1)
                    absolute(scratch[0], sc48[0:72, SC, :])
                    chain(dve.tensor_scalar(lam[:, 0, :], params[:, R_LAM:R_LAM + 4], -1.0, None, ALU.mult))
                    absolute(lam[:, 1, :], lam[:, 0, :])
                    softplus(sc48[0:72, SC, :], *scratch, 1)
                    softplus(lam[:, 0, :], *(lam[:, c, :] for c in range(1, 5)), 2)
                    chain(dve.tensor_scalar(lam[:, 0, :], lam[:, 0, :], LRU_C, None, ALU.mult))
                    dve.tensor_scalar(lam[:, 2, :], lam[:, 0, :], -1.0, None, ALU.mult)
                    dve.wait_ge(sem("coef_ready"), 1)
                    chain(dve.tensor_scalar(scratch[0], sc48[0:72, SC, :], col[0:72, 3:4], -1.0, ALU.mult, ALU.mult))
                    chain(dve.tensor_tensor_scan(sc48[0:72, CS, :], seqmask[0:72, :], scratch[0], 0.0, ALU.mult, ALU.add))
                    cs, wd = sc48[0:72, CS, :], sc48[0:72, WDC, :]
                    dve.tensor_scalar(wd[:, 0:NP_], cs[:, 0:NP_], -1.0, cs[:, NP_ - 1:NP_], ALU.mult, ALU.add)
                    dve.tensor_tensor(sampled(wd[:, NP_:N]), strided(cs, NP_ + NT - 1, (NT, ND), (0, NT)),
                                      sampled(cs[:, NP_:N]), ALU.subtract).then_inc(sem("sums_ready"), 1)
                    dve.tensor_scalar(negc[0:72, :], cs, -1.0, None, ALU.mult).then_inc(sem("negc_ready"), 1)
                elif what == "turn_gates":
                    src = take(dve, "nat")
                    dve.tensor_scalar(lfo[:, 0:2, :], strided(src[:, :], 0, (144, 2), (1, H_ATT)), -1.0, None, ALU.mult)
                    dve.tensor_scalar(lfo[0:NS, 2, :], src[0:NS, 288:288 + H_ATT], -1.0, None, ALU.mult)\
                        .then_inc(sem("nat_ready"), 1)
                    dve.tensor_copy(nat[:, 0:2, :].rearrange("p b c -> p (b c)"), src[:, 0:288])
                    dve.tensor_copy(nat_e[0:NS, :], src[0:NS, 432:480])
                    dve.tensor_copy(nat[0:NS, 2, :], src[0:NS, 288:432]).then_inc(side_read("nat"), 1)
                    src = take(dve, "dec")
                    dve.tensor_copy(dec[:].rearrange("p j b -> p (j b)"), src[:, 0:64]).then_inc(side_read("dec"), 1)
                elif what == "turn_kv":
                    for b in range(3):
                        src = take(dve, "k", b)
                        dve.tensor_copy(kvn[0:rows_of(b), b, 0:512], src[0:rows_of(b), :]).then_inc(side_read("k", b), 1)
                elif what == "prompt":
                    if i < H_ATT:
                        src = take(dve, "sc", i)
                        if i == 0:
                            dve.wait_ge(sem("maskp_step"), 3)
                        if i >= 2:
                            copied(dve, "p", i - 2)
                        at = i % 2 * 384
                        dve.tensor_tensor(ps[:, at:at + 384], src[:, 0:384], maskp[:], ALU.add).then_inc(side_read("sc", i), 1)
                        copied(dve, "sc", i)
                        blks = [(ps[:, at + c:at + c + w], 2 * (i % 2) + b) for b, (c, w) in enumerate(((0, P), (P, NP_)))]
                        for w, n in blks:
                            m = dve.tensor_reduce(nm[:, n:n + 1], w, AX.X, ALU.max, negate=True)
                        m.then_inc(sem("fox_max"), 1)
                        dve.wait_ge(sem("fox_exp"), i + 1)
                        n = 2 * (i % 2)
                        chain(dve.reciprocal(rr[:, n:n + 2], rsum[:, n:n + 2]))
                        for w, n in blks:
                            m = dve.tensor_scalar(w, w, rr[:, n:n + 1], None, ALU.mult)
                        m.then_inc(sem("probs_ready"), 1)
                    if i >= 2:
                        h = i - 2
                        src = take(dve, "pv", h)
                        if h == 0:
                            copied(dve, "v", 2)
                        half = slice(h % 2 * HD, (h % 2 + 1) * HD)
                        dve.tensor_copy(attT[half, h // 2, 0:NP_], src[half, 0:NP_]).then_inc(side_read("pv", h), 1)
                elif what == "keys":
                    g = i // 8
                    if i % 8 == 0:
                        if g == 0:
                            dve.wait_ge(sem("maskp_step"), 3)
                            dve.wait_ge(sem("masks_step"), 5)
                            chain(dve.tensor_scalar(masks[:], masks[:], -1.0, BIG, ALU.add, ALU.mult))
                        else:
                            dve.wait_ge(sem("scores_ready"), g)
                        for e in range(2):
                            half = slice(e * HD, (e + 1) * HD)
                            m = dve.tensor_copy(strided(qblk[half], NT * e, (P, 4), (40, 4), (1, NT)),
                                                strided(qT[half], NP_ + 16 * g, (NT, 4), (N, 4), (1, NT)))
                        m.then_inc(sem("qblk_ready"), 1)
                elif what == "max":
                    dve.wait_ge(sem("scores_ready"), i + 1)
                    dve.wait_ge(sem("bias_loaded"), 64 * (i + 1))
                    if i == 0:
                        copied(dve, "p", H_ATT - 1)
                    for c in range(2):
                        cs = slice(c * 512, (c + 1) * 512)
                        dve.tensor_tensor(ps[:, cs], bank[2 + c][:, :], bias[:, cs], ALU.add)
                    dve.tensor_tensor(ps[:, PAST:PAST + NS], bank[4][:, 0:NS], masks[:, i, :], ALU.add)\
                        .then_inc(sem("scores_read"), 1)
                    dve.wait_ge(sem("scores_read"), i + 1)
                    dve.tensor_reduce(nm[:, 0:1], ps[:, 0:PAST + NS], AX.X, ALU.max, negate=True)\
                        .then_inc(sem("sample_max"), 1)
                    dve.wait_ge(sem("sexp_ready"), i + 1)
                    chain(dve.reciprocal(rr[:, 0:1], rsum[:, 0:1]))
                elif what == "scale":
                    dve.wait_ge(sem("sample_pv"), i + 1)
                    dve.tensor_scalar(att_o, bank[4][:, :], rr[:, 0:1], None, ALU.mult).then_inc(sem("att_o_ready"), 1)
                elif what == "merge_heads":
                    src = take(dve, "heads", i)
                    for e in range(2):
                        half = slice(e * HD, (e + 1) * HD)
                        m = dve.tensor_copy(strided(attT[half], NP_ + 16 * i, (N, 4), (NT, 4), (1, NT)),
                                            strided(src[half, :], NT * e, (P + 2 * NT, 4), (32, 4), (1, NT)))
                    m.then_inc(side_read("heads", i), 1)
                elif what == "lru_decay":
                    copied(dve, "i", 3)
                    copied(dve, "i", 2)
                    dve.tensor_tensor(lru_i[:], lru_i[:], uT[:], ALU.mult).then_inc(sem("lru_step"), 1)
                    dve.wait_ge(sem("lru_decayed"), 1)
                    dve.wait_ge(sem("lru_step"), 1)
                    chain(dve.tensor_tensor(uT[:], lru_a[:], lru_a[:], ALU.mult))
                    dve.scalar_tensor_tensor(out=uT[:], in0=uT[:], scalar=1.0, in1=lru_r[:], op0=ALU.add, op1=ALU.mult)\
                        .then_inc(sem("lru_square"), 1)
                elif what == "lru_scan":
                    dve.wait_ge(sem("lru_root"), 1)
                    chain(dve.tensor_tensor(lru_i[:], lru_i[:], uT[:], ALU.mult))
                    for c in range(4):
                        dve.tensor_tensor_scan(lru_r[:, c, 0:NP_], lru_a[:, c, 0:NP_], lru_i[:, c, 0:NP_], 0.0,
                                               ALU.mult, ALU.add)
                    prev = h0T[:]
                    for t in range(NT):
                        a, b, h = (strided(x[:], NP_ + t, (N, 4), (NT, ND)) for x in (lru_a, lru_i, lru_r))
                        chain(dve.tensor_tensor(h, a, prev, ALU.mult))
                        chain(dve.tensor_tensor(h, h, b, ALU.add))
                        prev = h
                    dve.tensor_copy(lst[:, :, 0:1], lru_r[:, :, NP_ - 1:NP_])
                    dve.tensor_copy(lst[:, :, 1:], prev).then_inc(sem("lst_ready"), 1)
                elif what == "lru_out":
                    src = take(dve, "lru_state")
                    copied(dve, "i", 3)
                    dve.tensor_copy(lrs[0:1 + ND, :], src[0:1 + ND, :]).then_inc(side_read("lru_state"), 1)
                    dve.wait_ge(sem("g_ready"), 1)
                    dve.tensor_tensor(gT[:], gT[:], lru_r[:], ALU.mult).then_inc(sem("lru_done"), 1)
                elif what == "turn_x":
                    n = rows_of(i)
                    for half in range(2):
                        src = take(dve, "x", i, half)
                        dve.tensor_tensor(xsn[0:n, i, half * 512:(half + 1) * 512].rearrange("p (h c) -> p h c", c=HD),
                                          src[0:n, :].rearrange("p (h c) -> p h c", c=HD),
                                          spread(nat[0:n, i, 32 + 8 * half:40 + 8 * half], HD), ALU.mult)\
                            .then_inc(side_read("x", i, half), 1)
                    src = take(dve, "b", i)
                    dve.tensor_copy(bnat[0:rows_of(i), i, :], src[0:rows_of(i), 0:256]).then_inc(side_read("b", i), 1)
                elif what == "scores":
                    dve.tensor_copy(strided(cpad[:], 0, (ND * NS, 2), (NS + NT, ND), (1, NT)),
                                    strided(xsT[:, 10, :], NP_, (N, 2), (NT, ND), (1, NT)))
                    for g in range(2):
                        src = take(dve, "cb", g)
                        dve.tensor_tensor(cbm[:, g, 0:3 * P], src[:, 0:3 * P], tri[:], ALU.mult)
                        dve.tensor_tensor(cbm[0:NS, g, 3 * P:], src[0:NS, 3 * P:SEGW], tris[0:NS, :], ALU.mult)\
                            .then_inc(side_read("cb", g), 1)
                elif what == "merge":
                    dve.wait_ge(sem("m_rounded"), 1)
                    dve.tensor_tensor(xn_lo[:, 0:4, :], attT[:], xn_hi[:, 0:4, :].bitcast(F32), ALU.subtract)\
                        .then_inc(sem("merged"), 4)
                    dve.tensor_tensor(xn_lo[:, 12:16, :], gT[:], xn_hi[:, 12:16, :].bitcast(F32), ALU.subtract)\
                        .then_inc(sem("merged"), 4)
                elif what == "ssd":
                    if i < H_SSD:
                        src = take(dve, "acs", i)
                        if i >= 2:
                            dve.wait_ge(sem("mseg_ready"), i - 1)
                        for cs, kb, q in PAIRS:
                            n = rows_of(kb)
                            m = dve.tensor_scalar(lseg[0:n, i % 2, cs], src[0:n, q], nat[0:n, kb, 48 + 32 + i:48 + 33 + i], 0.0,
                                                  ALU.subtract, ALU.min)
                        m.then_inc(side_read("acs", i), 1)
                    if i >= 3 and i % 2:
                        j = (i - 3) // 2
                        src = take(dve, "y", j)
                        dve.scalar_tensor_tensor(out=xsT[:, j, :], in0=xsT[:, j, :], scalar=dcol[:, j:j + 1],
                                                 in1=src[:, 0:N], op0=ALU.mult, op1=ALU.add).then_inc(side_read("y", j), 1)
                elif what == "out":
                    if i:
                        out_add(i - 1, 0)
                    lo_mix(IN_TILES + i + 1)
                elif what == "decay_x":
                    for b in range(3):
                        n = rows_of(b)
                        xv = xsn[0:n, b, :].rearrange("p (h c) -> p h c", c=HD)
                        m = dve.tensor_tensor(xv, xv, spread(nat[0:n, b, 96 + 32:96 + 48], HD), ALU.mult)
                    m.then_inc(sem("xw_ready"), 1)
                elif what == "unit":
                    if i % 2 == 0 and i < 2 * ND:
                        b = i // 2
                        if b >= 4:
                            take(dve, "up", 2 * (b - 4) + 1)
                        dve.tensor_scalar(bexp[0:NS, b % 4, :], bnat[0:NS, 2, :], bmask[:, b:b + 1], None, ALU.mult)\
                            .then_inc(sem("bexp_ready"), 1)
                    if i:
                        u = i - 1
                        b, g = u // 2, u % 2
                        src = take(dve, "up", u)
                        if u >= 2:
                            dve.wait_ge(sem(f"snew_stored{u % 2}"), 16 * (u // 2))
                        else:
                            dve.wait_ge(sem("state_stored"), 32)
                        for j in range(4):
                            cs = slice(j * P, (j + 1) * P)
                            m = dve.scalar_tensor_tensor(out=snew[:, u % 2, cs], in0=h0[:, u % 4, cs],
                                                         scalar=dec[:, 4 * g + j, b:b + 1], in1=src[:, cs],
                                                         op0=ALU.mult, op1=ALU.add)
                        m.then_inc(side_read("up", u), 1)
                elif what == "carry":
                    dve.wait_ge(sem("h0t_used"), 2 * ND)
                    for g in range(2):
                        dve.tensor_tensor(ys[0:NS, g * 512:(g + 1) * 512].rearrange("p (h c) -> p h c", c=HD),
                                          bank[2 + g][0:NS, :].rearrange("p (h c) -> p h c", c=HD),
                                          spread(nat_e[0:NS, 32 + 8 * g:40 + 8 * g], HD), ALU.mult).then_inc(sem("ys_ready"), 1)
                    src = take(dve, "ys")
                    dve.tensor_tensor(xsT[:, 0:8, NP_:N], xsT[:, 0:8, NP_:N],
                                      src[:, 0:8 * NS].rearrange("p (j t) -> p j t", t=NS), ALU.add)\
                        .then_inc(side_read("ys"), 1)
                    copied(dve, "ys")
                elif what == "gate":
                    dve.wait_ge(sem("z_silu"), 2)
                    dve.tensor_tensor(xsT[:, 0:8, :], xsT[:, 0:8, :], zT[:], ALU.mult).then_inc(sem("gated_y"), 1)
                elif what == "group":
                    src = take(dve, "mean", i)
                    y, z, v = rs[:, 1, :], rs[:, 2, :], rs[:, 0, :]
                    dve.tensor_scalar(v, src[:, 0:N], 1.0 / 512, EPS, ALU.mult, ALU.add).then_inc(side_read("mean", i), 1)
                    dve.wait_ge(sem("groot_step"), 2 * i + 2)
                    chain(dve.tensor_tensor(z, y, y, ALU.mult))
                    chain(dve.tensor_tensor(z, z, v, ALU.mult))
                    chain(dve.tensor_scalar(z, z, -0.5, 1.5, ALU.mult, ALU.add))
                    chain(dve.tensor_tensor(z, z, y, ALU.mult))
                    for j in range(4 * i, 4 * i + 4):
                        m = dve.scalar_tensor_tensor(out=zT[:, j, :], in0=xsT[:, j, :], scalar=params[:, R_NRM + j:R_NRM + j + 1],
                                                     in1=z, op0=ALU.mult, op1=ALU.mult)
                    m.then_inc(sem("yn_done"), 1)
                    dve.wait_ge(sem("m_rounded"), i + 2)
                    dve.tensor_tensor(m_lo[:, 4 * i:4 * i + 4, :], zT[:, 4 * i:4 * i + 4, :],
                                      m_hi[:, 4 * i:4 * i + 4, :].bitcast(F32), ALU.subtract).then_inc(sem("merged"), 4)
            out_add(KT - 1, 0)
            for j in range(1, 4):
                lo(OUT0, 0, KT + j, 8)
                out_add(j - 1, 1)
                scale_x(2, j - 1, (j - 1) % 2, XO0 + KT + j)
                if j >= 2:
                    split_x(2, j - 2, j % 2)
            with dve.Fori(1, KT // 4) as it:
                for j in range(4):
                    lo(OUT0 + KT, it * 4, j, 8)
                    add_x(OUT0 + KT - 1 + j + it * 4, (j - 1) % 2, 0, it * 4 + (XO0 + j), it * 4 + (j - 1), 1.0)
                    scale_x(2, it * 4 + (j - 1), (j - 1) % 2, it * 4 + (XO0 + KT + j))
                    split_x(2, it * 4 + (j - 2), j % 2)
            for q in range(2):
                dve.wait_ge(sem(f"snew_stored{q}"), 16 * ND)

        for f in range(2):
            if f == 0:
                dve.wait_ge(sem("x_kept2"), 4)
                dve.wait_ge(sem("x_kept"), 5)
            else:
                mix_vector()
            for g, n in enumerate(GROUPS):
                base, ff0, xa0 = seg["up", f, g], FF0[f, g], XA0[f, g]
                for m in range(3):
                    i = base + 2 * m
                    lo(base, 0, 2 * m, KT)
                    if m:
                        gate(i - 1, (i - 1) % 4, ff0 + m - 1, (ff0 + m - 1) % 2, m - 1)
                    elif g:
                        add_x(i - 1, (i - 1) % 4, 0, xa0 - KT if xa0 - KT > 0 else None, KT - 1, 0.5)
                    elif f:
                        out_add(KT - 1, 1)
                        scale_x(2, KT - 1, 1, xa0)
                        split_x(2, KT - 2, 0)
                        split_x(2, KT - 1, 1)
                    else:
                        for k in range(KT + 1):
                            if k < KT:
                                scale_x(0, k, k % 2)
                            if k:
                                split_x(0, k - 1, (k - 1) % 2)
                    lo(base, 0, 2 * m + 1, KT)
                    if m == 0 and g == 0:
                        root(FN[f])
                    pre(i, i % 4, ff0 + m, (ff0 + m) % 2)
                with dve.Fori(0, (n - 3) // 2) as it:
                    for m in range(2):
                        lo(base + 6, it * 4, 2 * m, KT)
                        gate(base + 5 + 2 * m + it * 4, (base + 5 + 2 * m) % 4, it * 2 + (ff0 + 2 + m), (ff0 + m) % 2,
                             it * 2 + (2 + m))
                        lo(base + 6, it * 4, 2 * m + 1, KT)
                        pre(base + 6 + 2 * m + it * 4, (base + 6 + 2 * m) % 4, it * 2 + (ff0 + 3 + m), (ff0 + 3 + m) % 2)
                base = seg["down", f, g]
                for j in range(4):
                    lo(base, 0, j, n)
                    if j == 0:
                        gate(base - 1, (base - 1) % 4, ff0 + n - 1, (ff0 + n - 1) % 2, n - 1)
                    else:
                        add_x(base + j - 1, (base + j - 1) % 4, 0, xa0 - KT + j if g or f else None, j - 1, 0.5)
                        if g == 2:
                            scale_x(FN[f] + 1, j - 1, (j - 1) % 2, xa0 + j)
                            if j >= 2:
                                split_x(FN[f] + 1, j - 2, j % 2)
                with dve.Fori(1, KT // 4) as it:
                    for j in range(4):
                        lo(base, it * 4, j, n)
                        add_x(base + j - 1 + it * 4, (base + j - 1) % 4, 0,
                              it * 4 + (xa0 - KT + j) if g or f else None, it * 4 + (j - 1), 0.5)
                        if g == 2:
                            scale_x(FN[f] + 1, it * 4 + (j - 1), (j - 1) % 2, it * 4 + (xa0 + j))
                            split_x(FN[f] + 1, it * 4 + (j - 2), j % 2)
        add_x(base + KT - 1, (base + KT - 1) % 4, 0, xa0, KT - 1, 0.5)
        scale_x(3, KT - 1, 1, xa0 + KT)
        root(3, 3)
        for kg in range(4):
            for b in range(3):
                t = 3 * kg + b
                if t % 2 == 0:
                    rows = P if b < 2 else NS
                    dve.wait_ge(sem("y_turned"), t + 1)
                    dve.tensor_scalar(ynat[0:rows, b, kg * 512:(kg + 1) * 512], bank[t % 7][0:rows, :],
                                      rs[0:rows, 2, b:b + 1], None, ALU.mult)\
                        .then_inc(sem("y_ready"), 1)


_OUTS = {
    "y_prompt": (1, NP_, D), "y_sample": (ND, NT, D),
    "k_prompt": (1, 1, NP_, H_ATT, HD), "v_prompt": (1, 1, NP_, H_ATT, HD), "logf_prompt": (1, 1, NP_, H_ATT),
    "k_sample": (1, ND, NT, H_ATT, HD), "v_sample": (1, ND, NT, H_ATT, HD), "logf_sample": (1, ND, NT, H_ATT),
    "ssd_state_prompt": (1, 1, H_SSD, HD, ST), "ssd_conv_prompt": (1, 1, HC, XBC),
    "ssd_state_sample": (1, ND, H_SSD, HD, ST), "ssd_conv_sample": (1, ND, HC, XBC),
    "lru_state_prompt": (1, 1, DLRU), "lru_conv_prompt": (1, 1, HC, DLRU),
    "lru_state_sample": (1, ND, DLRU), "lru_conv_sample": (1, ND, HC, DLRU),
}
_INS = ["x_prompt", "x_sample", "cache_k", "cache_v", "cache_logf", "page_table", "state_ssd", "state_ssd_conv",
        "state_lru", "state_lru_conv", "ffn1_norm", "ffn1_w_gate", "ffn1_w_up", "ffn1_w_down", "mix_norm", "w_in",
        "fox_b_f", "ssd_conv_w", "ssd_conv_b", "ssd_dt_bias", "ssd_a_log", "ssd_d", "ssd_norm", "lru_conv_w",
        "lru_conv_b", "lru_w_a", "lru_b_a", "lru_w_x", "lru_b_x", "lru_lambda", "w_out", "ffn2_norm",
        "ffn2_w_gate", "ffn2_w_up", "ffn2_w_down", "final_norm"]


def kernel(**inputs):
    import concourse.bacc as _bacc
    from concourse.bass_utils import run_bass_kernel_spmd as _run
    nc = _bacc.Bacc("TRN2", target_bir_lowering=False, num_devices=1, dynamic_dma_scratch_size=4096)
    arrays = {k: np.ascontiguousarray(inputs[k]) for k in _INS}
    I = {k: nc.dram_tensor(k, a.shape, mybir.dt.from_np(a.dtype), kind="ExternalInput").ap() for k, a in arrays.items()}
    O = {k: nc.dram_tensor("out_" + k, shape, F32, kind="ExternalOutput").ap() for k, shape in _OUTS.items()}
    build(nc, I, O)
    r = _run(nc, [arrays], core_ids=[0])
    return tuple(r.results[0]["out_" + k] for k in _OUTS)
```

```python
from contextlib import ExitStack

import numpy as np

import concourse.bass as bass
from concourse import mybir

F32 = mybir.dt.float32
F32R = mybir.dt.float32r
I32 = mybir.dt.int32
ACT = mybir.ActivationFunctionType
ALU = mybir.AluOpType
AX = mybir.AxisListType

P = 128
D = 2048
KT = D // P
NP_, ND, NT = 256, 8, 4
NS = ND * NT
N = NP_ + NS
DFF = 5504
FT = DFF // P
GROUPS = (15, 15, 13)
HG = max(GROUPS)
EPS = 1e-6
H_ATT, H_SSD, HD, ST = 8, 16, 64, 128
PAGE, PAGES = 128, 8
PAST = PAGE * PAGES
POOLP = 80
VRING = 4
SEGW = 3 * P + NS
CW = 4
HC = CW - 1
XBC, DSSD, DLRU = 1536, 1024, 512
XT_, LT_ = XBC // P, DLRU // P
LRU_C = 8.0
O_Q, O_K, O_V, O_F, O_Z = 0, 512, 1024, 1536, 1544
O_XBC, O_DT, O_G, O_U = 2568, 4104, 4120, 4632
BIG = 1.0e30
MIX = 1
IN_TILES, OUT_TILES = 41, 32
LOADS = 4
R_CW, R_CB, R_LW, R_LB, R_BA, R_BX, R_LAM, R_NRM = 0, 48, 60, 76, 80, 84, 88, 92
NPAR = 100


AT = {}


class Plan:

    def __init__(self, nc, at, end):
        self.nc, self.at, self.end = nc, at, end

    def __call__(self, name, shape, dtype=F32):
        size = 4 * int(np.prod(shape[1:]))
        t = self.nc.alloc_sbuf_tensor_at(name, list(shape), dtype, offset=self.at)
        AT[name] = self.at
        self.at += -(-size // 32) * 32
        assert self.at <= self.end, (name, self.at, self.end)
        return t


def build(nc, I, O):
    ctx = ExitStack()
    sems = {}

    def sem(name):
        if name not in sems:
            sems[name] = ctx.enter_context(nc.semaphore(name))
        return sems[name]

    SB0, SB1 = 4224, 229344
    fixed = Plan(nc, SB0, SB1)
    wraw = fixed("wraw", [P, LOADS, KT * P])
    whi = fixed("whi", [P, 2, KT * P], F32R)
    wlo = fixed("wlo", [P, 2, KT * P], F32R)
    xn_hi = fixed("xn_hi", [P, KT, N], F32R)
    xn_lo = fixed("xn_lo", [P, KT, N], F32R)
    ident = fixed("ident", [P, P])
    ones = fixed("ones", [P, P])
    gains = fixed("gains", [P, 4, KT])
    params = fixed("params", [P, NPAR])
    xf = fixed("xf", [P, 3, N])
    sq = fixed("sq", [P, 2, N])
    ssum = fixed("ssum", [P, N])
    rs = fixed("rs", [P, 3, N])
    XAT = fixed.at
    xT = fixed("xT", [P, KT, N])
    ARENA = fixed.at

    ffn = Plan(nc, ARENA, SB1)
    h_hi = ffn("h_hi", [P, HG, N], F32R)
    h_lo = ffn("h_lo", [P, HG, N], F32R)
    sg = ffn("sg", [P, 2, N])
    hm = ffn("hm", [P, 2, N])
    fin = Plan(nc, ARENA, SB1)

    mix = Plan(nc, XAT, SB1)
    kpage = mix("kpage", [P, 4, 512])
    qblk = mix("qblk", [P, 4, 4, 32])
    vpage = mix("vpage", [P, VRING, 512])
    kts = mix("kts", [P, 2, 512])
    bias = mix("bias", [P, PAST])
    assert mix.at == AT["vpage"] + 2 * VRING * 2048
    vpages = Plan(nc, AT["vpage"], mix.at)("vpages", [P, 2 * VRING, 512])
    ps = mix("ps", [P, PAST + NS])
    att_o = ps[:, 0:512]
    pts = mix("pts", [P, PAST + P])
    qT = mix("qT", [P, 4, N])
    kT = mix("kT", [P, 4, N])
    kvn = mix("kvn", [P, 3, 1024])
    maskp = mix("maskp", [P, 384])
    masks = mix("masks", [P, 2, NS])
    A1 = mix.at
    pid = mix("pid", [1, ND * PAGES], I32)
    bmask = mix("bmask", [NS, ND])
    lfo = mix("lfo", [P, 3, H_ATT])
    head_rows = mix("head_rows", [H_ATT, NS])
    fold = mix("fold", [NS, NT])
    total = mix("total", [64, H_ATT])
    lafter = mix("lafter", [64, H_ATT])
    sc48 = mix("sc48", [P, 3, N])
    nat = mix("nat", [P, 3, 144])
    nat_e = mix("nat_e", [P, 48])
    negc = mix("negc", [P, N])
    seqmask = mix("seqmask", [P, N])
    col = mix("col", [P, 8])
    eend = mix("eend", [P, ND])
    e48 = mix("e48", [P, NS])
    dec = mix("dec", [P, 8, ND])
    histT = mix("histT", [P, 16, HC * ND])
    histO = mix("histO", [P, 16, HC + HC * ND])
    h0T = mix("h0T", [P, 4, ND])
    lam = mix("lam", [P, 8, 4])
    dcol = mix("dcol", [P, 8])
    raw = mix("raw", [P, 2, 315])
    ctmp = mix("ctmp", [P, 312])
    nm = mix("nm", [P, 4])
    rsum = mix("rsum", [P, 4])
    rr = mix("rr", [P, 4])
    lwa = mix("lwa", [P, 4, P])
    lwx = mix("lwx", [P, 4, P])
    cpad = mix("cpad", [P, 2, ND, NS])
    tri = mix("tri", [P, 384])
    tris = mix("tris", [P, NS])
    LATE = mix.at
    xsT = mix("xsT", [P, 12, N])
    attT = mix("attT", [P, 4, N])
    uT = mix("uT", [P, 4, N])
    gT = mix("gT", [P, 4, N])
    pro = Plan(nc, LATE, SB1)
    xnat = pro("xnat", [P, 3, D])
    gnat = pro("gnat", [64, P])
    pnat = pro("pnat", [NPAR, P])
    early = Plan(nc, LATE, SB1)
    lfp = early("lfp", [64, PAGE, H_ATT])
    sfx = early("sfx", [64, H_ATT, PAGE + 1])
    later = early("later", [64, 64])
    hin = Plan(nc, AT["attT"], AT["gnat"])
    histn = hin("histn", [HC * ND, 16 * P])
    h0n = hin("h0n", [ND, DLRU])
    ep = Plan(nc, XAT, A1)
    lru_r = ep("lru_r", [P, 4, N])
    lru_i = ep("lru_i", [P, 4, N])
    assert ep.at <= AT["vpage"]
    ep = Plan(nc, ARENA, A1)
    xsn = ep("xsn", [P, 3, DSSD])
    bnat = ep("bnat", [P, 3, 256])
    cbm = ep("cbm", [P, 2, SEGW])
    zT = ep("zT", [P, 8, N])
    lst = ep("lst", [P, 4, 9])
    lseg = ep("lseg", [P, 2, SEGW])
    mseg = ep("mseg", [P, 2, SEGW])
    sst = ep("sst", [P, 2, 512])
    hout = Plan(nc, AT["vpage"], ARENA)("hout", [P, 2, 512])
    bexp = Plan(nc, AT["lseg"], A1)("bexp", [P, 4, 256])
    snew = Plan(nc, AT["sst"], A1)("snew", [P, 2, 512])
    def over(other, name, shape):
        return Plan(nc, AT[other], SB1)(name, shape)

    h0 = Plan(nc, AT["xn_lo"] + 4 * 4 * N, AT["ident"])("h0", [P, 4, 512])
    grs = over("lwa", "grs", [P, 3, 2, N])
    m_hi = Plan(nc, AT["lseg"], A1)("m_hi", [P, 8, N], F32R)
    m_lo = Plan(nc, AT["attT"], AT["gT"])("m_lo", [P, 8, N], F32R)
    h0t = over("gT", "h0t", [P, 2, 512])
    ys = over("uT", "ys", [P, 1024])
    lrs = over("lwa", "lrs", [P, 512])
    gsq = over("xsn", "gsq", [P, 2, NS])
    fin.at += 4 * KT * N
    yT = Plan(nc, AT["xn_hi"], AT["xn_lo"])("yT", [P, KT, N])
    ynat = fin("ynat", [P, 3, D])

    bank = [ctx.enter_context(nc.psum_tensor(f"bank{i}", [P, 512], F32)) for i in range(8)]
    STAT = 7

    seg, at = {}, 0
    for f in range(2):
        for g, n in enumerate(GROUPS):
            for what, m in (("up", 2 * n), ("down", KT)):
                seg[what, f, g] = at
                at += m
        if f == 0 and MIX:
            seg["in"], seg["out"] = at, at + IN_TILES
            at += IN_TILES + OUT_TILES
    FF0 = {(f, g): f * FT + sum(GROUPS[:g]) for f in range(2) for g in range(3)}
    XA0 = {(f, g): (f * 3 + g) * KT + f * MIX * OUT_TILES for f in range(2) for g in range(3)}
    XO0 = 3 * KT
    NORM = {"ffn1": (0, 0, 0), "mix": (1, XO0, 1), "ffn2": (1 + MIX, XA0[1, 0], 2), "final": (2 + MIX, XA0[1, 2] + KT, 3)}
    FN = [NORM["ffn1"][0], NORM["ffn2"][0]]

    def cols(w, k0, nk, c0, width=P):
        rows = w.rearrange("(k p) c -> p k c", p=P)
        return rows[:, k0:k0 + nk, bass.ds(c0, width)]

    def tile_ap(buf, slot, nk):
        return buf[:, slot, 0:nk * P]

    WG = [I["ffn1_w_gate"][0], I["ffn2_w_gate"][0]]
    WU = [I["ffn1_w_up"][0], I["ffn2_w_up"][0]]
    WD = [I["ffn1_w_down"][0], I["ffn2_w_down"][0]]

    IN0, OUT0 = seg["in"], seg["out"]
    T_Q, T_K, T_V, T_X, T_U, T_G, T_Z = 1, 5, 9, 13, 25, 29, 33
    IN_COL = [O_F] + [o + P * j for o, c in ((O_Q, 4), (O_K, 4), (O_V, 4), (O_XBC, 12), (O_U, 4), (O_G, 4), (O_Z, 8))
                      for j in range(c)]
    x_save = nc.dram_tensor("x_save", [P, KT, N], F32, kind="Internal").ap()
    suf_d = nc.dram_tensor("suf_d", [ND, H_ATT, PAST], F32, kind="Internal").ap()
    SC, CS, WDC = 0, 1, 2
    SR = slice(32, 48)

    def sampled(ap):
        return ap.rearrange("p (b t) -> p b t", t=NT)

    def strided(ap, at, *dims):
        return bass.AP(ap.tensor, ap.offset + at, [list(ap.ap[0])] + [list(d) for d in dims])

    def windows(ap, at):
        return strided(ap, at, (HC + NT, ND), (1, NT))

    STEPS = [("in", 0), ("in", 1), ("in", 2), ("gates", 0), ("in", 3), ("gates", 1), ("in", 4), ("gates", 2), ("in", 5)]
    STEPS += [("turn_gates",), ("in", 6), ("lam",), ("in", 7), ("suffix",)]
    STEPS += [("in", t) for t in range(8, T_X + 1)] + [("turn_kv",)]
    tiles = iter(range(T_X + 1, IN_TILES))

    def tile():
        return [("in", next(tiles))]

    for n in range(H_ATT + 2):
        STEPS += [("prompt", n)] + [("keys", n)] * (n < PAGES) + [("keys_end", 0)] * (n == PAGES) + [("max", 0)] * (n > PAGES) + tile()
    STEPS += [("probs", 0)]
    for n in range(PAGES):
        STEPS += [("values", n)] + [("scale", 0)] * (n == PAGES - 1) + [("keys", PAGES + n)] + tile()
    STEPS += [("merge_heads", 0), ("keys_end", 1)] + tile() + [("max", 1)] + tile() + [("probs", 1)]
    for what, pages in (("lru_gates", (8, 9)), ("lru_decay", (10,)), ("lru_scan", (11, 12)), ("lru_out", (13,))):
        STEPS += [(what,)] + [("values", n) for n in pages] + tile()
    STEPS += [("values", 14), ("values", 15), ("scale", 1)] + tile() + [("merge_heads", 1)]
    heads = iter(range(H_SSD + 2))

    def ssd(n):
        return [("ssd", next(heads)) for _ in range(n)]

    STEPS += [("turn_x", b) for b in range(3)] + [("scores",), ("hist", 0), ("hist", 1)] + tile()
    STEPS += [("hist", 2), ("hist", 3)] + ssd(2) + tile()
    STEPS += ssd(2) + [("in", IN_TILES), ("merge", 0)]
    outs = iter(range(KT))
    for n, h in enumerate(heads):
        STEPS += [("ssd", h)] + ([("out", next(outs))] if n % 2 == 0 else [])
    STEPS += [("decay_x",), ("out", next(outs)), ("state", 0), ("state", 1)]
    for u in range(2 * ND + 1):
        STEPS += [("unit", u)] + ([("out", next(outs))] if u in (2, 6, 10) else [])
        STEPS += [("gate_prompt", u // 2) if u % 2 == 0 else ("sum_prompt", u // 2)] * (u < 2 * ND)
    rest = [("out", n) for n in outs]
    STEPS += [("carry",)] + rest[0:1]
    for n in range(4):
        STEPS += [("groups", n)] + rest[1 + n:2 + n if n < 3 else None]

    JOB = {}
    for step in STEPS:
        what, i = step[0], step[-1]
        names = {"suffix": [("later",)], "turn_gates": [("nat",), ("dec",)],
                 "turn_kv": [(x, b) for b in range(3) for x in "kv"],
                 "keys": [("kt", u) for u in range(4 * i, 4 * i + 4)] if what == "keys" else [],
                 "probs": [("pt", i, q) for q in range(3)], "merge_heads": [("heads", i)],
                 "lru_gates": [(x, c) for c in range(4) for x in ("r", "i")],
                 "hist": [("hist", i)], "lru_out": [("lru_state",)],
                 "turn_x": [("x", i, 0), ("x", i, 1), ("b", i)], "scores": [("cb", 0), ("cb", 1)],
                 "state": [("state", i)], "carry": [("ys",)], "groups": [("mean",)] if i == 0 else []}.get(what, [])
        if what == "prompt":
            names = [("sc", i)] * (i < H_ATT) + [("p", i - 1)] * (1 <= i <= H_ATT) \
                + [("pv", i - 2)] * (i >= 2)
        if what == "ssd":
            names = [("acs", i)] * (i < H_SSD) + [("y", (i - 2) // 2)] * (i >= 2 and i % 2 == 0)
        if what == "unit":
            names = ([("ht", i)] if i < 2 * ND else []) + ([("up", i - 1)] if i else [])
        for name in names:
            JOB[name] = len(JOB)

    def page_of(u):
        return (u // 32 * 4 + u % 4) * PAGES + u % 32 // 4

    def key_slot(r):
        return kts[:, r, :] if r < 2 else kvn[:, r - 2, 0:512]

    def value_slot(u):
        w = u - 32
        if w < 0:
            return u % VRING, u // VRING + 1
        slot = w % (2 * VRING)
        return slot, w // (2 * VRING) + 1 + (32 // VRING if slot < VRING else 0)

    def in_bank(t):
        return bank[t % 2 if t else 4]

    def side(*name):
        return bank[5 + JOB[name] % 3]

    def claim(pe, *name):
        j = JOB[name]
        if j >= 3:
            pe.wait_ge(sem(f"side_read{j % 3}"), j // 3)
        return side(*name)

    def side_done(*name):
        return sem(f"side_done{JOB[name] % 3}")

    def side_read(*name):
        return sem(f"side_read{JOB[name] % 3}")

    def take(eng, *name):
        eng.wait_ge(side_done(*name), JOB[name] // 3 + 1)
        return side(*name)

    def copied(eng, *name):
        eng.wait_ge(side_read(*name), JOB[name] // 3 + 1)

    def h0_of(name, u):
        t = I[name] if name in I else O[name]
        return t[0, u // 2, 8 * (u % 2):8 * (u % 2) + 8].rearrange("(j e) p n -> (e p) j n", e=2)

    def spread(ap, n):
        return ap.unsqueeze(2).to_broadcast([ap.shape[0], ap.shape[1], n])

    def back(ap):
        step, n = ap.ap[-1]
        return bass.AP(ap.tensor, ap.offset + step * (n - 1), [list(d) for d in ap.ap[:-1]] + [[-step, n]])

    def rows_of(blk):
        return P if blk < 2 else NS

    def toks(blk):
        return slice(blk * P, blk * P + rows_of(blk))

    PAIRS = ((slice(0, NP_), 0, slice(0, NP_)), (slice(NP_, 3 * P), 1, slice(P, NP_)),
             (slice(3 * P, SEGW), 2, slice(NP_, N)))

    block = ctx.enter_context(nc.Block())

    @block.sync
    def _(sp):
        for r in range(2):
            sp.dma_start(xnat[:, r, :], I["x_prompt"][0, r * P:(r + 1) * P, :]).then_inc(sem(f"x_loaded{r}"), 16)
        sp.dma_start(xnat[0:NS, 2, :], I["x_sample"].rearrange("b t d -> (b t) d")).then_inc(sem("x_loaded2"), 16)
        def load(base, it4, j, src, nk):
            i = base + j + it4
            if not isinstance(i, int) or i >= LOADS:
                sp.wait_ge(sem("lo_done"), i - LOADS + 1)
            slot = (base + j) % LOADS
            sp.dma_start(tile_ap(wraw, slot, nk).rearrange("p (k c) -> p k c", k=nk), src)\
                .then_inc(sem(f"raw_ready{slot}"), 16)

        for f in range(2):
            for g, n in enumerate(GROUPS):
                f0 = sum(GROUPS[:g])
                base = seg["up", f, g]
                for m in range(3):
                    for j, w in enumerate((WG, WU)):
                        load(base + 2 * m, 0, j, cols(w[f], 0, KT, (f0 + m) * P), KT)
                with sp.Fori(0, (n - 3) // 2) as it:
                    for m in range(2):
                        for j, w in enumerate((WG, WU)):
                            load(base + 6, it * 4, 2 * m + j, cols(w[f], 0, KT, it * (2 * P) + (f0 + 3 + m) * P), KT)
                base = seg["down", f, g]
                for j in range(4):
                    load(base, 0, j, cols(WD[f], f0, n, j * P), n)
                with sp.Fori(1, KT // 4) as it:
                    for j in range(4):
                        load(base, it * 4, j, cols(WD[f], f0, n, it * (4 * P) + j * P), n)

            if f == 0 and MIX:
                sp.wait_ge(sem("lo_done"), IN0 - LOADS + 1)
                win = I["w_in"][0]
                slot = IN0 % LOADS
                to = tile_ap(wraw, slot, KT).rearrange("p (k c) -> p k c", k=KT)
                sp.dma_start(to[:, :, 0:H_ATT], cols(win, 0, KT, O_F, H_ATT)).then_inc(sem("w_small"), 16)
                sp.dma_start(to[:, :, 64:72], cols(win, 0, KT, O_F, H_ATT)).then_inc(sem("w_small"), 16)
                sp.dma_start(to[:, :, 32:48], cols(win, 0, KT, O_DT, H_SSD)).then_inc(sem(f"raw_ready{slot}"), 16)
                wo = I["w_out"][0].rearrange("(a k p) c -> p a k c", a=4, p=P)

                def load_out(part, it4, j):
                    slot = (OUT0 + j) % LOADS
                    sp.wait_ge(sem("lo_done"), it4 + (OUT0 + part * KT + j - LOADS + 1))
                    for a, q in enumerate(((0, 3), (1, 2))[part]):
                        sp.dma_start(wraw[:, slot, a * 512:(a + 1) * 512].rearrange("p (k c) -> p k c", k=4),
                                     wo[:, q, :, bass.ds(it4 * P + j * P, P)])\
                            .then_inc(sem(f"wo_half{slot}" if a else f"raw_ready{slot}"), 16)

                def load_mix(n):
                    if n < IN_TILES:
                        load(IN0, 0, n, cols(win, 0, KT, IN_COL[n], P), KT)
                    else:
                        n -= IN_TILES
                        load_out(n // KT, 0, n % KT)

                def load_page(buf, slot, name, u):
                    at = page_of(u)
                    page = sp.value_load(pid[0:1, at:at + 1], min_val=0, max_val=POOLP - 1)
                    sp.dma_start(buf[:, slot, :],
                                 I[name][0].rearrange("n s h d -> (n s) (h d)")[bass.ds(page * PAGE, PAGE), :])\
                        .then_inc(sem(f"{name}_loaded{slot}"), 16)

                def value_page_free(u):
                    w = u - 32
                    if 4 <= w < 8:
                        sp.wait_ge(sem("scores_read"), 2)
                    elif w >= 8:
                        sp.wait_ge(sem("vpage_used"), u - 2 * VRING + 1)
                    elif u >= VRING:
                        sp.wait_ge(sem("vpage_used"), u - VRING + 1)

                def load_h0(u):
                    sp.dma_start(h0[:, u % 4, :].rearrange("q (j n) -> q j n", j=4), h0_of("state_ssd", u))\
                        .then_inc(sem(f"h0_loaded{u % 4}"), 16)

                AHEAD = LOADS - 1
                for n in range(1, AHEAD):
                    load_mix(n)
                sp.wait_ge(sem("pid_loaded"), 16)
                for step in STEPS:
                    what, i = step[0], step[-1]
                    if what == "in" and i < IN_TILES:
                        load_mix(i + AHEAD)
                    elif what == "out":
                        load_mix(IN_TILES + i + AHEAD)
                    elif what == "keys":
                        if i == 0:
                            sp.wait_ge(sem("x_saved"), 16)
                            sp.wait_ge(sem("xf_ready"), 2 * KT)
                        for u in range(4 * i, 4 * i + 4):
                            if u >= 4:
                                take(sp, "kt", u - 4)
                            load_page(kpage, u % 4, "cache_k", u)
                    elif what == "values":
                        for u in range(4 * i, 4 * i + 4):
                            value_page_free(u)
                            load_page(vpages, value_slot(u)[0], "cache_v", u)
                    elif what == "hist":
                        copied(sp, "hist", i)
                        so, po = ("ssd_conv_sample", "ssd_conv_prompt") if i < 3 else ("lru_conv_sample", "lru_conv_prompt")
                        c = slice(i * 512, (i + 1) * 512) if i < 3 else slice(0, 512)
                        sp.dma_start(O[po][0, 0, :, c], hout[0:HC, i % 2, :]).then_inc(sem(f"hist_stored{i % 2}"), 16)
                        sp.dma_start(O[so][0].rearrange("b w c -> (b w) c")[:, c], hout[HC:HC + HC * ND, i % 2, :])\
                            .then_inc(sem(f"hist_stored{i % 2}"), 16)
                        if i == 3:
                            for q in range(2):
                                sp.wait_ge(sem(f"hist_stored{q}"), 64)
                            sp.wait_ge(sem("lru_done"), 1)
                            sp.dma_start(xT[:], x_save).then_inc(sem("x_back"), 16)
                    elif what == "merge":
                        sp.wait_ge(sem("merged"), 8)
                        for u in range(4):
                            load_h0(u)
                    elif what == "unit" and i:
                        u = i - 1
                        copied(sp, "up", u)
                        sp.dma_start(h0_of("ssd_state_sample", u), snew[:, u % 2, :].rearrange("q (j n) -> q j n", j=4))\
                            .then_inc(sem(f"snew_stored{u % 2}"), 16)
                        if u + 4 < 2 * ND:
                            load_h0(u + 4)
                load_mix(IN_TILES + KT + AHEAD)
                with sp.Fori(1, KT // 4) as it:
                    for j in range(4):
                        load_out(1, it * 4, j)

        sp.wait_ge(sem("y_ready"), 6)
        sp.wait_ge(sem("y_ready2"), 6)
        for r in range(2):
            sp.dma_start(O["y_prompt"][0, r * P:(r + 1) * P, :], ynat[:, r, :]).then_inc(sem("stored"), 16)
        sp.dma_start(O["y_sample"].rearrange("b t d -> (b t) d"), ynat[0:NS, 2, :]).then_inc(sem("stored"), 16)
        sp.wait_ge(sem("stored"), 48)
        sp.wait_ge(sem("kv_stored"), 16 * 7)
        for q in range(2):
            sp.wait_ge(sem(f"hist_stored{q}"), 64)
            sp.wait_ge(sem(f"snew_stored{q}"), 16 * ND)
        sp.wait_ge(sem("lru_stored"), 16 * 2)
        sp.wait_ge(sem("state_stored"), 16 * 2)

    @block.gpsimd
    def _(pool):
        pool.memset(ident[:], 0.0).then_inc(sem("ident_zero"), 1)
        pool.memset(ones[:], 1.0).then_inc(sem("const_ready"), 1)
        pool.wait_ge(sem("ident_zero"), 1)
        pool.affine_select(out=ident[:], in_=ident[:], compare_op=ALU.not_equal, fill=1.0, base=0,
                           pattern=[[-1, P]], channel_multiplier=1).then_inc(sem("const_ready"), 1)

        pool.memset(tri[:], 1.0).then_inc(sem("pool_fill"), 1)
        pool.memset(tris[0:NS, :], 1.0).then_inc(sem("pool_fill"), 1)
        pool.memset(bmask[:], 1.0).then_inc(sem("pool_fill"), 1)
        pool.memset(seqmask[:], 1.0).then_inc(sem("pool_fill"), 1)
        pool.memset(head_rows[:], 1.0).then_inc(sem("pool_fill"), 1)
        pool.memset(cpad[:], 0.0)
        pool.memset(raw[:], 0.0)
        pool.memset(lwa[:], 0.0)
        pool.memset(lwx[:], 0.0)
        pool.memset(col[:], 0.0).then_inc(sem("pool_fill"), 1)
        pool.wait_ge(sem("pool_fill"), 6)
        for c in (0, 2):
            pool.affine_select(out=tri[:, c * P:(c + 1) * P], in_=tri[:, c * P:(c + 1) * P], compare_op=ALU.is_ge, fill=0.0,
                               base=0, pattern=[[1, P]], channel_multiplier=-1)
        bt = sampled(tris[0:NS, :])
        pool.affine_select(out=bt, in_=bt, compare_op=ALU.is_ge, fill=0.0, base=0, pattern=[[-NT, ND], [0, NT]],
                           channel_multiplier=1).then_inc(sem("pool_fill"), 1)
        pool.affine_select(out=bmask[:], in_=bmask[:], compare_op=ALU.is_ge, fill=0.0, base=0, pattern=[[-NT, ND]],
                           channel_multiplier=1).then_inc(sem("pool_fill"), 1)
        pool.affine_select(out=head_rows[:], in_=head_rows[:], compare_op=ALU.is_ge, fill=0.0, base=0, pattern=[[1, NS]],
                           channel_multiplier=-NT).then_inc(sem("pool_fill"), 1)
        pool.wait_ge(sem("pool_fill"), 9)
        pool.affine_select(out=head_rows[:], in_=head_rows[:], compare_op=ALU.is_ge, fill=0.0, base=NT - 1,
                           pattern=[[-1, NS]], channel_multiplier=NT)
        pool.affine_select(out=bt, in_=bt, compare_op=ALU.is_ge, fill=0.0, base=0, pattern=[[NT, ND], [1, NT]],
                           channel_multiplier=-1)
        pool.affine_select(out=bmask[:], in_=bmask[:], compare_op=ALU.is_ge, fill=0.0, base=NT - 1,
                           pattern=[[NT, ND]], channel_multiplier=-1)
        pool.memset(seqmask[:, 0:1], 0.0)
        pool.memset(strided(seqmask[:], NP_, (NT, ND)), 0.0)
        pool.memset(col[0:72, 0:1], -1.0).then_inc(sem("pool_fill"), 1)
        pool.wait_ge(sem("pool_fill"), 10)
        pool.memset(col[SR, 0:1], 1.0).then_inc(sem("tables_ready"), 1)
        pool.wait_ge(sem("tables_ready"), 1)
        pool.dma_start(pid[:], I["page_table"].rearrange("b g -> (b g)").unsqueeze(0)).then_inc(sem("pid_loaded"), 16)
        for r0 in (0, 64):
            pool.dma_start(col[r0:r0 + H_ATT, 1:2], I["fox_b_f"][0].unsqueeze(1)).then_inc(sem("small_loaded"), 16)
        pool.dma_start(col[SR, 1:2], I["ssd_dt_bias"][0].unsqueeze(1)).then_inc(sem("small_loaded"), 16)
        pool.dma_start(col[SR, 2:3], I["ssd_a_log"][0].unsqueeze(1)).then_inc(sem("small_loaded"), 16)
        d = I["ssd_d"]
        for e in range(2):
            half = slice(e * HD, (e + 1) * HD)
            pool.dma_start(dcol[half, :].unsqueeze(2), bass.AP(d.tensor, d.offset + e, [[0, HD], [2, H_SSD // 2], [1, 1]]),
                           allow_slow_non_contiguous=True)\
                .then_inc(sem("small_loaded"), 16)
            for w, name in ((lwa, "lru_w_a"), (lwx, "lru_w_x")):
                pool.dma_start(w[half, :, half], I[name][0].rearrange("(c e) i j -> e i c j", e=2)[e])\
                    .then_inc(sem("small_loaded"), 16)

        def sum_square(n, k):
            pool.wait_ge(sem("squared"), n * KT + k + 1)
            if isinstance(k, int) and k == 0:
                if n:
                    pool.wait_ge(sem("stat_ready"), n)
                pool.tensor_copy(ssum[:], sq[:, 0, :]).then_inc(sem("summed"), 1)
            else:
                raise AssertionError

        def sum_rest(n, k, odd):
            pool.wait_ge(sem("squared"), n * KT + k + 1)
            pool.wait_ge(sem("summed"), n * KT + k)
            pool.tensor_tensor(ssum[:], ssum[:], sq[:, odd, :], ALU.add).then_inc(sem("summed"), 1)

        def sums(n):
            sum_square(n, 0)
            sum_rest(n, 1, 1)
            with pool.Fori(1, KT // 2) as it:
                sum_rest(n, it * 2, 0)
                sum_rest(n, it * 2 + 1, 1)

        pool.wait_ge(sem("x_turned"), 9)
        pool.memset(later[:], 1.0).then_inc(sem("later_step"), 1)
        pool.wait_ge(sem("later_step"), 1)
        lv = later[:].rearrange("p (b g) -> p b g", g=PAGES)
        pool.affine_select(out=lv, in_=lv, compare_op=ALU.is_gt, fill=0.0, base=PAGES,
                           pattern=[[PAGES, ND], [0, PAGES]], channel_multiplier=-1).then_inc(sem("later_step"), 1)
        pool.wait_ge(sem("later_step"), 2)
        pool.affine_select(out=lv, in_=lv, compare_op=ALU.is_gt, fill=0.0, base=0,
                           pattern=[[-PAGES, ND], [-1, PAGES]], channel_multiplier=1).then_inc(sem("later_step"), 1)
        pool.wait_ge(sem("masks_step"), 1)
        for g in range(2):
            mv = sampled(masks[:, g, :])
            pool.affine_select(out=mv, in_=mv, compare_op=ALU.is_ge, fill=0.0, base=P * g, pattern=[[-32, ND], [0, NT]],
                               channel_multiplier=1).then_inc(sem("masks_step"), 1)
        pool.wait_ge(sem("masks_step"), 3)
        for g in range(2):
            mv = sampled(masks[:, g, :])
            pool.affine_select(out=mv, in_=mv, compare_op=ALU.is_ge, fill=0.0, base=31 - P * g,
                               pattern=[[32, ND], [0, NT]], channel_multiplier=-1).then_inc(sem("masks_step"), 1)
        pool.wait_ge(sem("pid_loaded"), 16)
        lf_pages = I["cache_logf"][0].rearrange("n s h -> n (s h)")
        for i in range(ND * PAGES):
            page = pool.value_load(pid[0:1, i:i + 1], min_val=0, max_val=POOLP - 1)
            pool.dma_start(lfp[i:i + 1].rearrange("p s h -> p (s h)"), lf_pages[bass.ds(page, 1), :])\
                .then_inc(sem("lf_loaded"), 16)
        sums(1)
        pool.dma_start(x_save, xT[:]).then_inc(sem("x_saved"), 16)
        pool.wait_ge(sem("x_saved"), 16)
        pool.wait_ge(sem("xf_ready"), 2 * KT)
        pool.memset(qblk[:], 0.0)
        pool.memset(maskp[:], 0.0).then_inc(sem("maskp_step"), 1)
        pool.wait_ge(sem("maskp_step"), 1)
        for c in (0, 2):
            pool.affine_select(out=maskp[:, c * P:(c + 1) * P], in_=maskp[:, c * P:(c + 1) * P], compare_op=ALU.is_ge,
                               fill=-BIG, base=0, pattern=[[-1, P]], channel_multiplier=1).then_inc(sem("maskp_step"), 1)

        KO, VO = [O["k_prompt"][0, 0], O["k_sample"][0]], [O["v_prompt"][0, 0], O["v_sample"][0]]
        for step in STEPS:
            what, i = step[0], step[-1]
            if what == "suffix":
                pool.wait_ge(sem("sfx_ready"), 1)
                for b in range(ND):
                    pool.dma_start(suf_d[b].rearrange("h (g s) -> g h s", g=PAGES), sfx[b * PAGES:(b + 1) * PAGES, :, 1:])\
                        .then_inc(sem("suf_stored"), 16)
            elif what == "turn_gates":
                pool.wait_ge(sem("nat_ready"), 1)
                for b in range(2):
                    pool.dma_start(O["logf_prompt"][0, 0, toks(b), :], lfo[:, b, :]).then_inc(sem("kv_stored"), 16)
                pool.dma_start(O["logf_sample"][0].rearrange("b t h -> (b t) h"), lfo[0:NS, 2, :]).then_inc(sem("kv_stored"), 16)
            elif what == "turn_kv":
                for x in "kv":
                    for b in range(3):
                        copied(pool, x, b)
                for o, (po, so) in enumerate((KO, VO)):
                    pool.dma_start(po.rearrange("(b s) h d -> s b (h d)", s=P), kvn[:, 0:2, o * 512:(o + 1) * 512])\
                        .then_inc(sem("kv_stored"), 16)
                    pool.dma_start(so.rearrange("b t h d -> (b t) (h d)"), kvn[0:NS, 2, o * 512:(o + 1) * 512])\
                        .then_inc(sem("kv_stored"), 16)
            elif what == "keys":
                g = i // 8
                if i % 8 == 0:
                    pool.wait_ge(sem("suf_stored"), 16 * ND)
                    if g:
                        pool.wait_ge(sem("scores_read"), g)
                    for q in range(4):
                        src = suf_d[4 * g + q]
                        pool.dma_start(bias[32 * q:32 * (q + 1), :],
                                       bass.AP(src.tensor, src.offset, [[PAST, H_ATT], [0, NT], [1, PAST]]))\
                            .then_inc(sem("bias_loaded"), 16)
            elif what == "lru_out":
                copied(pool, "lru_state")
                pool.dma_start(O["lru_state_prompt"][0], lrs[0:1, :]).then_inc(sem("lru_stored"), 16)
                pool.dma_start(O["lru_state_sample"][0], lrs[1:1 + ND, :]).then_inc(sem("lru_stored"), 16)
            elif what == "state":
                copied(pool, "state", i)
                pool.dma_start(O["ssd_state_prompt"][0, 0, 8 * i:8 * i + 8].rearrange("(j e) p n -> (e p) j n", e=2),
                               sst[:, i, :].rearrange("q (j n) -> q j n", j=4)).then_inc(sem("state_stored"), 16)
            elif what == "ssd" and 1 <= i <= H_SSD:
                h = i - 1
                pool.wait_ge(sem("lseg_exp"), h + 1)
                if h == 0:
                    copied(pool, "cb", 1)
                if h >= 2:
                    if h % 2:
                        take(pool, "y", (h - 2) // 2)
                    else:
                        pool.wait_ge(sem("y_even"), h // 2)
                for n, cs in ((P, slice(0, 3 * P)), (NS, slice(3 * P, SEGW))):
                    m = pool.tensor_tensor(mseg[0:n, h % 2, cs], lseg[0:n, h % 2, cs], cbm[0:n, h // 8, cs], ALU.mult)
                m.then_inc(sem("mseg_ready"), 1)
        sums(2)
        sums(3)

    @block.tensor
    def _(pe):
        pe.wait_ge(sem("const_ready"), 2)
        for b in range(2):
            for kg in range(4):
                to = bank[(1 + 4 * b + kg) % 8]
                if kg == 0:
                    pe.wait_ge(sem(f"x_loaded{b}"), 16)
                for k in range(4):
                    m = pe.transpose(to[:, k * P:(k + 1) * P], xnat[:, b, (4 * kg + k) * P:(4 * kg + k + 1) * P],
                                     ident[:])
                m.then_inc(sem("x_turned"), 1)
        pe.wait_ge(sem("x_loaded2"), 16)
        pe.wait_ge(sem("x_kept"), 1)
        for k in range(KT):
            m = pe.transpose(bank[1][:, k * NS:(k + 1) * NS], xnat[0:NS, 2, k * P:(k + 1) * P], ident[0:NS, 0:NS])
        m.then_inc(sem("x_turned"), 1)
        pe.wait_ge(sem("gains_loaded"), 4 * 16)
        pe.wait_ge(sem("x_kept2"), 1)
        pe.transpose(bank[2][0:P, 0:64], gnat[:], ident[0:64, 0:64]).then_inc(sem("gains_turned"), 1)

        def turn_histories():
            pe.wait_ge(sem("params_loaded"), 8 * 16)
            pe.wait_ge(sem("x_kept2"), 3)
            pe.transpose(bank[6][0:P, 0:NPAR], pnat[:], ident[0:NPAR, 0:NPAR])
            pe.wait_ge(sem("hist_loaded"), 48)
            pe.wait_ge(sem("x_kept2"), 2)
            for c in range(16):
                pe.transpose(bank[4][:, c * 24:(c + 1) * 24], histn[:, c * P:(c + 1) * P], ident[0:24, 0:24])
            for c in range(4):
                pe.transpose(bank[4][:, 384 + c * ND:384 + (c + 1) * ND], h0n[:, c * P:(c + 1) * P], ident[0:ND, 0:ND])
            pe.wait_ge(sem("tables_ready"), 1)
            pe.wait_ge(sem("fold_ready"), 1)
            for r in range(4):
                m = pe.matmul(bank[4][32 * r:32 * r + 32, 416:420], tris[0:NS, :], fold[:], start=True, stop=True)
            m.then_inc(sem("hist_turned"), 1)

        def stat(n):
            pe.wait_ge(sem("summed"), (n + 1) * KT)
            pe.matmul(bank[STAT][:, 0:N], ones[:], ssum[:], start=True, stop=True).then_inc(sem("stat_ready"), 1)

        def products(out, slot, k, nk, rhs_hi, rhs_lo):
            hi = whi[:, slot, k * P:(k + 1) * P]
            lo = wlo[:, slot, k * P:(k + 1) * P]
            pe.matmul(out, hi, rhs_hi, start=k == 0, stop=False)
            pe.matmul(out, lo, rhs_hi, start=False, stop=False)
            return pe.matmul(out, hi, rhs_lo, start=False, stop=k == nk - 1)

        def up_pair(f, base, it4, m, first_norm):
            for j in range(2):
                i = base + it4 + 2 * m + j
                pe.wait_ge(sem("lo_done"), i + 1)
                for k in range(KT):
                    if first_norm and j == 0:
                        pe.wait_ge(sem("xn_ready"), FN[f] * KT + k + 1)
                    last = products(bank[(base + 2 * m + j) % 4][:, 0:N], (base + j) % 2, k, KT,
                                    xn_hi[:, k, :], xn_lo[:, k, :])
                last.then_inc(sem("w_used"), 1)
                if first_norm and j == 1 - f:
                    stat(FN[f])

        def mix_tensor():
            def one_row(rows, r, n=P):
                return ident[rows, r:r + 1].to_broadcast([rows.stop - rows.start, n])

            def turn(out, src, n=P):
                return pe.transpose(out, src, ident[0:n, 0:n])

            def in_tile(t):
                i = IN0 + t
                pe.wait_ge(sem("lo_done"), i + 1)
                if t >= 3:
                    pe.wait_ge(sem("in_taken"), t - 1)
                for k in range(KT):
                    if t == 0:
                        pe.wait_ge(sem("xn_ready"), KT + k + 1)
                    last = products(in_bank(t)[:, 0:N], i % 2, k, KT, xn_hi[:, k, :], xn_lo[:, k, :])
                last.then_inc(sem("w_used"), 1)
                if t == 0:
                    stat(1)

            def prompt_pv(h):
                to = claim(pe, "pv", h)[(h % 2) * HD:(h % 2 + 1) * HD, :]
                at = (h % 2) * 384
                v = slice(512 + h * HD, 512 + (h + 1) * HD)
                copied(pe, "p", h)
                pe.matmul(to[:, 0:P], kvn[:, 0, v], pts[:, at:at + P], start=True, stop=True)
                pe.matmul(to[:, P:NP_], kvn[:, 0, v], pts[:, at + P:at + NP_], start=True, stop=False)
                m = pe.matmul(to[:, P:NP_], kvn[:, 1, v], pts[:, at + NP_:at + 384], start=False, stop=True)
                m.then_inc(side_done("pv", h), 1)

            def key_scores(n):
                g, pg = n // PAGES, n % PAGES
                for u in range(4 * n, 4 * n + 4):
                    copied(pe, "kt", u)
                if pg == 0:
                    pe.wait_ge(sem("qblk_ready"), g + 1)
                    if g:
                        pe.wait_ge(sem("scores_read"), g)
                    else:
                        pe.wait_ge(sem("x_added"), XO0)
                for p in range(4):
                    for r in range(4):
                        m = pe.matmul(bank[2 + pg // 4][32 * r:32 * r + 32, pg % 4 * P:(pg % 4 + 1) * P], qblk[:, r, p, :],
                                      key_slot(r)[:, p * P:(p + 1) * P], start=p == 0, stop=p == 3)
                m.then_inc(sem("kts_used"), 1)

            def ssd_y(h):
                if h % 2 == 0:
                    claim(pe, "y", h // 2)
                to = side("y", h // 2)[(h % 2) * HD:(h % 2 + 1) * HD, :]
                c = slice(h * HD, (h + 1) * HD)
                m = mseg[:, h % 2, :]
                pe.wait_ge(sem("mseg_ready"), h + 1)
                pe.matmul(to[:, 0:P], xsn[:, 0, c], m[:, 0:P], start=True, stop=True)
                pe.matmul(to[:, P:NP_], xsn[:, 0, c], m[:, P:NP_], start=True, stop=False)
                pe.matmul(to[:, P:NP_], xsn[:, 1, c], m[:, NP_:3 * P], start=False, stop=True)
                last = pe.matmul(to[:, NP_:N], xsn[0:NS, 2, c], m[0:NS, 3 * P:SEGW], start=True, stop=True)
                last.then_inc(side_done("y", h // 2) if h % 2 else sem("y_even"), 1)

            def out_tile(part, n, it4, first):
                i = OUT0 + part * KT + n + it4
                pe.wait_ge(sem("lo_done"), i + 1)
                if not (first and part == 0 and n < 2):
                    pe.wait_ge(sem("x_added"), XO0 + part * KT + n + it4 - 1)
                for k in range(8):
                    if first and part == 0 and n == 0 and k in (0, 4):
                        pe.wait_ge(sem("merged"), k + 4)
                    if part == 0:
                        rhs = [x[:, k + 8 * (k >= 4), :] for x in (xn_hi, xn_lo)]
                    else:
                        rhs = [x[:, k, :] for x in (m_hi, m_lo)]
                    last = products(bank[n % 2][:, 0:N], (OUT0 + n) % 2, k, 8, *rhs)
                last.then_inc(sem("w_used"), 1)

            for step in STEPS:
                what, i = step[0], step[-1]
                if what == "in" and i < IN_TILES:
                    in_tile(i)
                elif what == "suffix":
                    to = claim(pe, "later")
                    pe.wait_ge(sem("total_ready"), 1)
                    pe.wait_ge(sem("later_step"), 3)
                    pe.matmul(to[0:64, 0:H_ATT], later[:], total[:], start=True, stop=True)\
                        .then_inc(side_done("later"), 1)
                elif what == "turn_gates":
                    to = claim(pe, "nat")
                    pe.wait_ge(sem("decay_ready"), 1)
                    for b in range(3):
                        for pl in range(3):
                            turn(to[0:rows_of(b), b * 144 + pl * 48:b * 144 + pl * 48 + 48], sc48[0:48, pl, toks(b)], 48)
                    turn(to[0:NS, 432:480], e48[0:48, :], 48).then_inc(side_done("nat"), 1)
                    to = claim(pe, "dec")
                    for j in range(8):
                        for e in range(2):
                            m = pe.matmul(to[e * HD:(e + 1) * HD, j * ND:(j + 1) * ND], one_row(SR, 32 + 2 * j + e, HD),
                                          strided(e48[SR, :], NT - 1, (NT, ND)), start=True, stop=True)
                    m.then_inc(side_done("dec"), 1)
                elif what == "turn_kv":
                    for b in range(3):
                        for x, src in (("k", kT), ("v", attT)):
                            to = claim(pe, x, b)
                            pe.wait_ge(sem("in_taken"), T_V if x == "k" else T_X)
                            for j in range(4):
                                m = turn(to[0:rows_of(b), j * P:(j + 1) * P], src[:, j, toks(b)])
                            m.then_inc(side_done(x, b), 1)
                elif what == "prompt":
                    if i < H_ATT:
                        to = claim(pe, "sc", i)
                        f = slice((i % 2) * HD, (i % 2 + 1) * HD)
                        c = slice((i % 2) * HD, (i % 2) * HD + H_ATT)
                        if i == 0:
                            pe.wait_ge(sem("negc_ready"), 1)
                        for out, q, k in ((to[:, 0:P], slice(0, P), slice(0, P)),
                                          (to[:, P:384], slice(P, NP_), slice(0, NP_))):
                            pe.matmul(out, qT[f, i // 2, q], kT[f, i // 2, k], start=True, stop=False)
                            m = pe.matmul(out, one_row(c, c.start + i), negc[c, k], start=False, stop=True)
                        m.then_inc(side_done("sc", i), 1)
                    if 1 <= i <= H_ATT:
                        to = claim(pe, "p", i - 1)
                        pe.wait_ge(sem("probs_ready"), i)
                        for q in range(3):
                            at = (i - 1) % 2 * 384 + q * P
                            m = turn(to[:, q * P:(q + 1) * P], ps[:, at:at + P])
                        m.then_inc(side_done("p", i - 1), 1)
                    if i >= 2:
                        prompt_pv(i - 2)
                elif what == "keys":
                    if i % PAGES:
                        key_scores(i - 1)
                    for u in range(4 * i, 4 * i + 4):
                        to = claim(pe, "kt", u)
                        pe.wait_ge(sem(f"cache_k_loaded{u % 4}"), 16 * (u // 4 + 1))
                        for p in range(4):
                            m = turn(to[:, p * P:(p + 1) * P], kpage[:, u % 4, p * P:(p + 1) * P])
                        m.then_inc(side_done("kt", u), 1)
                elif what == "keys_end":
                    key_scores(PAGES * i + PAGES - 1)
                    if i:
                        pe.wait_ge(sem("att_o_ready"), i)
                    else:
                        pe.wait_ge(sem("x_added"), XO0)
                    for p in range(4):
                        for r in range(4):
                            pe.matmul(bank[4][32 * r:32 * r + 32, 0:NS], qblk[:, r, p, :], kT[:, p, NP_:N],
                                      start=p == 0, stop=False)
                    for r in range(4):
                        m = pe.matmul(bank[4][32 * r:32 * r + 32, 0:NS], head_rows[:], negc[0:H_ATT, NP_:N],
                                      start=False, stop=True)
                    m.then_inc(sem("scores_ready"), 1)
                elif what == "probs":
                    pe.wait_ge(sem("sexp_ready"), i + 1)
                    for q in range(3):
                        to = claim(pe, "pt", i, q)
                        for c in range(4 if q < 2 else 1):
                            at = q * 512 + c * P
                            if q < 2:
                                m = turn(to[:, c * P:(c + 1) * P], ps[:, at:at + P])
                            else:
                                m = turn(to[0:NS, 0:P], ps[:, at:at + NS])
                        m.then_inc(side_done("pt", i, q), 1)
                elif what == "values":
                    pg = i % PAGES
                    if pg == 0:
                        copied(pe, "pt", i // PAGES, 2)
                    for r in range(4):
                        slot, loads = value_slot(4 * i + r)
                        pe.wait_ge(sem(f"cache_v_loaded{slot}"), 16 * loads)
                    for r in range(4):
                        slot, loads = value_slot(4 * i + r)
                        pe.matmul(bank[4][32 * r:32 * r + 32, :], pts[:, pg * P + 32 * r:pg * P + 32 * r + 32],
                                  vpages[:, slot, :], start=pg == 0, stop=False).then_inc(sem("vpage_used"), 1)
                    if pg == PAGES - 1:
                        for r in range(4):
                            m = pe.matmul(bank[4][32 * r:32 * r + 32, :], pts[0:NS, PAST + 32 * r:PAST + 32 * r + 32],
                                          kvn[0:NS, 2, 512:], start=False, stop=True)
                        m.then_inc(sem("sample_pv"), 1)
                elif what == "merge_heads":
                    to = claim(pe, "heads", i)
                    pe.wait_ge(sem("att_o_ready"), i + 1)
                    for p in range(4):
                        m = turn(to[:, p * P:(p + 1) * P], att_o[:, p * P:(p + 1) * P])
                    m.then_inc(side_done("heads", i), 1)
                elif what == "lru_gates":
                    pe.wait_ge(sem("conv_done"), XT_ + LT_)
                    pe.wait_ge(sem("small_loaded"), 16 * 10)
                    for c in range(4):
                        for x, w in (("r", lwa), ("i", lwx)):
                            to = claim(pe, x, c)
                            pe.matmul(to[:, 0:N], w[:, c, :], uT[:, c, :], start=True, stop=True)\
                                .then_inc(side_done(x, c), 1)
                elif what == "hist":
                    to = claim(pe, "hist", i)
                    pe.wait_ge(sem("conv_done"), XT_ + LT_)
                    for c in range(4):
                        m = turn(to[0:HC + HC * ND, c * P:(c + 1) * P], histO[:, 4 * i + c, :])
                    m.then_inc(side_done("hist", i), 1)
                elif what == "lru_out":
                    to = claim(pe, "lru_state")
                    pe.wait_ge(sem("lst_ready"), 1)
                    for c in range(4):
                        m = turn(to[0:1 + ND, c * P:(c + 1) * P], lst[:, c, :])
                    m.then_inc(side_done("lru_state"), 1)
                elif what == "turn_x":
                    pe.wait_ge(sem("conv_silu"), 3)
                    for half in range(2):
                        to = claim(pe, "x", i, half)
                        for c in range(4):
                            m = turn(to[0:rows_of(i), c * P:(c + 1) * P], xsT[:, 4 * half + c, toks(i)])
                        m.then_inc(side_done("x", i, half), 1)
                    to = claim(pe, "b", i)
                    for c in range(2):
                        m = turn(to[0:rows_of(i), c * P:(c + 1) * P], xsT[:, 8 + c, toks(i)])
                    m.then_inc(side_done("b", i), 1)
                elif what == "scores":
                    for g in range(2):
                        to = claim(pe, "cb", g)
                        for cs, kb, q in PAIRS:
                            m = pe.matmul(to[0:rows_of(kb), cs], xsT[:, 8 + g, toks(kb)], xsT[:, 10 + g, q],
                                          start=True, stop=True)
                        m.then_inc(side_done("cb", g), 1)
                elif what == "ssd":
                    if i < H_SSD:
                        to = claim(pe, "acs", i)
                        pe.matmul(to[:, 0:N], one_row(SR, 32 + i), sc48[SR, CS, :], start=True, stop=True)\
                            .then_inc(side_done("acs", i), 1)
                    if i >= 2:
                        ssd_y(i - 2)
                elif what == "out":
                    out_tile(0, i, 0, True)
                elif what == "state":
                    to = claim(pe, "state", i)
                    pe.wait_ge(sem("xw_ready"), 1)
                    for j in range(4):
                        c = 4 * i + j
                        for b in range(2):
                            m = pe.matmul(to[:, j * P:(j + 1) * P], xsn[:, b, c * P:(c + 1) * P], bnat[:, b, i * ST:(i + 1) * ST],
                                          start=b == 0, stop=b == 1)
                    m.then_inc(side_done("state", i), 1)
                elif what == "unit":
                    if i < 2 * ND:
                        to = claim(pe, "ht", i)
                        pe.wait_ge(sem(f"h0_loaded{i % 4}"), 16 * (i // 4 + 1))
                        for j in range(4):
                            m = turn(to[:, j * P:(j + 1) * P], h0[:, i % 4, j * P:(j + 1) * P])
                        m.then_inc(side_done("ht", i), 1)
                    if i:
                        b, g = (i - 1) // 2, (i - 1) % 2
                        to = claim(pe, "up", i - 1)
                        pe.wait_ge(sem("bexp_ready"), b + 1)
                        for j in range(4):
                            c = 4 * g + j
                            m = pe.matmul(to[:, j * P:(j + 1) * P], xsn[0:NS, 2, c * P:(c + 1) * P],
                                          bexp[0:NS, b % 4, g * ST:(g + 1) * ST], start=True, stop=True)
                        m.then_inc(side_done("up", i - 1), 1)
                        if g == 1:
                            for q in range(2):
                                copied(pe, "ht", 2 * b + q)
                            for q in range(2):
                                pe.matmul(bank[2 + q][NS * q:NS * (q + 1), :], cpad[:, q, b, :], h0t[:, q, :],
                                          start=b == 0, stop=b == ND - 1).then_inc(sem("h0t_used"), 1)
                elif what == "carry":
                    to = claim(pe, "ys")
                    pe.wait_ge(sem("ys_ready"), 2)
                    for j in range(8):
                        m = turn(to[:, j * NS:(j + 1) * NS], ys[0:NS, j * P:(j + 1) * P], NS)
                    m.then_inc(side_done("ys"), 1)
                elif what == "sum_prompt":
                    g = i // 4
                    pe.wait_ge(sem("y_squared"), i + 1)
                    pe.matmul(bank[4][:, g * NP_:(g + 1) * NP_], ones[:], zT[:, i, 0:NP_], start=i % 4 == 0, stop=i % 4 == 3)\
                        .then_inc(sem("prompt_mean"), 1)
                elif step == ("groups", 0):
                    to = claim(pe, "mean")
                    pe.wait_ge(sem("gsq_ready"), 1)
                    pe.matmul(to[:, 0:2 * NS], ones[:], gsq[:].rearrange("p g t -> p (g t)"), start=True, stop=True)\
                        .then_inc(side_done("mean"), 1)
            pe.wait_ge(sem("merged"), 16)
            for j in range(4):
                out_tile(1, j, 0, True)
            with pe.Fori(1, KT // 4) as it:
                for j in range(4):
                    out_tile(1, j, it * 4, False)

        for f in range(2):
            if f:
                mix_tensor()
            for g, n in enumerate(GROUPS):
                base, ff0, xa0 = seg["up", f, g], FF0[f, g], XA0[f, g]
                for m in range(3):
                    if m == 0 and xa0:
                        pe.wait_ge(sem("x_added"), xa0 - 2)
                    if m == 1 and xa0:
                        pe.wait_ge(sem("x_added"), xa0)
                    if m == 2:
                        pe.wait_ge(sem("gated"), ff0 + 1)
                    up_pair(f, base, 0, m, g == 0 and m == 0)
                    if base == 0 and m == 0:
                        turn_histories()
                with pe.Fori(0, (n - 3) // 2) as it:
                    for m in range(2):
                        pe.wait_ge(sem("gated"), it * 2 + (ff0 + m + 2))
                        up_pair(f, base + 6, it * 4, m, False)
                base = seg["down", f, g]

                def down(it4, j, first):
                    i = base + it4 + j
                    pe.wait_ge(sem("lo_done"), i + 1)
                    if first:
                        pe.wait_ge(sem("gated"), ff0 + n - 1 + (j >= 2))
                    else:
                        pe.wait_ge(sem("x_added"), xa0 + it4 + j - 3)
                    for k in range(n):
                        if first and j == 0 and k in (0, n - 1):
                            pe.wait_ge(sem("h_ready"), ff0 + (n - 1 if k == 0 else n))
                        last = products(bank[(base + j) % 4][:, 0:N], (base + j) % 2, k, n,
                                        h_hi[:, k, :], h_lo[:, k, :])
                    last.then_inc(sem("w_used"), 1)

                for j in range(4):
                    down(0, j, True)
                with pe.Fori(1, KT // 4) as it:
                    for j in range(4):
                        down(it * 4, j, False)
        pe.wait_ge(sem("summed"), 4 * KT)
        pe.matmul(bank[STAT][:, 0:3], ones[:], ones[:, 0:3], start=True, stop=True)
        for b in range(3):
            m = pe.matmul(bank[STAT][0:rows_of(b), b:b + 1], ssum[:, toks(b)], ones[:, 0:1], start=True, stop=True)
        m.then_inc(sem("stat_ready"), 1)
        for kg in range(4):
            for b in range(3):
                rows = P if b < 2 else NS
                t = 3 * kg + b
                if t >= 7:
                    pe.wait_ge(sem("y_ready2" if (t - 7) % 2 else "y_ready"), (t - 7) // 2 + 1)
                for k in range(4):
                    pe.wait_ge(sem("xf_ready"), 3 * KT + 4 * kg + k + 1)
                    m = pe.transpose(bank[t % 7][0:rows, k * P:(k + 1) * P], yT[:, 4 * kg + k, b * P:b * P + rows],
                                     ident[:])
                m.then_inc(sem("y_turned"), 1)

    @block.scalar
    def _(act):
        for n, name in enumerate(("ffn1_norm", "mix_norm", "ffn2_norm")):
            act.dma_start(gnat[n * KT:(n + 1) * KT, :], I[name][0].rearrange("(k p) -> k p", p=P))\
                .then_inc(sem("gains_loaded"), 16)
        act.dma_start(gnat[3 * KT:, :], I["final_norm"].rearrange("(k p) -> k p", p=P))\
            .then_inc(sem("gains_loaded"), 16)
        rows = ((R_CW, I["ssd_conv_w"][0].rearrange("w (c p) -> (w c) p", p=P)),
                (R_CB, I["ssd_conv_b"][0].rearrange("(c p) -> c p", p=P)),
                (R_LW, I["lru_conv_w"][0].rearrange("w (c p) -> (w c) p", p=P)),
                (R_LB, I["lru_conv_b"][0].rearrange("(c p) -> c p", p=P)),
                (R_BA, I["lru_b_a"][0].rearrange("(c p) -> c p", p=P)),
                (R_BX, I["lru_b_x"][0].rearrange("(c p) -> c p", p=P)),
                (R_LAM, I["lru_lambda"][0].rearrange("(c p) -> c p", p=P)),
                (R_NRM, I["ssd_norm"][0].rearrange("(c p) -> c p", p=P)))
        for r, src in rows:
            act.dma_start(pnat[r:r + src.shape[0], :], src).then_inc(sem("params_loaded"), 16)

        def square(n, k, odd, wait_pool):
            if wait_pool:
                act.wait_ge(sem("summed"), n * KT + k - 1)
            act.activation(sq[:, odd, :], xT[:, bass.ds(k, 1), :].rearrange("p o t -> p (o t)"), ACT.Square)\
                .then_inc(sem("squared"), 1)

        def hi(base, it4, j, nk):
            i = base + it4 + j
            slot = (base + j) % LOADS
            act.wait_ge(sem(f"raw_ready{slot}"), 16 * ((base + j) // LOADS + 1) + it4 * 4)
            if not isinstance(i, int) or i >= 2:
                act.wait_ge(sem("w_used"), i - 1)
            act.copy(tile_ap(whi, (base + j) % 2, nk), tile_ap(wraw, slot, nk)).then_inc(sem("hi_done"), 1)

        for b in range(2):
            for kg in (1, 3):
                act.wait_ge(sem("x_turned"), 4 * b + kg + 1)
                act.copy(xT[:, 4 * kg:4 * kg + 4, b * P:(b + 1) * P],
                         bank[(1 + 4 * b + kg) % 8][:, :].rearrange("p (k t) -> p k t", k=4)).then_inc(sem("x_kept2"), 1)
            hi(0, 0, b, KT)
        act.wait_ge(sem("x_turned"), 9)
        act.dma_start(histn[:, 0:XBC], I["state_ssd_conv"][0].rearrange("b w c -> (b w) c")).then_inc(sem("hist_loaded"), 16)
        act.dma_start(histn[:, XBC:], I["state_lru_conv"][0].rearrange("b w c -> (b w) c")).then_inc(sem("hist_loaded"), 16)
        act.dma_start(h0n[:], I["state_lru"][0]).then_inc(sem("hist_loaded"), 16)

        def silu(ff, par):
            act.wait_ge(sem("scaled"), ff + 1)
            act.activation(sg[:, par, :], sg[:, par, :], ACT.Silu).then_inc(sem("silu_done"), 1)

        def root(n):
            act.wait_ge(sem("mean_ready"), n + 1)
            act.activation(rs[:, 1, :], rs[:, 0, :], ACT.Ln).then_inc(sem("root_step"), 1)
            act.wait_ge(sem("root_step"), 2 * n + 1)
            act.activation(rs[:, 1, :], rs[:, 1, :], ACT.Exp, scale=-0.5).then_inc(sem("root_step"), 1)

        def finish_x(n, k, odd, wait_pool):
            act.wait_ge(sem("xf_ready"), n * KT + k + 1)
            if n < 3:
                act.copy(xn_hi[:, bass.ds(k, 1), :].rearrange("p o t -> p (o t)"), xf[:, odd, :])\
                    .then_inc(sem("xhi_ready"), 1)
            square(n, k, odd, wait_pool)

        def mix_scalar():
            def hi_mix(n):
                if n < IN_TILES:
                    hi(IN0, 0, n, KT)
                else:
                    n -= IN_TILES
                    act.wait_ge(sem(f"wo_half{(OUT0 + n) % LOADS}"), 16 * (n // 4 + 1))
                    hi(OUT0, 0, n, 8)

            act.wait_ge(sem("w_small"), 32)
            hi_mix(0)
            finish_x(1, KT - 1, 1, True)
            for step in STEPS:
                what, i = step[0], step[-1]
                if what == "in":
                    if i < IN_TILES:
                        hi_mix(i + 1)
                    if i == 1:
                        root(1)
                    if i in (T_Z + 5, T_Z + 8):
                        q = (i - T_Z) // 8
                        act.wait_ge(sem("in_taken"), T_Z + 4 * q + 4)
                        act.activation(zT[:, 4 * q:4 * q + 4, :], zT[:, 4 * q:4 * q + 4, :], ACT.Silu)\
                            .then_inc(sem("z_silu"), 1)
                    if i in (T_X + 5, T_X + 9, T_X + 13):
                        q = (i - T_X - 5) // 4
                        act.wait_ge(sem("conv_done"), 4 * q + 4)
                        act.activation(xsT[:, 4 * q:4 * q + 4, :], xsT[:, 4 * q:4 * q + 4, :], ACT.Silu)\
                            .then_inc(sem("conv_silu"), 1)
                elif what == "lam":
                    act.wait_ge(sem("abs_ready"), 2)
                    act.activation(lam[:, 1, :], lam[:, 1, :], ACT.Exp, scale=-1.0).then_inc(sem("exp_ready"), 1)
                elif step == ("gates", 0):
                    act.wait_ge(sem("abs_ready"), 1)
                    act.activation(ps[0:72, 0:N], ps[0:72, 0:N], ACT.Exp, scale=-1.0).then_inc(sem("exp_ready"), 1)
                elif step == ("gates", 2):
                    act.wait_ge(sem("tables_ready"), 1)
                    act.wait_ge(sem("small_loaded"), 16 * 10)
                    act.activation(col[0:72, 3:4], col[0:72, 2:3], ACT.Exp).then_inc(sem("coef_ready"), 1)
                    act.wait_ge(sem("sums_ready"), 1)
                    act.activation(e48[0:72, :], sc48[0:72, CS, NP_:N], ACT.Exp)
                    act.activation(sc48[0:72, WDC, :], sc48[0:72, WDC, :], ACT.Exp).then_inc(sem("decay_ready"), 1)
                elif what == "turn_kv":
                    for b in range(3):
                        src = take(act, "v", b)
                        act.copy(kvn[0:rows_of(b), b, 512:], src[0:rows_of(b), :]).then_inc(side_read("v", b), 1)
                elif what == "prompt":
                    if i < H_ATT:
                        act.wait_ge(sem("fox_max"), i + 1)
                        for b, c in enumerate((slice(0, P), slice(P, 384))):
                            w = ps[:, (i % 2) * 384 + c.start:(i % 2) * 384 + c.stop]
                            n = 2 * (i % 2) + b
                            m = act.activation(w, w, ACT.Exp, bias=nm[:, n:n + 1], accum_out=rsum[:, n:n + 1])
                        m.then_inc(sem("fox_exp"), 1)
                    if 1 <= i <= H_ATT:
                        h = i - 1
                        src = take(act, "p", h)
                        if h >= 2:
                            take(act, "pv", h - 2)
                        act.copy(pts[:, h % 2 * 384:(h % 2 + 1) * 384], src[:, 0:384]).then_inc(side_read("p", h), 1)
                elif what == "keys":
                    for u in range(4 * i, 4 * i + 4):
                        src = take(act, "kt", u)
                        if i and u % 4 == 0:
                            act.wait_ge(sem("kts_used"), i)
                        if u == 2:
                            act.wait_ge(sem("kv_stored"), 16 * 7)
                        act.copy(key_slot(u % 4), src[:, :]).then_inc(side_read("kt", u), 1)
                elif what == "max":
                    act.wait_ge(sem("sample_max"), i + 1)
                    act.activation(ps[:, 0:PAST + NS], ps[:, 0:PAST + NS], ACT.Exp, bias=nm[:, 0:1],
                                   accum_out=rsum[:, 0:1]).then_inc(sem("sexp_ready"), 1)
                elif what == "probs":
                    for q in range(3):
                        src = take(act, "pt", i, q)
                        if q == 0:
                            if i:
                                act.wait_ge(sem("sample_pv"), i)
                            else:
                                take(act, "pv", H_ATT - 1)
                        if q < 2:
                            m = act.copy(pts[:, q * 512:(q + 1) * 512], src[:, :])
                        else:
                            m = act.copy(pts[0:NS, PAST:PAST + P], src[0:NS, 0:P])
                        m.then_inc(side_read("pt", i, q), 1)
                elif what == "lru_gates":
                    for c in range(4):
                        for x, to, r0 in (("r", lru_r, R_BA), ("i", lru_i, R_BX)):
                            src = take(act, x, c)
                            act.activation(to[:, c, :], src[:, 0:N], ACT.Sigmoid, bias=params[:, r0 + c:r0 + c + 1])\
                                .then_inc(side_read(x, c), 1)
                elif what == "lru_decay":
                    for x, c in (("r", 3), ("i", 3), ("i", 2)):
                        copied(act, x, c)
                    act.wait_ge(sem("lru_step"), 1)
                    for c in range(4):
                        m = act.activation(uT[:, c, :], lru_r[:, c, :], ACT.Tanh, scale=lam[:, 0, c:c + 1])
                    m.then_inc(sem("lru_decayed"), 1)
                    act.wait_ge(sem("lru_decayed"), 1)
                    for c in range(4):
                        m = act.activation(lru_r[:, c, :], lru_r[:, c, :], ACT.Exp, scale=lam[:, 2, c:c + 1])
                    m.then_inc(sem("lru_decayed"), 1)
                elif what == "hist":
                    src = take(act, "hist", i)
                    if i >= 2:
                        act.wait_ge(sem(f"hist_stored{i % 2}"), 32)
                    act.copy(hout[0:HC + HC * ND, i % 2, :], src[0:HC + HC * ND, :]).then_inc(side_read("hist", i), 1)
                elif what == "lru_scan":
                    act.wait_ge(sem("lru_square"), 4)
                    act.activation(uT[:], uT[:], ACT.Sqrt).then_inc(sem("lru_root"), 1)
                elif what == "lru_out":
                    act.wait_ge(sem("in_taken"), T_Z)
                    act.activation(gT[:], gT[:], ACT.Gelu_apprx_tanh).then_inc(sem("g_ready"), 1)
                elif what == "merge":
                    act.wait_ge(sem("w_used"), IN0 + IN_TILES)
                    copied(act, "heads", 1)
                    act.copy(xn_hi[:, 0:4, :], attT[:]).then_inc(sem("m_rounded"), 1)
                    act.wait_ge(sem("lru_done"), 1)
                    act.copy(xn_hi[:, 12:16, :], gT[:]).then_inc(sem("m_rounded"), 1)
                elif what == "ssd":
                    if i < H_SSD:
                        copied(act, "acs", i)
                        w, s = lseg[:, i % 2, 0:3 * P], lseg[0:NS, i % 2, 3 * P:]
                        act.activation(w, w, ACT.Exp)
                        act.activation(s, s, ACT.Exp).then_inc(sem("lseg_exp"), 1)
                elif what == "out":
                    hi_mix(IN_TILES + i + 1)
                elif what == "state":
                    src = take(act, "state", i)
                    act.copy(sst[:, i, :], src[:, :]).then_inc(side_read("state", i), 1)
                elif what == "unit" and i < 2 * ND:
                    src = take(act, "ht", i)
                    if i >= 2:
                        act.wait_ge(sem("h0t_used"), i - 1)
                    act.copy(h0t[:, i % 2, :], src[:, :]).then_inc(side_read("ht", i), 1)
                elif what == "gate_prompt":
                    act.wait_ge(sem("gated_y"), i + 1)
                    act.activation(zT[:, i, 0:NP_], xsT[:, i, 0:NP_], ACT.Square).then_inc(sem("y_squared"), 1)
                elif what == "carry":
                    act.wait_ge(sem("gated_y"), 9)
                    act.activation(zT[:, :, NP_:N], xsT[:, 0:8, NP_:N], ACT.Square).then_inc(sem("y_squared"), 1)
                elif step == ("groups", 0):
                    copied(act, "mean")
                    act.activation(grs[:, 1], grs[:, 0], ACT.Ln).then_inc(sem("groot_step"), 1)
                    act.wait_ge(sem("groot_step"), 1)
                    act.activation(grs[:, 1], grs[:, 1], ACT.Exp, scale=-0.5).then_inc(sem("groot_step"), 1)
                elif step == ("groups", 2):
                    for q in range(2):
                        act.wait_ge(sem(f"snew_stored{q}"), 16 * ND)
                    for g in range(2):
                        act.wait_ge(sem("yn_done"), g + 1)
                        act.copy(m_hi[:, 4 * g:4 * g + 4, :], zT[:, 4 * g:4 * g + 4, :]).then_inc(sem("m_rounded"), 1)
            for j in range(1, 4):
                hi_mix(IN_TILES + KT + j)
                if j >= 2:
                    finish_x(2, j - 2, j % 2, False)
            with act.Fori(1, KT // 4) as it:
                for j in range(4):
                    act.wait_ge(sem(f"wo_half{(OUT0 + j) % LOADS}"), it * 16 + 16 * 5)
                    hi(OUT0 + KT, it * 4, j, 8)
                    finish_x(2, it * 4 + (j - 2), j % 2, True)
            finish_x(2, KT - 2, 0, True)
            for q in range(2):
                act.wait_ge(sem(f"snew_stored{q}"), 16 * ND)

        for f in range(2):
            if f:
                mix_scalar()
            if f == 0:
                for k in range(KT):
                    act.wait_ge(sem("xf_ready"), k + 1)
                    act.copy(xn_hi[:, k, :], xf[:, k % 2, :]).then_inc(sem("xhi_ready"), 1)
                for k in range(KT):
                    square(0, k, k % 2, k >= 2)
                hi(0, 0, 2, KT)
            else:
                hi(seg["up", f, 0], 0, 0, KT)
                finish_x(2, KT - 1, 1, True)
                hi(seg["up", f, 0], 0, 1, KT)
            root(FN[f])
            for g, n in enumerate(GROUPS):
                base, ff0 = seg["up", f, g], FF0[f, g]
                for m in range(3):
                    for j in range(2):
                        if g or m > 1 or m == 1 and (f or j):
                            hi(base + 2 * m, 0, j, KT)
                    silu(ff0 + m, (ff0 + m) % 2)
                with act.Fori(0, (n - 3) // 2) as it:
                    for m in range(2):
                        for j in range(2):
                            hi(base + 6, it * 4, 2 * m + j, KT)
                        silu(it * 2 + (ff0 + 3 + m), (ff0 + 3 + m) % 2)
                base = seg["down", f, g]
                for j in range(4):
                    hi(base, 0, j, n)
                    if g == 2 and j >= 2:
                        finish_x(FN[f] + 1, j - 2, j % 2, False)
                with act.Fori(1, KT // 4) as it:
                    for j in range(4):
                        hi(base, it * 4, j, n)
                        if g == 2:
                            finish_x(FN[f] + 1, it * 4 + (j - 2), j % 2, True)
                if g == 2:
                    finish_x(FN[f] + 1, KT - 2, 0, True)
        finish_x(3, KT - 1, 1, True)
        act.wait_ge(sem("mean_ready"), 4)
        act.activation(rs[:, 1, 0:3], rs[:, 0, 0:3], ACT.Ln).then_inc(sem("root_step"), 1)
        act.wait_ge(sem("root_step"), 7)
        act.activation(rs[:, 1, 0:3], rs[:, 1, 0:3], ACT.Exp, scale=-0.5).then_inc(sem("root_step"), 1)
        for kg in range(4):
            for b in range(3):
                t = 3 * kg + b
                if t % 2:
                    rows = P if b < 2 else NS
                    act.wait_ge(sem("y_turned"), t + 1)
                    act.wait_ge(sem("newton"), 16)
                    act.activation(ynat[0:rows, b, kg * 512:(kg + 1) * 512], bank[t % 7][0:rows, :], ACT.Copy,
                                   scale=rs[0:rows, 2, b:b + 1]).then_inc(sem("y_ready2"), 1)

    @block.vector
    def _(dve):
        for b in range(2):
            for kg in (0, 2):
                dve.wait_ge(sem("x_turned"), 4 * b + kg + 1)
                dve.tensor_copy(xT[:, 4 * kg:4 * kg + 4, b * P:(b + 1) * P],
                                bank[(1 + 4 * b + kg) % 8][:, :].rearrange("p (k t) -> p k t", k=4))\
                    .then_inc(sem("x_kept"), 1)
        dve.wait_ge(sem("x_turned"), 9)
        dve.tensor_copy(xT[:, :, NP_:], bank[1][:, :].rearrange("p (k t) -> p k t", k=KT)).then_inc(sem("x_kept"), 1)
        dve.wait_ge(sem("gains_turned"), 1)
        dve.tensor_copy(gains[:].rearrange("p n k -> p (n k)"), bank[2][:, 0:64]).then_inc(sem("gains_kept"), 1)

        def root(n, w=N):
            y, z, v = rs[:, 1, 0:w], rs[:, 2, 0:w], rs[:, 0, 0:w]
            dve.wait_ge(sem("stat_ready"), n + 1)
            dve.tensor_scalar(v, bank[STAT][:, 0:w], 1.0 / D, EPS, ALU.mult, ALU.add).then_inc(sem("mean_ready"), 1)
            dve.wait_ge(sem("root_step"), 2 * n + 2)
            dve.tensor_tensor(z, y, y, ALU.mult).then_inc(sem("newton"), 1)
            dve.wait_ge(sem("newton"), 4 * n + 1)
            dve.tensor_tensor(z, z, v, ALU.mult).then_inc(sem("newton"), 1)
            dve.wait_ge(sem("newton"), 4 * n + 2)
            dve.tensor_scalar(z, z, -0.5, 1.5, ALU.mult, ALU.add).then_inc(sem("newton"), 1)
            dve.wait_ge(sem("newton"), 4 * n + 3)
            dve.tensor_tensor(z, z, y, ALU.mult).then_inc(sem("newton"), 1)
            dve.wait_ge(sem("newton"), 4 * n + 4)

        def scale_x(n, k, odd, added=None):
            if added is not None:
                dve.wait_ge(sem("x_added"), added)
            gain = gains[:, n, bass.ds(k, 1)]
            xk = xT[:, bass.ds(k, 1), :].rearrange("p o t -> p (o t)")
            if n == 3:
                to = yT[:, bass.ds(k, 1), :].rearrange("p o t -> p (o t)")
            else:
                to = xf[:, odd, :]
                if n or k >= 2:
                    dve.wait_ge(sem("xn_ready"), n * KT + k - 1)
            dve.tensor_scalar(to, xk, gain, None, ALU.mult).then_inc(sem("xf_ready"), 1)

        def split_x(n, k, odd):
            if n < 3:
                dve.wait_ge(sem("xhi_ready"), n * KT + k + 1)
                dve.tensor_tensor(xn_lo[:, bass.ds(k, 1), :].rearrange("p o t -> p (o t)"), xf[:, odd, :],
                                  xn_hi[:, bass.ds(k, 1), :].rearrange("p o t -> p (o t)").bitcast(F32), ALU.subtract)\
                    .then_inc(sem("xn_ready"), 1)

        def lo(base, it4, j, nk):
            i = base + it4 + j
            dve.wait_ge(sem("hi_done"), i + 1)
            s = (base + j) % 2
            dve.tensor_tensor(tile_ap(wlo, s, nk), tile_ap(wraw, (base + j) % LOADS, nk),
                              tile_ap(whi, s, nk).bitcast(F32), ALU.subtract).then_inc(sem("lo_done"), 1)

        def pre(i, bk, ff, par):
            dve.wait_ge(sem("w_used"), i + 1)
            if not isinstance(ff, int) or ff >= 2:
                dve.wait_ge(sem("gated"), ff - 1)
            dve.tensor_tensor(sg[:, par, :], bank[bk][:, 0:N], rs[:, 2, :], ALU.mult).then_inc(sem("scaled"), 1)

        def gate(i, bk, ff, par, slot):
            dve.wait_ge(sem("w_used"), i + 1)
            if not isinstance(ff, int) or ff >= 2:
                dve.wait_ge(sem("h_ready"), ff - 1)
            dve.tensor_tensor(hm[:, par, :], bank[bk][:, 0:N], rs[:, 2, :], ALU.mult).then_inc(sem("up_scaled"), 1)
            dve.wait_ge(sem("up_scaled"), ff + 1)
            dve.wait_ge(sem("silu_done"), ff + 1)
            dve.tensor_tensor(hm[:, par, :], hm[:, par, :], sg[:, par, :], ALU.mult).then_inc(sem("gated"), 1)
            dve.wait_ge(sem("gated"), ff + 1)
            dve.tensor_copy(h_hi[:, bass.ds(slot, 1), :].rearrange("p o t -> p (o t)"), hm[:, par, :])\
                .then_inc(sem("h_rounded"), 1)
            dve.wait_ge(sem("h_rounded"), ff + 1)
            dve.tensor_tensor(h_lo[:, bass.ds(slot, 1), :].rearrange("p o t -> p (o t)"), hm[:, par, :],
                              h_hi[:, bass.ds(slot, 1), :].rearrange("p o t -> p (o t)").bitcast(F32),
                              ALU.subtract).then_inc(sem("h_ready"), 1)

        def add_x(i, bk, n_add, before, k, scale):
            dve.wait_ge(sem("w_used"), i + 1)
            if before is not None:
                dve.wait_ge(sem("x_added"), before)
            xk = xT[:, bass.ds(k, 1), :].rearrange("p o t -> p (o t)")
            dve.scalar_tensor_tensor(out=xk, in0=bank[bk][:, 0:N], scalar=scale, in1=xk, op0=ALU.mult,
                                     op1=ALU.add).then_inc(sem("x_added"), 1)

        class Chain:
            n = 0

            def __call__(self, instruction):
                instruction.then_inc(sem("chain"), 1)
                self.n += 1
                dve.wait_ge(sem("chain"), self.n)

        chain = Chain()

        def absolute(e, v):
            dve.scalar_tensor_tensor(out=e, in0=v, scalar=-1.0, in1=v, op0=ALU.mult, op1=ALU.max)\
                .then_inc(sem("abs_ready"), 1)

        def softplus(v, e, s, p, q, nth):
            softplus_start(e, s, p, q, nth)
            softplus_end(v, s, p, q)

        def softplus_start(e, s, p, q, nth):
            dve.wait_ge(sem("exp_ready"), nth)
            chain(dve.tensor_scalar(s, e, 2.0, None, ALU.add))
            chain(dve.reciprocal(s, s))
            chain(dve.tensor_tensor(s, s, e, ALU.mult))
            chain(dve.tensor_tensor(p, s, s, ALU.mult))
            chain(dve.tensor_scalar(q, p, 1.0 / 17, None, ALU.mult))

        def softplus_end(v, s, p, q):
            for c in range(15, 1, -2):
                chain(dve.scalar_tensor_tensor(out=q, in0=q, scalar=1.0 / c, in1=p, op0=ALU.add, op1=ALU.mult))
            chain(dve.scalar_tensor_tensor(out=q, in0=q, scalar=1.0, in1=s, op0=ALU.add, op1=ALU.mult))
            chain(dve.tensor_scalar(v, v, 0.0, None, ALU.max))
            chain(dve.scalar_tensor_tensor(out=v, in0=q, scalar=2.0, in1=v, op0=ALU.mult, op1=ALU.add))

        dve.wait_ge(sem("const_ready"), 2)
        dve.tensor_reduce(fold[:], ident[0:NS, 0:NS].rearrange("p (b t) -> p t b", t=NT), AX.X, ALU.add)\
            .then_inc(sem("fold_ready"), 1)

        def keep_histories():
            dve.wait_ge(sem("hist_turned"), 1)
            dve.tensor_copy(params[:], bank[6][:, 0:NPAR])
            dve.tensor_copy(histT[:].rearrange("p c h -> p (c h)"), bank[4][:, 0:384])
            dve.tensor_copy(h0T[:].rearrange("p c b -> p (c b)"), bank[4][:, 384:416])
            dve.tensor_copy(masks[:].rearrange("p g (b t) -> p (g b) t", t=NT),
                            bank[4][:, 416:420].unsqueeze(1).to_broadcast([P, 2 * ND, NT])).then_inc(sem("masks_step"), 1)

        def out_add(n, part):
            dve.wait_ge(sem("w_used"), OUT0 + part * KT + n + 1)
            if part:
                dve.wait_ge(sem("x_added"), XO0 + n + 1)
            elif n == 0:
                dve.wait_ge(sem("x_back"), 16)
            dve.tensor_tensor(xT[:, n, :], xT[:, n, :], bank[n % 2][:, 0:N], ALU.add).then_inc(sem("x_added"), 1)

        def mix_vector():
            rms = rs[:, 2, :]

            def take_in(t):
                dve.wait_ge(sem("w_used"), IN0 + t + 1)
                acc = in_bank(t)[:, 0:N]
                if t == 0:
                    dve.wait_ge(sem("tables_ready"), 1)
                    dve.wait_ge(sem("small_loaded"), 16 * 10)
                    dve.tensor_tensor(col[0:72, 1:2], col[0:72, 1:2], col[0:72, 0:1], ALU.mult)
                    chain(dve.tensor_tensor(sc48[0:72, SC, :], acc[0:72, :], rms[0:72, :], ALU.mult))
                    dve.tensor_scalar(sc48[0:72, SC, :], sc48[0:72, SC, :], col[0:72, 0:1], col[0:72, 1:2], ALU.mult, ALU.add)\
                        .then_inc(sem("in_taken"), 1)
                elif t < T_K:
                    dve.scalar_tensor_tensor(out=qT[:, t - T_Q, :], in0=acc, scalar=HD ** -0.5, in1=rms, op0=ALU.mult,
                                             op1=ALU.mult).then_inc(sem("in_taken"), 1)
                elif t < T_X:
                    to = kT[:, t - T_K, :] if t < T_V else attT[:, t - T_V, :]
                    dve.tensor_tensor(to, acc, rms, ALU.mult).then_inc(sem("in_taken"), 1)
                elif t < T_G:
                    c = t - T_X
                    conv(c, t, acc)
                else:
                    to = gT[:, t - T_G, :] if t < T_Z else zT[:, t - T_Z, :]
                    dve.tensor_tensor(to, acc, rms, ALU.mult).then_inc(sem("in_taken"), 1)

            def conv(c, t, acc):
                r = raw[:, c % 2, :]
                if c == 0:
                    dve.wait_ge(sem("suf_stored"), 16 * ND)
                if c >= 2:
                    dve.wait_ge(sem("conv_done"), c - 1)
                dve.tensor_tensor(r[:, HC:HC + NP_], acc[:, 0:NP_], rms[:, 0:NP_], ALU.mult)
                dve.tensor_copy(strided(r, HC + NP_, (HC + NT, ND), (1, HC)), strided(histT[:, c, :], 0, (HC, ND), (1, HC)))
                dve.tensor_tensor(windows(r, 2 * HC + NP_), sampled(acc[:, NP_:N]), sampled(rms[:, NP_:N]), ALU.mult).then_inc(sem("in_taken"), 1)
                dve.wait_ge(sem("in_taken"), t + 1)
                n, r0, rb, to = (XT_, R_CW, R_CB, xsT) if c < XT_ else (LT_, R_LW, R_LB, uT)
                k = c if c < XT_ else c - XT_
                w = [params[:, r0 + j * n + k:r0 + j * n + k + 1] for j in range(CW)]
                if c:
                    dve.wait_ge(sem("conv_done"), c)
                chain(dve.tensor_scalar(ctmp[:], r[:, 0:312], w[0], params[:, rb + k:rb + k + 1], ALU.mult, ALU.add))
                for j in (1, 2):
                    chain(dve.scalar_tensor_tensor(out=ctmp[:], in0=r[:, j:j + 312], scalar=w[j], in1=ctmp[:],
                                                   op0=ALU.mult, op1=ALU.add))
                dve.scalar_tensor_tensor(out=to[:, k, 0:NP_], in0=r[:, HC:HC + NP_], scalar=w[3], in1=ctmp[:, 0:NP_],
                                         op0=ALU.mult, op1=ALU.add)
                dve.scalar_tensor_tensor(out=sampled(to[:, k, NP_:N]), in0=windows(r, 2 * HC + NP_), scalar=w[3],
                                         in1=windows(ctmp[:], HC + NP_), op0=ALU.mult, op1=ALU.add)
                dve.tensor_copy(histO[:, c, 0:HC], r[:, NP_:NP_ + HC])
                dve.tensor_copy(strided(histO[:, c, :], HC, (HC, ND), (1, HC)),
                                strided(r, HC + NP_ + NT, (HC + NT, ND), (1, HC))).then_inc(sem("conv_done"), 1)

            scratch = [ps[0:72, c * N:(c + 1) * N] for c in range(3)] + [bias[0:72, 0:N]]
            def lo_mix(n):
                if n < IN_TILES:
                    lo(IN0, 0, n, KT)
                else:
                    lo(OUT0, 0, n - IN_TILES, 8)

            lo_mix(0)
            add_x(IN0 - 1, (IN0 - 1) % 4, 0, XO0 - KT, KT - 1, 0.5)
            scale_x(1, KT - 1, 1, XO0)
            split_x(1, KT - 2, 0)
            split_x(1, KT - 1, 1)
            for step in STEPS:
                what, i = step[0], step[-1]
                if what == "in":
                    if i == 1:
                        lo_mix(2)
                        root(1)
                    if i:
                        take_in(i - 1)
                    if i < IN_TILES and i != 1:
                        lo_mix(i + 1)
                elif what == "suffix":
                    dve.wait_ge(sem("lf_loaded"), 16 * ND * PAGES)
                    by_head = lfp[:].rearrange("p s h -> p h s")
                    dve.tensor_reduce(total[:], by_head, AX.X, ALU.add).then_inc(sem("total_ready"), 1)
                    src = take(dve, "later")
                    dve.tensor_copy(lafter[:], src[0:64, 0:H_ATT]).then_inc(side_read("later"), 1)
                    copied(dve, "later")
                    dve.tensor_copy(sfx[:, :, PAGE:].rearrange("p h o -> p (h o)"), lafter[:])
                    for h in range(H_ATT):
                        m = dve.tensor_tensor_scan(back(sfx[:, h, 0:PAGE]), ones[0:64, :],
                                                   back(lfp[:, :, h]), lafter[:, h:h + 1], ALU.mult, ALU.add)
                    m.then_inc(sem("sfx_ready"), 1)
                elif what == "lam":
                    chain(dve.tensor_scalar(lam[:, 0, :], params[:, R_LAM:R_LAM + 4], -1.0, None, ALU.mult))
                    absolute(lam[:, 1, :], lam[:, 0, :])
                    softplus(lam[:, 0, :], *(lam[:, c, :] for c in range(1, 5)), 2)
                    chain(dve.tensor_scalar(lam[:, 0, :], lam[:, 0, :], LRU_C, None, ALU.mult))
                    dve.tensor_scalar(lam[:, 2, :], lam[:, 0, :], -1.0, None, ALU.mult).then_inc(sem("lam_ready"), 1)
                elif step == ("gates", 0):
                    dve.wait_ge(sem("in_taken"), 1)
                    absolute(scratch[0], sc48[0:72, SC, :])
                    softplus_start(*scratch, 1)
                elif step == ("gates", 1):
                    softplus_end(sc48[0:72, SC, :], *scratch[1:])
                elif what == "gates":
                    dve.wait_ge(sem("coef_ready"), 1)
                    chain(dve.tensor_scalar(scratch[0], sc48[0:72, SC, :], col[0:72, 3:4], -1.0, ALU.mult, ALU.mult))
                    chain(dve.tensor_tensor_scan(sc48[0:72, CS, :], seqmask[0:72, :], scratch[0], 0.0, ALU.mult, ALU.add))
                    cs, wd = sc48[0:72, CS, :], sc48[0:72, WDC, :]
                    dve.tensor_scalar(wd[:, 0:NP_], cs[:, 0:NP_], -1.0, cs[:, NP_ - 1:NP_], ALU.mult, ALU.add)
                    dve.tensor_tensor(sampled(wd[:, NP_:N]), strided(cs, NP_ + NT - 1, (NT, ND), (0, NT)),
                                      sampled(cs[:, NP_:N]), ALU.subtract).then_inc(sem("sums_ready"), 1)
                    dve.tensor_scalar(negc[0:72, :], cs, -1.0, None, ALU.mult).then_inc(sem("negc_ready"), 1)
                elif what == "turn_gates":
                    src = take(dve, "nat")
                    dve.tensor_scalar(lfo[:, 0:2, :], strided(src[:, :], 0, (144, 2), (1, H_ATT)), -1.0, None, ALU.mult)
                    dve.tensor_scalar(lfo[0:NS, 2, :], src[0:NS, 288:288 + H_ATT], -1.0, None, ALU.mult)\
                        .then_inc(sem("nat_ready"), 1)
                    dve.tensor_copy(nat[:, 0:2, :].rearrange("p b c -> p (b c)"), src[:, 0:288])
                    dve.tensor_copy(nat_e[0:NS, :], src[0:NS, 432:480])
                    dve.tensor_copy(nat[0:NS, 2, :], src[0:NS, 288:432]).then_inc(side_read("nat"), 1)
                    src = take(dve, "dec")
                    dve.tensor_copy(dec[:].rearrange("p j b -> p (j b)"), src[:, 0:64]).then_inc(side_read("dec"), 1)
                elif what == "turn_kv":
                    for b in range(3):
                        src = take(dve, "k", b)
                        dve.tensor_copy(kvn[0:rows_of(b), b, 0:512], src[0:rows_of(b), :]).then_inc(side_read("k", b), 1)
                elif what == "prompt":
                    if i < H_ATT:
                        src = take(dve, "sc", i)
                        if i == 0:
                            dve.wait_ge(sem("maskp_step"), 3)
                        if i >= 2:
                            copied(dve, "p", i - 2)
                        at = i % 2 * 384
                        dve.tensor_tensor(ps[:, at:at + 384], src[:, 0:384], maskp[:], ALU.add).then_inc(side_read("sc", i), 1)
                        copied(dve, "sc", i)
                        blks = [(ps[:, at + c:at + c + w], 2 * (i % 2) + b) for b, (c, w) in enumerate(((0, P), (P, NP_)))]
                        for w, n in blks:
                            m = dve.tensor_reduce(nm[:, n:n + 1], w, AX.X, ALU.max, negate=True)
                        m.then_inc(sem("fox_max"), 1)
                        dve.wait_ge(sem("fox_exp"), i + 1)
                        n = 2 * (i % 2)
                        chain(dve.reciprocal(rr[:, n:n + 2], rsum[:, n:n + 2]))
                        for w, n in blks:
                            m = dve.tensor_scalar(w, w, rr[:, n:n + 1], None, ALU.mult)
                        m.then_inc(sem("probs_ready"), 1)
                    if i >= 2:
                        h = i - 2
                        src = take(dve, "pv", h)
                        if h == 0:
                            copied(dve, "v", 2)
                        half = slice(h % 2 * HD, (h % 2 + 1) * HD)
                        dve.tensor_copy(attT[half, h // 2, 0:NP_], src[half, 0:NP_]).then_inc(side_read("pv", h), 1)
                elif what == "keys":
                    g = i // 8
                    if i % 8 == 0:
                        if g == 0:
                            dve.wait_ge(sem("maskp_step"), 3)
                            dve.wait_ge(sem("masks_step"), 5)
                            chain(dve.tensor_scalar(masks[:], masks[:], -1.0, BIG, ALU.add, ALU.mult))
                        else:
                            dve.wait_ge(sem("scores_ready"), g)
                        for e in range(2):
                            half = slice(e * HD, (e + 1) * HD)
                            m = dve.tensor_copy(strided(qblk[half], NT * e, (P, 4), (40, 4), (1, NT)),
                                                strided(qT[half], NP_ + 16 * g, (NT, 4), (N, 4), (1, NT)))
                        m.then_inc(sem("qblk_ready"), 1)
                elif what == "max":
                    dve.wait_ge(sem("scores_ready"), i + 1)
                    dve.wait_ge(sem("bias_loaded"), 64 * (i + 1))
                    if i == 0:
                        copied(dve, "p", H_ATT - 1)
                    for c in range(2):
                        cs = slice(c * 512, (c + 1) * 512)
                        dve.tensor_tensor(ps[:, cs], bank[2 + c][:, :], bias[:, cs], ALU.add)
                    dve.tensor_tensor(ps[:, PAST:PAST + NS], bank[4][:, 0:NS], masks[:, i, :], ALU.add)\
                        .then_inc(sem("scores_read"), 1)
                    dve.wait_ge(sem("scores_read"), i + 1)
                    dve.tensor_reduce(nm[:, 0:1], ps[:, 0:PAST + NS], AX.X, ALU.max, negate=True)\
                        .then_inc(sem("sample_max"), 1)
                    dve.wait_ge(sem("sexp_ready"), i + 1)
                    chain(dve.reciprocal(rr[:, 0:1], rsum[:, 0:1]))
                elif what == "scale":
                    dve.wait_ge(sem("sample_pv"), i + 1)
                    dve.tensor_scalar(att_o, bank[4][:, :], rr[:, 0:1], None, ALU.mult).then_inc(sem("att_o_ready"), 1)
                elif what == "merge_heads":
                    src = take(dve, "heads", i)
                    for e in range(2):
                        half = slice(e * HD, (e + 1) * HD)
                        m = dve.tensor_copy(strided(attT[half], NP_ + 16 * i, (N, 4), (NT, 4), (1, NT)),
                                            strided(src[half, :], NT * e, (P + 2 * NT, 4), (32, 4), (1, NT)))
                    m.then_inc(side_read("heads", i), 1)
                elif what == "lru_decay":
                    copied(dve, "i", 3)
                    copied(dve, "i", 2)
                    dve.tensor_tensor(lru_i[:], lru_i[:], uT[:], ALU.mult).then_inc(sem("lru_step"), 1)
                    dve.wait_ge(sem("lru_decayed"), 2)
                    dve.wait_ge(sem("lru_step"), 1)
                    for c in range(4):
                        a2 = ctmp[:, 0:N]
                        chain(dve.tensor_tensor(a2, lru_r[:, c, :], lru_r[:, c, :], ALU.mult))
                        dve.scalar_tensor_tensor(out=uT[:, c, :], in0=a2, scalar=1.0, in1=uT[:, c, :], op0=ALU.add,
                                                 op1=ALU.mult).then_inc(sem("lru_square"), 1)
                        dve.wait_ge(sem("lru_square"), c + 1)
                elif what == "lru_scan":
                    dve.wait_ge(sem("lru_root"), 1)
                    chain(dve.tensor_tensor(lru_i[:], lru_i[:], uT[:], ALU.mult))
                    for c in range(4):
                        dve.tensor_tensor_scan(lru_r[:, c, 0:NP_], lru_r[:, c, 0:NP_], lru_i[:, c, 0:NP_], 0.0,
                                               ALU.mult, ALU.add)
                    prev = h0T[:]
                    for t in range(NT):
                        b, h = (strided(x[:], NP_ + t, (N, 4), (NT, ND)) for x in (lru_i, lru_r))
                        chain(dve.tensor_tensor(h, h, prev, ALU.mult))
                        chain(dve.tensor_tensor(h, h, b, ALU.add))
                        prev = h
                    dve.tensor_copy(lst[:, :, 0:1], lru_r[:, :, NP_ - 1:NP_])
                    dve.tensor_copy(lst[:, :, 1:], prev).then_inc(sem("lst_ready"), 1)
                elif what == "lru_out":
                    src = take(dve, "lru_state")
                    copied(dve, "i", 3)
                    dve.tensor_copy(lrs[0:1 + ND, :], src[0:1 + ND, :]).then_inc(side_read("lru_state"), 1)
                    dve.wait_ge(sem("g_ready"), 1)
                    dve.tensor_tensor(gT[:], gT[:], lru_r[:], ALU.mult).then_inc(sem("lru_done"), 1)
                elif what == "turn_x":
                    n = rows_of(i)
                    for half in range(2):
                        src = take(dve, "x", i, half)
                        dve.tensor_tensor(xsn[0:n, i, half * 512:(half + 1) * 512].rearrange("p (h c) -> p h c", c=HD),
                                          src[0:n, :].rearrange("p (h c) -> p h c", c=HD),
                                          spread(nat[0:n, i, 32 + 8 * half:40 + 8 * half], HD), ALU.mult)\
                            .then_inc(side_read("x", i, half), 1)
                    src = take(dve, "b", i)
                    dve.tensor_copy(bnat[0:rows_of(i), i, :], src[0:rows_of(i), 0:256]).then_inc(side_read("b", i), 1)
                elif what == "scores":
                    dve.tensor_copy(strided(cpad[:], 0, (ND * NS, 2), (NS + NT, ND), (1, NT)),
                                    strided(xsT[:, 10, :], NP_, (N, 2), (NT, ND), (1, NT)))
                    for g in range(2):
                        src = take(dve, "cb", g)
                        dve.tensor_tensor(cbm[:, g, 0:3 * P], src[:, 0:3 * P], tri[:], ALU.mult)
                        dve.tensor_tensor(cbm[0:NS, g, 3 * P:], src[0:NS, 3 * P:SEGW], tris[0:NS, :], ALU.mult)\
                            .then_inc(side_read("cb", g), 1)
                elif what == "merge":
                    dve.wait_ge(sem("m_rounded"), 1)
                    dve.tensor_tensor(xn_lo[:, 0:4, :], attT[:], xn_hi[:, 0:4, :].bitcast(F32), ALU.subtract)\
                        .then_inc(sem("merged"), 4)
                    dve.wait_ge(sem("m_rounded"), 2)
                    dve.tensor_tensor(xn_lo[:, 12:16, :], gT[:], xn_hi[:, 12:16, :].bitcast(F32), ALU.subtract)\
                        .then_inc(sem("merged"), 4)
                elif what == "ssd":
                    if i < H_SSD:
                        src = take(dve, "acs", i)
                        if i >= 2:
                            dve.wait_ge(sem("mseg_ready"), i - 1)
                        for cs, kb, q in PAIRS:
                            n = rows_of(kb)
                            m = dve.tensor_scalar(lseg[0:n, i % 2, cs], src[0:n, q], nat[0:n, kb, 48 + 32 + i:48 + 33 + i], 0.0,
                                                  ALU.subtract, ALU.min)
                        m.then_inc(side_read("acs", i), 1)
                    if i >= 3 and i % 2:
                        j = (i - 3) // 2
                        src = take(dve, "y", j)
                        dve.scalar_tensor_tensor(out=xsT[:, j, :], in0=xsT[:, j, :], scalar=dcol[:, j:j + 1],
                                                 in1=src[:, 0:N], op0=ALU.mult, op1=ALU.add).then_inc(side_read("y", j), 1)
                elif what == "out":
                    if i:
                        out_add(i - 1, 0)
                    lo_mix(IN_TILES + i + 1)
                elif what == "decay_x":
                    for b in range(3):
                        n = rows_of(b)
                        xv = xsn[0:n, b, :].rearrange("p (h c) -> p h c", c=HD)
                        m = dve.tensor_tensor(xv, xv, spread(nat[0:n, b, 96 + 32:96 + 48], HD), ALU.mult)
                    m.then_inc(sem("xw_ready"), 1)
                elif what == "unit":
                    if i % 2 == 0 and i < 2 * ND:
                        b = i // 2
                        if b >= 4:
                            take(dve, "up", 2 * (b - 4) + 1)
                        dve.tensor_scalar(bexp[0:NS, b % 4, :], bnat[0:NS, 2, :], bmask[:, b:b + 1], None, ALU.mult)\
                            .then_inc(sem("bexp_ready"), 1)
                    if i:
                        u = i - 1
                        b, g = u // 2, u % 2
                        src = take(dve, "up", u)
                        if u >= 2:
                            dve.wait_ge(sem(f"snew_stored{u % 2}"), 16 * (u // 2))
                        else:
                            dve.wait_ge(sem("state_stored"), 32)
                        for j in range(4):
                            cs = slice(j * P, (j + 1) * P)
                            m = dve.scalar_tensor_tensor(out=snew[:, u % 2, cs], in0=h0[:, u % 4, cs],
                                                         scalar=dec[:, 4 * g + j, b:b + 1], in1=src[:, cs],
                                                         op0=ALU.mult, op1=ALU.add)
                        m.then_inc(side_read("up", u), 1)
                elif what == "carry":
                    dve.wait_ge(sem("h0t_used"), 2 * ND)
                    for g in range(2):
                        dve.tensor_tensor(ys[0:NS, g * 512:(g + 1) * 512].rearrange("p (h c) -> p h c", c=HD),
                                          bank[2 + g][NS * g:NS * (g + 1), :].rearrange("p (h c) -> p h c", c=HD),
                                          spread(nat_e[0:NS, 32 + 8 * g:40 + 8 * g], HD), ALU.mult).then_inc(sem("ys_ready"), 1)
                    src = take(dve, "ys")
                    dve.tensor_tensor(xsT[:, 0:8, NP_:N], xsT[:, 0:8, NP_:N],
                                      src[:, 0:8 * NS].rearrange("p (j t) -> p j t", t=NS), ALU.add)\
                        .then_inc(side_read("ys"), 1)
                    copied(dve, "ys")
                    dve.tensor_tensor(xsT[:, 0:8, NP_:N], xsT[:, 0:8, NP_:N], zT[:, :, NP_:N], ALU.mult)\
                        .then_inc(sem("gated_y"), 1)
                    dve.wait_ge(sem("y_squared"), 9)
                    dve.tensor_reduce(gsq[:], zT[:, :, NP_:N].rearrange("p (g j) t -> p g t j", g=2), AX.X, ALU.add)\
                        .then_inc(sem("gsq_ready"), 1)
                elif what == "gate_prompt":
                    if i == 0:
                        dve.wait_ge(sem("z_silu"), 2)
                    dve.tensor_tensor(xsT[:, i, 0:NP_], xsT[:, i, 0:NP_], zT[:, i, 0:NP_], ALU.mult)\
                        .then_inc(sem("gated_y"), 1)
                elif step == ("groups", 0):
                    v, y, z = (grs[:, c] for c in range(3))
                    dve.wait_ge(sem("prompt_mean"), 8)
                    dve.tensor_scalar(v[:, :, 0:NP_], bank[4][:, :].rearrange("p (g t) -> p g t", g=2), 1.0 / 512, EPS,
                                      ALU.mult, ALU.add)
                    src = take(dve, "mean")
                    dve.tensor_scalar(v[:, :, NP_:N], src[:, 0:2 * NS].rearrange("p (g t) -> p g t", g=2), 1.0 / 512, EPS,
                                      ALU.mult, ALU.add).then_inc(side_read("mean"), 1)
                elif step == ("groups", 1):
                    dve.wait_ge(sem("groot_step"), 2)
                    chain(dve.tensor_tensor(z, y, y, ALU.mult))
                    chain(dve.tensor_tensor(z, z, v, ALU.mult))
                    chain(dve.tensor_scalar(z, z, -0.5, 1.5, ALU.mult, ALU.add))
                    chain(dve.tensor_tensor(z, z, y, ALU.mult))
                elif step == ("groups", 2):
                    for g in range(2):
                        for j in range(4 * g, 4 * g + 4):
                            m = dve.scalar_tensor_tensor(out=zT[:, j, :], in0=xsT[:, j, :],
                                                         scalar=params[:, R_NRM + j:R_NRM + j + 1], in1=z[:, g, :],
                                                         op0=ALU.mult, op1=ALU.mult)
                        m.then_inc(sem("yn_done"), 1)
                elif step == ("groups", 3):
                    for g in range(2):
                        dve.wait_ge(sem("m_rounded"), g + 3)
                        dve.tensor_tensor(m_lo[:, 4 * g:4 * g + 4, :], zT[:, 4 * g:4 * g + 4, :],
                                          m_hi[:, 4 * g:4 * g + 4, :].bitcast(F32), ALU.subtract).then_inc(sem("merged"), 4)
            out_add(KT - 1, 0)
            for j in range(1, 4):
                lo(OUT0, 0, KT + j, 8)
                out_add(j - 1, 1)
                scale_x(2, j - 1, (j - 1) % 2, XO0 + KT + j)
                if j >= 2:
                    split_x(2, j - 2, j % 2)
            with dve.Fori(1, KT // 4) as it:
                for j in range(4):
                    lo(OUT0 + KT, it * 4, j, 8)
                    add_x(OUT0 + KT - 1 + j + it * 4, (j - 1) % 2, 0, it * 4 + (XO0 + j), it * 4 + (j - 1), 1.0)
                    scale_x(2, it * 4 + (j - 1), (j - 1) % 2, it * 4 + (XO0 + KT + j))
                    split_x(2, it * 4 + (j - 2), j % 2)
            for q in range(2):
                dve.wait_ge(sem(f"snew_stored{q}"), 16 * ND)

        for f in range(2):
            if f == 0:
                dve.wait_ge(sem("x_kept2"), 4)
                dve.wait_ge(sem("x_kept"), 5)
                dve.wait_ge(sem("gains_kept"), 1)
            else:
                mix_vector()
            for g, n in enumerate(GROUPS):
                base, ff0, xa0 = seg["up", f, g], FF0[f, g], XA0[f, g]
                for m in range(3):
                    i = base + 2 * m
                    if base or m != 1:
                        lo(base, 0, 2 * m, KT)
                    if m:
                        gate(i - 1, (i - 1) % 4, ff0 + m - 1, (ff0 + m - 1) % 2, m - 1)
                    elif g:
                        add_x(i - 1, (i - 1) % 4, 0, xa0 - KT if xa0 - KT > 0 else None, KT - 1, 0.5)
                    elif f:
                        out_add(KT - 1, 1)
                        scale_x(2, KT - 1, 1, xa0)
                        split_x(2, KT - 2, 0)
                        split_x(2, KT - 1, 1)
                    else:
                        for k in range(KT + 1):
                            if k < KT:
                                scale_x(0, k, k % 2)
                            if k:
                                split_x(0, k - 1, (k - 1) % 2)
                    lo(base, 0, 2 * m + 1, KT)
                    if m == 0 and g == 0:
                        if f == 0:
                            for k in range(KT):
                                dve.wait_ge(sem("squared"), k + 1)
                                if k == 0:
                                    dve.tensor_copy(ssum[:], sq[:, 0, :]).then_inc(sem("summed"), 1)
                                else:
                                    dve.wait_ge(sem("summed"), k)
                                    dve.tensor_tensor(ssum[:], ssum[:], sq[:, k % 2, :], ALU.add).then_inc(sem("summed"), 1)
                            lo(0, 0, 2, KT)
                        root(FN[f])
                    pre(i, i % 4, ff0 + m, (ff0 + m) % 2)
                    if base == 0 and m == 1:
                        keep_histories()
                with dve.Fori(0, (n - 3) // 2) as it:
                    for m in range(2):
                        lo(base + 6, it * 4, 2 * m, KT)
                        gate(base + 5 + 2 * m + it * 4, (base + 5 + 2 * m) % 4, it * 2 + (ff0 + 2 + m), (ff0 + m) % 2,
                             it * 2 + (2 + m))
                        lo(base + 6, it * 4, 2 * m + 1, KT)
                        pre(base + 6 + 2 * m + it * 4, (base + 6 + 2 * m) % 4, it * 2 + (ff0 + 3 + m), (ff0 + 3 + m) % 2)
                base = seg["down", f, g]
                for j in range(4):
                    lo(base, 0, j, n)
                    if j == 0:
                        gate(base - 1, (base - 1) % 4, ff0 + n - 1, (ff0 + n - 1) % 2, n - 1)
                    else:
                        add_x(base + j - 1, (base + j - 1) % 4, 0, xa0 - KT + j if g or f else None, j - 1, 0.5)
                        if g == 2:
                            scale_x(FN[f] + 1, j - 1, (j - 1) % 2, xa0 + j)
                            if j >= 2:
                                split_x(FN[f] + 1, j - 2, j % 2)
                with dve.Fori(1, KT // 4) as it:
                    for j in range(4):
                        lo(base, it * 4, j, n)
                        add_x(base + j - 1 + it * 4, (base + j - 1) % 4, 0,
                              it * 4 + (xa0 - KT + j) if g or f else None, it * 4 + (j - 1), 0.5)
                        if g == 2:
                            scale_x(FN[f] + 1, it * 4 + (j - 1), (j - 1) % 2, it * 4 + (xa0 + j))
                            split_x(FN[f] + 1, it * 4 + (j - 2), j % 2)
        add_x(base + KT - 1, (base + KT - 1) % 4, 0, xa0, KT - 1, 0.5)
        scale_x(3, KT - 1, 1, xa0 + KT)
        root(3, 3)
        for kg in range(4):
            for b in range(3):
                t = 3 * kg + b
                if t % 2 == 0:
                    rows = P if b < 2 else NS
                    dve.wait_ge(sem("y_turned"), t + 1)
                    dve.tensor_scalar(ynat[0:rows, b, kg * 512:(kg + 1) * 512], bank[t % 7][0:rows, :],
                                      rs[0:rows, 2, b:b + 1], None, ALU.mult)\
                        .then_inc(sem("y_ready"), 1)


_OUTS = {
    "y_prompt": (1, NP_, D), "y_sample": (ND, NT, D),
    "k_prompt": (1, 1, NP_, H_ATT, HD), "v_prompt": (1, 1, NP_, H_ATT, HD), "logf_prompt": (1, 1, NP_, H_ATT),
    "k_sample": (1, ND, NT, H_ATT, HD), "v_sample": (1, ND, NT, H_ATT, HD), "logf_sample": (1, ND, NT, H_ATT),
    "ssd_state_prompt": (1, 1, H_SSD, HD, ST), "ssd_conv_prompt": (1, 1, HC, XBC),
    "ssd_state_sample": (1, ND, H_SSD, HD, ST), "ssd_conv_sample": (1, ND, HC, XBC),
    "lru_state_prompt": (1, 1, DLRU), "lru_conv_prompt": (1, 1, HC, DLRU),
    "lru_state_sample": (1, ND, DLRU), "lru_conv_sample": (1, ND, HC, DLRU),
}
_INS = ["x_prompt", "x_sample", "cache_k", "cache_v", "cache_logf", "page_table", "state_ssd", "state_ssd_conv",
        "state_lru", "state_lru_conv", "ffn1_norm", "ffn1_w_gate", "ffn1_w_up", "ffn1_w_down", "mix_norm", "w_in",
        "fox_b_f", "ssd_conv_w", "ssd_conv_b", "ssd_dt_bias", "ssd_a_log", "ssd_d", "ssd_norm", "lru_conv_w",
        "lru_conv_b", "lru_w_a", "lru_b_a", "lru_w_x", "lru_b_x", "lru_lambda", "w_out", "ffn2_norm",
        "ffn2_w_gate", "ffn2_w_up", "ffn2_w_down", "final_norm"]


def kernel(**inputs):
    import concourse.bacc as _bacc
    from concourse.bass_utils import run_bass_kernel_spmd as _run
    nc = _bacc.Bacc("TRN2", target_bir_lowering=False, num_devices=1, dynamic_dma_scratch_size=4096)
    arrays = {k: np.ascontiguousarray(inputs[k]) for k in _INS}
    I = {k: nc.dram_tensor(k, a.shape, mybir.dt.from_np(a.dtype), kind="ExternalInput").ap() for k, a in arrays.items()}
    O = {k: nc.dram_tensor("out_" + k, shape, F32, kind="ExternalOutput").ap() for k, shape in _OUTS.items()}
    build(nc, I, O)
    r = _run(nc, [arrays], core_ids=[0])
    return tuple(r.results[0]["out_" + k] for k in _OUTS)
```
